# Optimizing a Trainium2 kernel written in Bass

```python
import math
import jax, jax.numpy as jnp
from jax import lax
import numpy as np

D_MODEL = 1024
BATCH = 1
SEQ = 1024
DEPTH = 2

CTX_LEN = 256
GRID_W = 64

GMLP_HEADS = 4
GMLP_HEAD_DIM = 64
GMLP_CHUNK = 128
W_A = GMLP_HEADS * GMLP_HEAD_DIM

DIFF_HEADS = 4
DIFF_HEAD_DIM = 64
DIFF_V_DIM = 2 * DIFF_HEAD_DIM
W_B = DIFF_HEADS * DIFF_V_DIM

CONV_GROUPS = 4
CONV_GROUP_DIM = 64
CONV_WIDTH = 3
W_C = CONV_GROUPS * CONV_GROUP_DIM

D_MIX = W_A + W_B + W_C
D_IN = 3 * W_A + 4 * W_B + 4 * W_C
KV_START = 3 * W_A + W_B
KV_END = KV_START + 2 * W_B

Q_BLOCK = 128
ROPE_BASE = 10000.0
ROPE_PAIRS = DIFF_HEAD_DIM // 4
EPS = 1e-6

kernel_name = "hybrid_parallel_heads_dit_trunk"

def rmsnorm(x, g):
    xf = x.astype(jnp.float32)
    y = xf * lax.rsqrt(jnp.mean(xf * xf, axis=-1, keepdims=True) + EPS)
    return (y * g.astype(jnp.float32)).astype(x.dtype)

def adaln(cond, w_mod, b_mod):
    m = jax.nn.silu(cond) @ w_mod + b_mod
    return jnp.split(m, 3, axis=-1)

def split_cols(p):
    widths = (W_A, W_A, W_A, W_B, W_B, W_B, W_B, W_C, W_C, W_C, W_C)
    idx = [int(i) for i in np.cumsum(widths)[:-1]]
    return jnp.split(p, idx, axis=-1)

def axial_rope_tables(rows):
    row = jnp.broadcast_to(jnp.arange(rows)[:, None], (rows, GRID_W)).reshape(-1).astype(jnp.float32)
    col = jnp.broadcast_to(jnp.arange(GRID_W)[None, :], (rows, GRID_W)).reshape(-1).astype(jnp.float32)
    inv = ROPE_BASE ** (-jnp.arange(ROPE_PAIRS, dtype=jnp.float32) / ROPE_PAIRS)
    ang = jnp.stack([row[:, None] * inv, col[:, None] * inv], axis=1)
    return jnp.cos(ang), jnp.sin(ang)

def apply_rope(x, cos, sin):
    xs = x.reshape(x.shape[:-1] + (2, 2, ROPE_PAIRS))
    x1, x2 = xs[..., 0, :], xs[..., 1, :]
    c = cos[None, :, None, None]
    s = sin[None, :, None, None]
    out = jnp.stack([x1 * c - x2 * s, x2 * c + x1 * s], axis=-2)
    return out.reshape(x.shape).astype(x.dtype)

def short_conv3(x, w, b):
    xp = jnp.pad(x, ((0, 0), (1, 1), (0, 0)))
    return xp[:, :-2] * w[0] + xp[:, 1:-1] * w[1] + xp[:, 2:] * w[2] + b

def chunk_sgu(u, v, g, w_s, b_s):
    bsz, length, _ = v.shape
    v = rmsnorm(v, g)
    vc = v.reshape(bsz, length // GMLP_CHUNK, GMLP_CHUNK, GMLP_HEADS, GMLP_HEAD_DIM)
    mixed = jnp.einsum('hpq,bnqhd->bnphd', w_s, vc) + b_s.T[None, None, :, :, None]
    return u * mixed.reshape(bsz, length, W_A)

def diff_attention(q, k_all, v_all, lam):
    bsz, length = q.shape[:2]
    nb = length // Q_BLOCK
    scale = 1.0 / math.sqrt(DIFF_HEAD_DIM)
    qb = q.reshape(bsz, nb, Q_BLOCK, DIFF_HEADS, 2, DIFF_HEAD_DIM).transpose(1, 0, 2, 3, 4, 5)

    def block(qblk):
        s = jnp.einsum('bqhmd,bkhmd->bhmqk', qblk, k_all).astype(jnp.float32) * scale
        p = jax.nn.softmax(s, axis=-1)
        a = p[:, :, 0] - lam * p[:, :, 1]
        return jnp.einsum('bhqk,bkhe->bqhe', a.astype(v_all.dtype), v_all)

    o = lax.map(block, qb)
    return o.transpose(1, 0, 2, 3, 4).reshape(bsz, length, DIFF_HEADS, DIFF_V_DIM)

def mixer(parts, k_all, v_all, rope, lam, lam_init, w_out, sgu_g, sgu_w, sgu_b, subln_g, conv_w, conv_b):
    au, av, az, bq, _, _, bz, cb, cc, cx, cz = parts
    bsz, length, _ = au.shape
    ya = chunk_sgu(jax.nn.gelu(au), jax.nn.gelu(av), sgu_g, sgu_w, sgu_b) * jax.nn.silu(az)
    q = bq.reshape(bsz, length, DIFF_HEADS, 2, DIFF_HEAD_DIM)
    if rope is not None:
        q = apply_rope(q, rope[0], rope[1])
    ob = rmsnorm(diff_attention(q, k_all, v_all, lam), subln_g) * (1.0 - lam_init)
    yb = ob.reshape(bsz, length, W_B) * jax.nn.silu(bz)
    yc = cb * short_conv3(cc * cx, conv_w, conv_b) * jax.nn.silu(cz)
    return jnp.concatenate([ya, yb, yc], axis=-1) @ w_out

def setup_inputs(seed: int = 0) -> dict:
    key = jax.random.key(seed)
    ks = jax.random.split(key, 24)
    f32 = jnp.float32
    nrm = lambda k, shape, s: jax.random.normal(k, shape, f32) * s
    return {
        "x": nrm(ks[0], (BATCH, SEQ, D_MODEL), 1.0),
        "c": nrm(ks[1], (BATCH, D_MODEL), 1.0),
        "ctx": nrm(ks[2], (BATCH, CTX_LEN, D_MODEL), 1.0),
        "c_ctx": nrm(ks[3], (D_MODEL,), 1.0),
        "w_mod": nrm(ks[4], (DEPTH, D_MODEL, 3 * D_MODEL), 0.5 * D_MODEL ** -0.5),
        "b_mod": nrm(ks[5], (DEPTH, 3 * D_MODEL), 0.02),
        "norm_g": 1.0 + nrm(ks[6], (DEPTH, D_MODEL), 0.02),
        "w_in": nrm(ks[7], (DEPTH, D_MODEL, D_IN), D_MODEL ** -0.5),
        "w_out": nrm(ks[8], (DEPTH, D_MIX, D_MODEL), D_MIX ** -0.5),
        "sgu_norm_g": 1.0 + nrm(ks[9], (DEPTH, W_A), 0.02),
        "sgu_w": nrm(ks[10], (DEPTH, GMLP_HEADS, GMLP_CHUNK, GMLP_CHUNK), GMLP_CHUNK ** -0.5),
        "sgu_b": 1.0 + nrm(ks[11], (DEPTH, GMLP_HEADS, GMLP_CHUNK), 0.02),
        "lambda_q1": nrm(ks[12], (DEPTH, DIFF_HEAD_DIM), 0.1),
        "lambda_k1": nrm(ks[13], (DEPTH, DIFF_HEAD_DIM), 0.1),
        "lambda_q2": nrm(ks[14], (DEPTH, DIFF_HEAD_DIM), 0.1),
        "lambda_k2": nrm(ks[15], (DEPTH, DIFF_HEAD_DIM), 0.1),
        "subln_g": 1.0 + nrm(ks[16], (DEPTH, DIFF_V_DIM), 0.02),
        "conv_w": nrm(ks[17], (DEPTH, CONV_WIDTH, W_C), CONV_WIDTH ** -0.5),
        "conv_b": nrm(ks[18], (DEPTH, W_C), 0.02),
        "final_g": 1.0 + nrm(ks[19], (D_MODEL,), 0.02),
    }

def reference(x, c, ctx, c_ctx, w_mod, b_mod, norm_g, w_in, w_out, sgu_norm_g, sgu_w, sgu_b,
              lambda_q1, lambda_k1, lambda_q2, lambda_k2, subln_g, conv_w, conv_b, final_g):
    bsz, length, _ = x.shape
    ctx_len = ctx.shape[1]
    rows = length // GRID_W
    cos, sin = axial_rope_tables(rows)
    for l in range(DEPTH):
        lam_init = 0.8 - 0.6 * math.exp(-0.3 * l)
        update_ctx = l < DEPTH - 1
        lam = (jnp.exp(jnp.sum(lambda_q1[l].astype(jnp.float32) * lambda_k1[l].astype(jnp.float32)))
               - jnp.exp(jnp.sum(lambda_q2[l].astype(jnp.float32) * lambda_k2[l].astype(jnp.float32)))
               + lam_init)
        sh, sc, gt = adaln(c, w_mod[l], b_mod[l])
        sh_c, sc_c, gt_c = adaln(c_ctx, w_mod[l], b_mod[l])
        h = rmsnorm(x, norm_g[l]) * (1.0 + sc[:, None]) + sh[:, None]
        hc = rmsnorm(ctx, norm_g[l]) * (1.0 + sc_c) + sh_c

        parts = split_cols(h @ w_in[l])
        k_lat = apply_rope(parts[4].reshape(bsz, length, DIFF_HEADS, 2, DIFF_HEAD_DIM), cos, sin)
        v_lat = parts[5].reshape(bsz, length, DIFF_HEADS, DIFF_V_DIM)
        if update_ctx:
            cparts = split_cols(hc @ w_in[l])
            kc_flat, vc_flat = cparts[4], cparts[5]
        else:
            kc_flat, vc_flat = jnp.split(hc @ w_in[l][:, KV_START:KV_END], 2, axis=-1)
        k_ctx = kc_flat.reshape(bsz, ctx_len, DIFF_HEADS, 2, DIFF_HEAD_DIM)
        v_ctx = vc_flat.reshape(bsz, ctx_len, DIFF_HEADS, DIFF_V_DIM)
        k_all = jnp.concatenate([k_ctx, k_lat], axis=1)
        v_all = jnp.concatenate([v_ctx, v_lat], axis=1)

        lw = (w_out[l], sgu_norm_g[l], sgu_w[l], sgu_b[l], subln_g[l], conv_w[l], conv_b[l])
        y_lat = mixer(parts, k_all, v_all, (cos, sin), lam, lam_init, *lw)
        if update_ctx:
            y_ctx = mixer(cparts, k_ctx, v_ctx, None, lam, lam_init, *lw)
            ctx = ctx + gt_c * y_ctx
        x = x + gt[:, None] * y_lat
    return rmsnorm(x, final_g)


_drawn_inputs = setup_inputs


def setup_inputs(seed=0):
    import zlib

    import numpy as np

    out = dict(_drawn_inputs(seed))
    spreads = {}
    factors = {'ctx': 2.97,
     'norm_g': 6.203,
     'sgu_norm_g': 64.0,
     'sgu_b': 64.0,
     'lambda_q1': 7.455,
     'lambda_k1': 5.764,
     'lambda_q2': 6.372,
     'lambda_k2': 8.0,
     'subln_g': 64.0,
     'conv_b': 63.278,
     'final_g': 8.046}
    for name, (base, spread) in spreads.items():
        noise = np.random.default_rng([zlib.crc32(name.encode()), seed]).standard_normal(out[name].shape)
        drawn = base * np.exp(spread * noise) if base else spread * noise
        out[name] = __import__('jax').numpy.asarray(drawn.astype(out[name].dtype))
    for name, factor in factors.items():
        out[name] = (out[name] * factor).astype(out[name].dtype)
    return out
```

```python
import math
from contextlib import ExitStack

import numpy as np

import concourse.bass as bass
from concourse import mybir

F32 = mybir.dt.float32
F32R = mybir.dt.float32r
ACT = mybir.ActivationFunctionType
ALU = mybir.AluOpType
AX = mybir.AxisListType

P = 128
D = 1024
KT = D // P
DEPTH = 2
CTX_TILES = 2
LAT_TILES = 8
TILES = CTX_TILES + LAT_TILES
ROWS = TILES * P
D_IN = 3840
GRID_W = 64
HEADS = 4
HD = 64
EPS = 1e-6
GW = 512

COL_U, COL_AZ, COL_Q, COL_K, COL_V, COL_BZ, COL_CB, COL_CX = 0, 512, 768, 1280, 1792, 2304, 2816, 3328
GROUPS = [(COL_U, 512), (COL_AZ, 256), (COL_CB, 512), (COL_CX, 512), (COL_BZ, 512),
          (COL_Q, 512), (COL_K, 512), (COL_V, 512), (0, 512), (512, 512)]
G_UV, G_AZ, G_CBC, G_CXZ, G_BZ, G_Q, G_K, G_V, G_O0, G_O1 = range(10)
NG = len(GROUPS)
NORM_CHUNKS = [(0, 2), (2, 6), (6, 10)]
SC = 1.0 / math.sqrt(HD)

V_BSH, V_BSC, V_G, V_SUB, V_CW, V_CB, V_SB, V_ROWS = 0, 8, 16, 24, 25, 31, 33, 37


def q_tiles(l):
    return list(range(TILES)) if l < DEPTH - 1 else list(range(CTX_TILES, TILES))


def row_chunks(l):
    c = [(0, 256, 0, 256), (256, 512, 1, 0), (768, 512, 2, 0)]
    return c if l < DEPTH - 1 else c[1:]


def lam_init(l):
    return 0.8 - 0.6 * math.exp(-0.3 * l)


def q_turns(l):
    return [(0, 4), (4, 8), (8, 10)] if l < DEPTH - 1 else [(2, 6), (6, 10)]


K_TURNS = [(0, 4), (4, 8), (8, 10)]


def key_turns(t):
    return [(0, 2)] if t < CTX_TILES else K_TURNS


def chunk_of(t):
    return (0, 2) if t < 2 else ((2, 6) if t < 6 else (6, 10))


def head_steps(l):
    steps, ts, values, rms = [], q_tiles(l), None, None
    for n, t in enumerate(ts):
        steps.append(("scores", t))
        if rms:
            steps.append(("rms", rms))
        rms = values
        if values:
            steps.append(("values", values))
        values = None
        if n:
            steps.append(("turn", ts[n - 1]))
            if chunk_of(ts[n - 1])[1] == t:
                values = chunk_of(ts[n - 1])
    if rms:
        steps.append(("rms", rms))
    steps += [("turn", ts[-1]), ("values", chunk_of(ts[-1])), ("rms", chunk_of(ts[-1]))]
    return steps


def head_rounds(l):
    rounds = []
    for kind, what in head_steps(l):
        if kind == "scores":
            rounds.append((what, []))
        else:
            rounds[-1][1].append((kind, what))
    return rounds


def head_slots(l):
    n = 2 * len(q_turns(l)) + 2 * len(K_TURNS)
    for kind, what in head_steps(l):
        n += {"scores": 0, "rms": 1, "values": 1, "turn": len(key_turns(what)) if kind == "turn" else 0}[kind]
    assert n % 2 == 0
    return n


def build(nc, x, c, ctx_in, c_ctx, w_mod, b_mod, norm_g, w_in, w_out, sgu_g, sgu_w, sgu_b,
          lq1, lk1, lq2, lk2, subln_g, conv_w, conv_b, final_g, cos_t, sin_t, out,
          x1_d, yT_d, bz_d, gate_d):
    with ExitStack() as st:
        def sb(name, shape, dt=F32):
            return st.enter_context(nc.sbuf_tensor(name, shape, dt))

        def sem(name):
            return st.enter_context(nc.semaphore(name))

        H = sb("H", [P, 2 * KT * ROWS], F32R)
        QX = sb("QX", [P, TILES * 3 * GW])
        W = sb("W", [P, 2, KT, GW], F32R)
        RAW = sb("RAW", [P, 4 * ROWS])
        SM = sb("SM", [P, 2048])
        ident = sb("ident", [P, P])
        ones = sb("ones", [P, P])
        cosT = sb("cosT", [P, LAT_TILES, HD])
        sinT = sb("sinT", [P, LAT_TILES, HD])
        sguG = sb("sguG", [P, 256])
        vc = sb("vc", [P, DEPTH, V_ROWS])
        condT = sb("condT", [P, 2, KT])
        shA = sb("shA", [P, DEPTH, 2, 2, KT])
        stat = sb("stat", [P, 3, TILES])
        lamE = sb("lamE", [P, DEPTH, 4])
        nlam = sb("nlam", [P, DEPTH])
        gsub = sb("gsub", [P, DEPTH])
        nmax = sb("nmax", [P, 2, 2])
        Z = sb("Z", [P, 2, 2])
        rz = sb("rz", [P, 4, 2])
        ez = sb("ez", [P, TILES])
        PS = st.enter_context(nc.psum_tensor("PS", [P, 8, 512], F32))
        PF = PS[:, :, :].rearrange("p b n -> p (b n)")

        Hs = H[:, :].rearrange("p (s k n) -> p s k n", s=2, k=KT)
        X = QX[:, 0:TILES * D].rearrange("p (r d) -> p r d", d=D)
        XT = TILES * D
        uv = QX[:, 0:5120].rearrange("p (r n) -> p r n", n=512)
        az = QX[:, 5120:7680].rearrange("p (r n) -> p r n", n=256)
        cbc = QX[:, 7680:12800].rearrange("p (c n) -> p c n", c=4)
        cxz = QX[:, 12800:15360].rearrange("p (c n) -> p c n", c=2)
        ws_in = QX[:, 12800:13312].rearrange("p (h n) -> p h n", h=4)
        wsT = QX[:, 13312:13824].rearrange("p (h n) -> p h n", h=4)
        bzs = QX[:, 0:5120].rearrange("p (c n) -> p c n", c=4)
        qkv = QX[:, :].rearrange("p (r n) -> p r n", n=3 * GW)
        wraw = RAW[:, 0:KT * GW].rearrange("p (k n) -> p k n", k=KT)
        kst = H[:, 0:5120].rearrange("p (s m n) -> p s m n", s=2, m=2)
        qst = H[:, 5120:7680].rearrange("p (m n) -> p m n", m=2)
        vhl = H[:, 7680:10240].rearrange("p (s r e) -> p s r e", s=2, e=P)
        aT = H[:, 10240:20480].rearrange("p (s k q) -> p s k q", s=2, q=512)
        prob = RAW[:, :].rearrange("p (b m n) -> p b m n", b=2, m=2)
        rope = RAW[:, :].rearrange("p (b r n) -> p b r n", b=2, n=2 * P)
        swap = SM[:, 0:LAT_TILES * P].rearrange("p (r n) -> p r n", n=P)

        vec_in, tab_in = sem("vec_in"), sem("tab_in")
        ident_ready, setup_turned, setup_cols = sem("ident_ready"), sem("setup_turned"), sem("setup_cols")
        cond_ready, lam_dve, lam_exp = sem("cond_ready"), sem("lam_dve"), sem("lam_exp")
        wm_in = [sem(f"wm_in{b}") for b in range(5)]
        wm_used, mod_sums, mod_rows = sem("wm_used"), sem("mod_sums"), sem("mod_rows")
        mod_turned, mod_cols, gate_sums = sem("mod_turned"), sem("mod_cols"), sem("gate_sums")
        gate_rows, gate_out, bgate_in = sem("gate_rows"), sem("gate_out"), sem("bgate_in")
        w_raw, w_hi, w_lo, w_used = sem("w_raw"), sem("w_hi"), sem("w_lo"), sem("w_used")
        shared = [
            "n_sq", "n_ms", "n_root", "n_rstd", "n_xn", "n_turned", "n_hi", "n_h", "sg_ms",
            "sg_root", "sg_rstd", "sg_in", "sgw_turned", "sgw_ready", "sg_full", "sg_free",
            "ya_ready", "cc_cx", "yc_ready", "yc_out", "bz_ready", "bz_out", "rope_mul",
            "rope_swap", "rope_ready", "ctx_qk", "v_hi", "v_lo", "gate_in", "y_hi", "y_lo", "n_lo"]
        own = [
            "p_full", "p_free", "sg_sq", "sg_v", "ya_turned", "ya_cols", "conv", "slot_full",
            "slot_hi", "slot_free", "max0", "max1", "s_full0", "s_full1", "exp0", "exp1", "rz_done",
            "coef", "comb", "comb_mul", "comb_low", "sq_done", "ln_done", "yb_ready", "y_out", "bzh_in", "o_full", "o_z",
            "o_x"]
        once = [
            "f_sq", "f_ms", "f_root", "f_rstd", "f_y", "f_out", "fg_in", "x_out"]
        common = {n: sem(n) for n in shared + once}
        common["x_in"] = [sem(f"x_in{i}") for i in range(3)]
        common["y_in"] = [sem(f"y_in{i}") for i in range(4)]
        S = [{**common, **{n: sem(f"L{l}_{n}") for n in own}} for l in range(DEPTH)]

        def unit_base(l):
            nq = len(q_tiles(l))
            base, n = [], 0
            for units in (nq, nq, 4, 4, 4, nq, TILES, TILES):
                base.append(n)
                n += units
            return base + [n]

        def group_end(l, g):
            if g >= G_O0:
                return S[l]["o_full"], len(q_tiles(l)) * (g - G_O0 + 1)
            return S[l]["p_full"], unit_base(l)[g + 1]

        block = st.enter_context(nc.Block())

        @block.sync
        def _(sp):
            for l in range(DEPTH):
                v = RAW[0:V_ROWS, 256 * l:256 * l + P]
                rows = [(V_BSH, b_mod[l, 0:2 * D], 16), (V_G, norm_g[l, :], 8), (V_SUB, subln_g[l, :], 1)]
                for at, src, n in rows:
                    sp.dma_start(v[at:at + n, :], src.rearrange("(n p) -> n p", p=P)).then_inc(vec_in, 16)
                sp.dma_start(v[V_CW:V_CW + 6, :], conv_w[l].rearrange("w (n p) -> (w n) p", p=P)).then_inc(vec_in, 16)
                sp.dma_start(v[V_CB:V_CB + 2, :], conv_b[l].rearrange("(n p) -> n p", p=P)).then_inc(vec_in, 16)
                sp.dma_start(v[V_SB:V_SB + 4, :], sgu_b[l]).then_inc(vec_in, 16)
                for i, a in enumerate((lq1, lk1, lq2, lk2)):
                    sp.dma_start(SM[:, 256 * l + HD * i:256 * l + HD * (i + 1)],
                                 a[l].partition_broadcast(P)).then_inc(vec_in, 16)
            sp.dma_start(RAW[0:8, 512:640], c[0].rearrange("(n p) -> n p", p=P)).then_inc(vec_in, 16)
            sp.dma_start(RAW[8:16, 512:640], c_ctx.rearrange("(n p) -> n p", p=P)).then_inc(vec_in, 16)
            def load_gate_bias(l):
                sp.dma_start(RAW[:, 3 * D:4 * D], b_mod[l, 2 * D:3 * D].partition_broadcast(P)).then_inc(bgate_in, 16)

            def store_gates(l):
                for j in range(2):
                    sp.wait_ge(gate_rows, 4 * l + 2 * j + 2)
                    sp.dma_start(gate_d[l, j], RAW[:, 4 * D:5 * D]).then_inc(gate_out, 16)

            for j in range(DEPTH * KT):
                if j >= 5:
                    sp.wait_ge(wm_used, j - 4)
                sp.dma_start(QX[:, 3 * D * (j % 5):3 * D * (j % 5 + 1)],
                             w_mod[j // KT, P * (j % KT):P * (j % KT + 1), :]).then_inc(wm_in[j % 5], 16)
                if j == 4:
                    sp.wait_ge(setup_turned, 1)
                    load_gate_bias(0)
                    sp.dma_start(cosT[:, :, :], cos_t).then_inc(tab_in, 16)
                    sp.dma_start(sinT[:, :, :], sin_t).then_inc(tab_in, 16)
                if j == KT + 4:
                    store_gates(0)
                    load_gate_bias(1)
            store_gates(1)

            def load_group(l, g):
                n = NG * l + g
                if n:
                    sp.wait_ge(w_lo, KT * n)
                else:
                    sp.wait_ge(gate_out, 16 * 2 * DEPTH)
                col, w = GROUPS[g]
                src = (w_out if g >= G_O0 else w_in)[l, :, col:col + w]
                sp.dma_start(wraw[:, :, 0:w], src.rearrange("(k p) n -> p k n", p=P)).then_inc(w_raw, 16)

            for l in range(DEPTH):
                s = S[l]
                ts = q_tiles(l)
                nq, lo_row = len(ts), ts[0] * P
                if l == 0:
                    load_group(l, G_UV)
                    sp.wait_ge(wm_used, DEPTH * KT)
                    sp.dma_start(X[:, 0:2, :], ctx_in[0].rearrange("(r p) d -> p r d", p=P)).then_inc(s["x_in"][0], 16)
                    xv = x[0].rearrange("(r p) d -> p r d", p=P)
                    sp.dma_start(X[:, 2:6, :], xv[:, 0:4, :]).then_inc(s["x_in"][1], 16)
                    sp.dma_start(X[:, 6:10, :], xv[:, 4:8, :]).then_inc(s["x_in"][2], 16)
                if l:
                    sp.wait_ge(S[l - 1]["sg_v"], len(q_tiles(l - 1)))
                sp.dma_start(sguG[:, :], sgu_g[l].partition_broadcast(P)).then_inc(s["sg_in"], 16)
                load_group(l, G_AZ)
                sp.wait_ge(s["n_lo"], 8 * len(NORM_CHUNKS) + 24 * l)
                sp.dma_start(ws_in, sgu_w[l].rearrange("h p q -> p h q")).then_inc(s["sg_in"], 16)
                load_group(l, G_CBC)
                load_group(l, G_CXZ)
                load_group(l, G_BZ)
                sp.wait_ge(s["ya_cols"], 6 if l == 0 else 4)
                for a in range(2):
                    sp.dma_start(yT_d[a, :, lo_row:ROWS].rearrange("p (r n) -> p r n", n=P),
                                 uv[:, ts[0]:TILES, 256 + P * a:256 + P * (a + 1)]).then_inc(s["y_out"], 16)
                load_group(l, G_Q)
                for i in range(2):
                    sp.wait_ge(s["yc_ready"], i + 1 + 2 * l)
                    sp.dma_start(yT_d[6 + i, :, lo_row:ROWS], SM[:, lo_row:ROWS]).then_inc(s["yc_out"], 16)
                for i in range(4):
                    sp.wait_ge(s["bz_ready"], i + 1 + 4 * l)
                    sp.dma_start(bz_d[i, :, lo_row:ROWS], bzs[:, i, lo_row:ROWS]).then_inc(s["bz_out"], 16)
                load_group(l, G_K)
                load_group(l, G_V)
                load_group(l, G_O0)
                chunks = NORM_CHUNKS if l == 0 else NORM_CHUNKS[1:]
                nch = len(chunks)
                with sp.Fori(0, HEADS) as h:
                    for i, (a, b) in enumerate(chunks):
                        sp.dma_start(SM[:, 1536:1536 + P * (b - a)],
                                     bz_d[bass.ds(h, 1), :, P * a:P * b].rearrange("o p n -> p (o n)")).then_inc(s["bzh_in"], 16)
                        sp.wait_ge(s["yb_ready"], h * nch + (i + 1))
                        sp.dma_start(yT_d[bass.ds(h + 2, 1), :, P * a:P * b].rearrange("o p n -> p (o n)"),
                                     SM[:, 1024:1024 + P * (b - a)]).then_inc(s["y_out"], 16)
                sp.wait_ge(s["y_out"], 16 * HEADS * nch + 32)
                sp.wait_ge(s["yc_out"], 32 + 32 * l)
                sp.wait_ge(s["slot_free"], HEADS * head_slots(l))
                for j in range(2):
                    sp.dma_start(SM[:, D * j:D * (j + 1)], gate_d[l, j]).then_inc(s["gate_in"], 16)
                for i in range(KT):
                    if i >= 4:
                        sp.wait_ge(s["y_lo"], i - 3 + 8 * l)
                    o = XT + ROWS * (i % 4)
                    sp.dma_start(QX[:, o + lo_row:o + ROWS], yT_d[i, :, lo_row:ROWS]).then_inc(s["y_in"][i % 4], 16)
                if l == 0:
                    x0 = S[l]["x_in"][0]
                    sp.dma_start(X[:, 0:2, :], ctx_in[0].rearrange("(r p) d -> p r d", p=P)).then_inc(x0, 16)
                    sp.dma_start(X[:, 2:10, :], x[0].rearrange("(r p) d -> p r d", p=P)).then_inc(x0, 16)
                else:
                    sp.wait_ge(S[0]["x_out"], 16 * TILES)
                    sp.dma_start(X[:, 2:10, :], x1_d[2:10].rearrange("r p d -> p r d")).then_inc(s["x_in"][0], 16)
                load_group(l, G_O1)
                if l == 0:
                    load_group(l + 1, G_UV)
                    for n, r in enumerate(ts):
                        sp.wait_ge(s["o_x"], nq + n + 1)
                        sp.dma_start(x1_d[r], X[:, r, :]).then_inc(s["x_out"], 16)
                else:
                    sp.wait_ge(s["y_lo"], KT + 8 * l)
                    sp.dma_start(QX[:, XT + 1024:XT + 2048], final_g.partition_broadcast(P)).then_inc(s["fg_in"], 16)
                    for n, r in enumerate(ts):
                        sp.wait_ge(s["f_y"], n + 1)
                        sp.dma_start(out[0, P * n:P * (n + 1), :], X[:, r, :]).then_inc(s["f_out"], 16)
                    sp.wait_ge(s["f_out"], 16 * nq)

        @block.gpsimd
        def _(pool):
            nc.gpsimd.memset(ident[:, :], 0.0).then_inc(ident_ready, 1)
            pool.wait_ge(ident_ready, 1)
            nc.gpsimd.affine_select(out=ident[:, :], in_=ident[:, :], compare_op=ALU.not_equal, fill=1.0,
                                    base=0, pattern=[[-1, P]], channel_multiplier=1).then_inc(ident_ready, 1)
            nc.gpsimd.memset(ones[:, :], 1.0 / P).then_inc(ident_ready, 1)
            pool.wait_ge(tab_in, 32)
            for l in range(DEPTH):
                s = S[l]
                nq, nslot = len(q_tiles(l)), head_slots(l)
                pool.wait_ge(s["p_full"], unit_base(l)[-1])
                pool.wait_ge(s["p_free"], unit_base(l)[-1])
                pool.wait_ge(w_lo, KT * (NG * l + G_O0 + 1))
                with pool.Fori(0, HEADS) as h:
                    for i in range(2):
                        if i:
                            pool.wait_ge(s["rope_ready"], h * 2 + 1 + 8 * l)
                        src = qkv[:, CTX_TILES:TILES, bass.ds(h * P + GW * i, P)].rearrange(
                            "p r (a f e) -> p r a f e", f=2, e=16)
                        dst = swap.rearrange("p r (a f e) -> p r a f e", f=2, e=16)
                        tab = sinT[:, :, :].rearrange("p r (a f e) -> p r a f e", f=2, e=16)
                        for m in range(2):
                            for f in range(2):
                                nc.gpsimd.tensor_tensor(dst[:, :, 2 * m:2 * m + 2, f, :], src[:, :, 2 * m:2 * m + 2, 1 - f, :],
                                                        tab[:, :, :, f, :], ALU.mult).then_inc(s["rope_swap"], 1)
                    for n in range(nq):
                        w = 256 if q_tiles(l)[n] < CTX_TILES else ROWS
                        b = n % 2
                        pool.wait_ge(s["coef"], h * nq + (n + 1))
                        e0, e1 = prob[:, n % 2, 0, w // 2:w], prob[:, n % 2, 1, w // 2:w]
                        nc.gpsimd.tensor_tensor(e1, e1, rz[:, 3, b:b + 1].to_broadcast([P, w - w // 2]), ALU.mult).then_inc(s["comb_mul"], 1)
                        pool.wait_ge(s["comb_mul"], h * nq + (n + 1))
                        nc.gpsimd.tensor_tensor(e0, e0, e1, ALU.add).then_inc(s["comb"], 1)
                    pool.wait_ge(s["slot_free"], h * nslot + nslot)

        @block.tensor
        def _(pe):
            mm = nc.tensor.matmul
            pe.wait_ge(ident_ready, 3)
            pe.wait_ge(vec_in, 16 * 22)
            for l in range(DEPTH):
                nc.tensor.transpose(PS[:, 0, 64 * l:64 * l + V_ROWS], RAW[0:V_ROWS, 256 * l:256 * l + P],
                                    ident[0:V_ROWS, 0:V_ROWS])
            nc.tensor.transpose(PS[:, 0, 128:144], RAW[0:16, 512:640], ident[0:16, 0:16]).then_inc(setup_turned, 1)
            pe.wait_ge(cond_ready, 1)
            for l in range(DEPTH):
                if l:
                    pe.wait_ge(mod_rows, 6 * l)
                    pe.wait_ge(gate_rows, 4 * l)
                for k in range(KT):
                    j = KT * l + k
                    pe.wait_ge(wm_in[j % 5], 16 * (j // 5 + 1))
                    for b in range(6):
                        o = 3 * D * (j % 5) + 512 * b
                        last = mm(PS[0:2, 1 + b, :], condT[:, :, k], QX[:, o:o + 512], start=(k == 0), stop=(k == KT - 1))
                    last.then_inc(wm_used, 1)
                pe.wait_ge(mod_rows, 6 * l + 6)
                for n in range(16):
                    last = nc.tensor.transpose(PS[:, 7, 2 * n:2 * n + 2], RAW[0:2, P * n:P * (n + 1)], ident[0:2, 0:2])
                last.then_inc(mod_turned, 1)
                for j in range(2):
                    for b in range(2):
                        if j:
                            pe.wait_ge(gate_rows, 4 * l + 2 * (j - 1) + b + 1)
                        mm(PS[:, 1 + b, :], ident[0:2, j:j + 1].to_broadcast([2, P]), RAW[0:2, 2 * D + 512 * b:2 * D + 512 * (b + 1)],
                           start=True, stop=True).then_inc(gate_sums, 1)

            def three(o, wt, mv, start, stop):
                mm(o, wt(0), mv(0), start=start, stop=False)
                mm(o, wt(0), mv(1), start=False, stop=False)
                return mm(o, wt(1), mv(0), start=False, stop=stop)

            def rows_unit(bank, r, w, wait_n, last_of_group):
                for k in range(KT):
                    if wait_n is not None:
                        pe.wait_ge(w_lo, wait_n + k + 1)
                    t = three(PS[:, bank, 0:w], lambda i: Hs[:, i, k, P * r:P * (r + 1)],
                              lambda i: W[:, i, k, 0:w], k == 0, k == KT - 1)
                    if last_of_group and k < KT - 1:
                        t.then_inc(w_used, 1)
                return t

            def cols_unit(bank, ct, l, wait_n, last_of_group):
                for k in range(KT):
                    if wait_n is not None:
                        pe.wait_ge(w_lo, wait_n + k + 1)
                    for r0, n, b, o in row_chunks(l):
                        t = three(PS[:, bank + b, o:o + n], lambda i: W[:, i, k, P * ct:P * (ct + 1)],
                                  lambda i: Hs[:, i, k, r0:r0 + n], k == 0, k == KT - 1)
                    if last_of_group and k < KT - 1:
                        t.then_inc(w_used, 1)
                return t

            for l in range(DEPTH):
                s = S[l]
                ts = q_tiles(l)
                nq, ub = len(ts), unit_base(l)
                if l == 0:
                    pe.wait_ge(mod_cols, DEPTH * 2)
                    pe.wait_ge(gate_rows, 4 * DEPTH)
                else:
                    pe.wait_ge(S[l - 1]["o_z"], 2 * len(q_tiles(l - 1)))
                for ci, (a, b) in enumerate(NORM_CHUNKS):
                    for k in range(KT):
                        if k == 0:
                            pe.wait_ge(s["n_xn"], b + 10 * l)
                        if ci:
                            pe.wait_ge(s["n_lo"], KT * (ci - 1) + k + 1 + 24 * l)
                        for r in range(a, b):
                            t = nc.tensor.transpose(PS[:, k, P * (r - a):P * (r - a + 1)], X[:, r, P * k:P * (k + 1)], ident[:, :])
                        t.then_inc(s["n_turned"], 1)
                pe.wait_ge(s["n_lo"], KT * len(NORM_CHUNKS) + 24 * l)
                for g in (G_UV, G_AZ):
                    for n, r in enumerate(ts):
                        u = ub[g] + n
                        if u >= 5:
                            pe.wait_ge(s["p_free"], u - 4)
                        t = rows_unit(u % 5, r, GROUPS[g][1], KT * (NG * l + g) if n == 0 else None, n == nq - 1)
                        t.then_inc(s["p_full"], 1)
                pe.wait_ge(s["p_free"], ub[G_CBC])
                for g in (G_CBC, G_CXZ, G_BZ):
                    for ct in range(4):
                        u = ub[g] + ct
                        if u >= ub[G_CBC] + 2:
                            pe.wait_ge(s["p_free"], u - 1)
                        t = cols_unit(3 * (ct % 2), ct, l, KT * (NG * l + g) if ct == 0 else None, ct == 3)
                        t.then_inc(s["p_full"], 1)
                        if (g, ct) == (G_CBC, 0):
                            pe.wait_ge(s["sg_in"], 32 + 32 * l)
                            for hh in range(4):
                                t = nc.tensor.transpose(PS[:, 6, P * hh:P * (hh + 1)], ws_in[:, hh, :], ident[:, :])
                            t.then_inc(s["sgw_turned"], 1)
                        if (g, ct) == (G_CBC, 1):
                            pe.wait_ge(s["sgw_ready"], 1 + 1 * l)
                            pe.wait_ge(s["sg_v"], nq)
                            half = nq // 2
                            for hh in range(4):
                                for i in range(2):
                                    n = 2 * hh + i
                                    if n >= 2:
                                        pe.wait_ge(s["sg_free"], n - 1 + 8 * l)
                                    a = ts[0] + half * i
                                    mm(PS[:, 6 + i, 0:half * HD].rearrange("p (r n) -> p r n", n=HD), wsT[:, hh, :],
                                       uv[:, a:a + half, 256 + HD * hh:256 + HD * (hh + 1)],
                                       start=True, stop=True).then_inc(s["sg_full"], 1)
                        if (g, ct) == (G_CXZ, 1):
                            pe.wait_ge(s["ya_ready"], 1 + 1 * l)
                            n = 0
                            for a in range(2):
                                for r0, r1 in q_turns(l):
                                    if n >= 2:
                                        pe.wait_ge(s["ya_cols"], n - 1)
                                    for r in range(r0, r1):
                                        t = nc.tensor.transpose(PS[:, 6 + n % 2, P * (r - r0):P * (r - r0 + 1)],
                                                                uv[:, r, P * a:P * (a + 1)], ident[:, :])
                                    t.then_inc(s["ya_turned"], 1)
                                    n += 1
                pe.wait_ge(s["p_free"], ub[G_Q])
                if l == DEPTH - 1:
                    for n, r in enumerate(ts):
                        if n >= 5:
                            pe.wait_ge(s["p_free"], ub[G_Q] + n - 4)
                        t = rows_unit(n % 5, r, GW, KT * (NG * l + G_Q) if n == 0 else None, n == nq - 1)
                        t.then_inc(s["p_full"], 1)
                    pe.wait_ge(s["p_free"], ub[G_K])
                g0 = G_Q if l < DEPTH - 1 else G_K
                with pe.Fori(0, G_O0 - g0) as i:
                    for r in range(TILES):
                        pe.wait_ge(s["p_free"], i * TILES + (ub[g0] + r - 4))
                        t = rows_unit(r % 5, r, GW, None if r else i * KT + KT * (NG * l + g0), r == TILES - 1)
                        t.then_inc(s["p_full"], 1)

                pe.wait_ge(s["p_free"], ub[-1])
                nslot = head_slots(l)
                with pe.Fori(0, HEADS) as h:
                    used = [0]

                    def slot():
                        n = used[0]
                        used[0] += 1
                        if n >= 2:
                            pe.wait_ge(s["slot_free"], h * nslot + (n - 1))
                        return 6 + n % 2

                    for i, turns in enumerate((q_turns(l), K_TURNS)):
                        pe.wait_ge(s["rope_ready"], h * 2 + (i + 1) + 8 * l)
                        pe.wait_ge(s["ctx_qk"], h * 2 + (i + 1) + 8 * l)
                        for m in range(2):
                            for r0, r1 in turns:
                                b = slot()
                                for r in range(r0, r1):
                                    t = nc.tensor.transpose(
                                        PS[:, b, P * (r - r0):P * (r - r0 + 1)],
                                        rope[:, i, r, P * m:P * (m + 1)], ident[:, :])
                                t.then_inc(s["slot_full"], 1)
                    nprep = used[0]
                    pe.wait_ge(s["slot_free"], h * nslot + nprep)
                    pe.wait_ge(s["v_lo"], h + 1 + 4 * l)
                    done = 0
                    for kind, what in head_steps(l):
                        if kind == "scores":
                            for m in range(2):
                                if done:
                                    pe.wait_ge(s[f"exp{m}"], h * nq + done)
                                for r0, n in (((0, 256),) if what < CTX_TILES else ((0, 512), (512, 512), (1024, 256))):
                                    o = 1536 * m + r0
                                    for part in range(2):
                                        t = mm(PF[:, o:o + n], qst[:, m, P * what:P * (what + 1)],
                                               kst[:, part, m, r0:r0 + n], start=(part == 0), stop=(part == 1))
                                t.then_inc(s[f"s_full{m}"], 1)
                            done += 1
                        if kind == "turn":
                            n = what - ts[0]
                            pe.wait_ge(s["comb"], h * nq + (n + 1))
                            pe.wait_ge(s["comb_low"], h * nq + (n + 1))
                            for k0, k1 in key_turns(what):
                                b = slot()
                                for kk in range(k0, k1):
                                    t = nc.tensor.transpose(PS[:, b, P * (kk - k0):P * (kk - k0 + 1)],
                                                            prob[:, n % 2, 0, P * kk:P * (kk + 1)], ident[:, :])
                                t.then_inc(s["slot_full"], 1)
                        if kind == "values":
                            a, e = what
                            w = P * (e - a)
                            nk = CTX_TILES if a < CTX_TILES else TILES
                            b = slot()
                            pe.wait_ge(s["slot_free"], h * nslot + (used[0] - 1))
                            for kk in range(nk):
                                t = three(PS[:, b, 0:w], lambda i: vhl[:, i, kk, :], lambda i: aT[:, i, kk, 0:w],
                                          kk == 0, kk == nk - 1)
                            t.then_inc(s["slot_full"], 1)
                        if kind == "rms":
                            a, e = what
                            w = P * (e - a)
                            b = slot()
                            chunks = NORM_CHUNKS if l == 0 else NORM_CHUNKS[1:]
                            pe.wait_ge(s["sq_done"], h * len(chunks) + (chunks.index(what) + 1))
                            mm(PS[:, b, 0:w], ones[:, :], SM[:, 0:w], start=True, stop=True).then_inc(s["slot_full"], 1)
                    pe.wait_ge(s["slot_free"], h * nslot + nslot)
                pe.wait_ge(s["slot_free"], HEADS * nslot)
                pe.wait_ge(s["y_lo"], KT + 8 * l)
                for g in range(2):
                    for n, r in enumerate(ts):
                        u = nq * g + n
                        if u >= 5:
                            pe.wait_ge(s["o_z"], u - 4)
                        t = rows_unit(u % 5, r, GW, KT * (NG * l + G_O0 + g) if n == 0 else None, n == nq - 1)
                        t.then_inc(s["o_full"], 1)

        @block.scalar
        def _(act):
            A = nc.scalar.activation
            act.wait_ge(setup_turned, 1)
            A(condT[:, :, :], PS[:, 0, 128:144].rearrange("p (j k) -> p j k", j=2), ACT.Silu).then_inc(cond_ready, 1)
            act.wait_ge(lam_dve, 2 * DEPTH)
            for l in range(DEPTH):
                A(lamE[:, l, 2:4], lamE[:, l, 0:2], ACT.Exp).then_inc(lam_exp, 1)
            for l in range(DEPTH):
                act.wait_ge(wm_used, KT * (l + 1))
                if l:
                    act.wait_ge(gate_rows, 4 * l)
                    act.wait_ge(mod_turned, l)
                for b in range(6):
                    A(RAW[0:2, 512 * b:512 * (b + 1)], PS[0:2, 1 + b, :], ACT.Copy).then_inc(mod_rows, 1)

            def split_hi(l, g):
                n = NG * l + g
                w = GROUPS[g][1]
                act.wait_ge(w_raw, 16 * (n + 1))
                for k in range(KT):
                    if n and k < KT - 1:
                        act.wait_ge(w_used, (KT - 1) * (n - 1) + k + 1)
                    elif n:
                        act.wait_ge(*group_end(*divmod(n - 1, NG)))
                    A(W[:, 0, k, 0:w], wraw[:, k, 0:w], ACT.Copy).then_inc(w_hi, 1)

            split_hi(0, G_UV)
            for l in range(DEPTH):
                s = S[l]
                ts = q_tiles(l)
                nq, ub = len(ts), unit_base(l)
                lo = ts[0] * P
                for ci, (a, b) in enumerate(NORM_CHUNKS):
                    if l == 0:
                        act.wait_ge(s["x_in"][ci], 16)
                    for r in range(a, b):
                        if l:
                            act.wait_ge(S[l - 1]["o_x"], len(q_tiles(l - 1)) + r + 1)
                        if r:
                            act.wait_ge(s["n_sq"], r + 10 * l)
                        A(QX[:, XT:XT + D], X[:, r, :], ACT.Square, accum_out=stat[:, 0, r:r + 1]).then_inc(s["n_sq"], 1)
                    act.wait_ge(s["n_ms"], ci + 1 + 3 * l)
                    A(stat[:, 1, a:b], stat[:, 1, a:b], ACT.Sqrt).then_inc(s["n_root"], 1)
                for ci, (a, b) in enumerate(NORM_CHUNKS):
                    j = 1 if ci == 0 else 0
                    for k in range(KT):
                        act.wait_ge(s["n_turned"], KT * ci + k + 1 + 24 * l)
                        A(Hs[:, 0, k, P * a:P * b], PS[:, k, 0:P * (b - a)], ACT.Identity,
                          scale=shA[:, l, 1, j, k:k + 1], bias=shA[:, l, 0, j, k:k + 1]).then_inc(s["n_hi"], 1)
                for n, r in enumerate(ts):
                    if n == nq - 1:
                        split_hi(l, G_AZ)
                    act.wait_ge(s["p_full"], n + 1)
                    A(uv[:, r, :], PS[:, n % 5, :], ACT.Gelu_apprx_tanh).then_inc(s["p_free"], 1)
                    act.wait_ge(s["p_free"], n + 1)
                    if n:
                        act.wait_ge(s["sg_sq"], n)
                    A(QX[:, 7680:7936], uv[:, r, 256:512], ACT.Square, accum_out=stat[:, 2, r:r + 1]).then_inc(s["sg_sq"], 1)
                act.wait_ge(s["sg_ms"], 1 + 1 * l)
                A(stat[:, 0, ts[0]:], stat[:, 0, ts[0]:], ACT.Sqrt).then_inc(s["sg_root"], 1)
                for n, r in enumerate(ts):
                    if n == nq - 1:
                        split_hi(l, G_CBC)
                    u = ub[G_AZ] + n
                    act.wait_ge(s["p_full"], u + 1)
                    A(az[:, r, :], PS[:, u % 5, 0:256], ACT.Silu).then_inc(s["p_free"], 1)
                for g in (G_CBC, G_CXZ, G_BZ):
                    for ct in range(4):
                        if ct == 3:
                            split_hi(l, g + 1)
                        u = ub[g] + ct
                        act.wait_ge(s["p_full"], u + 1)
                        src = PF[:, 1536 * (ct % 2) + 256 + lo:1536 * (ct % 2) + 256 + ROWS]
                        if g == G_CBC:
                            A(cbc[:, ct, lo:], src, ACT.Copy).then_inc(s["p_free"], 1)
                        elif g == G_CXZ:
                            if ct < 2:
                                act.wait_ge(s["sg_full"], 8 + 8 * l)
                                A(cxz[:, ct, lo:], src, ACT.Copy).then_inc(s["p_free"], 1)
                            else:
                                act.wait_ge(s["cc_cx"], ct - 1 + 2 * l)
                                A(cxz[:, ct - 2, lo:], src, ACT.Silu).then_inc(s["p_free"], 1)
                        else:
                            if ct == 0:
                                act.wait_ge(s["y_out"], 32)
                            A(bzs[:, ct, lo:], src, ACT.Silu).then_inc(s["p_free"], 1)
                            act.wait_ge(s["p_free"], u + 1)
                            A(stat[0:1, 1, 0:1], stat[0:1, 1, 0:1], ACT.Copy).then_inc(s["bz_ready"], 1)
                        if (g, ct) == (G_CBC, 0):
                            act.wait_ge(s["sgw_turned"], 1 + 1 * l)
                            A(wsT[:, :, :], PS[:, 6, :].rearrange("p (h n) -> p h n", h=4), ACT.Copy).then_inc(s["sgw_ready"], 1)
                        if (g, ct) == (G_CXZ, 1):
                            n = 0
                            for a in range(2):
                                for r0, r1 in q_turns(l):
                                    act.wait_ge(s["ya_turned"], n + 1)
                                    A(uv[:, r0:r1, 256 + P * a:256 + P * (a + 1)],
                                      PS[:, 6 + n % 2, 0:P * (r1 - r0)].rearrange("p (r n) -> p r n", n=P),
                                      ACT.Copy).then_inc(s["ya_cols"], 1)
                                    n += 1
                act.wait_ge(s["bz_out"], 64 + 64 * l)
                act.wait_ge(s["yc_out"], 32 + 32 * l)
                if l == DEPTH - 1:
                    for n, r in enumerate(ts):
                        if n == nq - 1:
                            split_hi(l, G_K)
                        act.wait_ge(s["p_full"], ub[G_Q] + n + 1)
                        A(qkv[:, r, 0:GW], PS[:, n % 5, :], ACT.Copy).then_inc(s["p_free"], 1)
                g0 = G_Q if l < DEPTH - 1 else G_K
                with act.Fori(0, G_O0 - g0) as i:
                    for r in range(TILES):
                        if r == TILES - 1:
                            n = NG * l + g0
                            act.wait_ge(w_raw, i * 16 + 16 * (n + 2))
                            for k in range(KT):
                                if k < KT - 1:
                                    act.wait_ge(w_used, i * (KT - 1) + ((KT - 1) * n + k + 1))
                                else:
                                    act.wait_ge(s["p_full"], i * TILES + ub[g0 + 1])
                                A(W[:, 0, k, :], wraw[:, k, :], ACT.Copy).then_inc(w_hi, 1)
                        act.wait_ge(s["p_full"], i * TILES + (ub[g0] + r + 1))
                        A(qkv[:, r, bass.ds(i * GW + GW * (g0 - G_Q), GW)], PS[:, r % 5, :], ACT.Copy).then_inc(s["p_free"], 1)

                nslot = head_slots(l)
                chunks = NORM_CHUNKS if l == 0 else NORM_CHUNKS[1:]
                act.wait_ge(s["p_free"], ub[-1])
                act.wait_ge(w_lo, KT * (NG * l + G_O0 + 1))
                with act.Fori(0, HEADS) as h:
                    for i in range(2):
                        src = qkv[:, 0:CTX_TILES, bass.ds(h * P + GW * (i if l == 0 else 1), P)]
                        for m in range(2):
                            t = A(rope[:, i, 0:CTX_TILES, P * m:P * (m + 1)].rearrange("p r (d n) -> p r d n", d=2),
                                  src[:, :, HD * m:HD * (m + 1)].unsqueeze(2).to_broadcast([P, CTX_TILES, 2, HD]), ACT.Copy)
                        t.then_inc(s["ctx_qk"], 1)
                    A(vhl[:, 0, :, :], qkv[:, :, bass.ds(h * P + 2 * GW, P)], ACT.Copy).then_inc(s["v_hi"], 1)
                    n = 0
                    for i, turns in enumerate((q_turns(l), K_TURNS)):
                        for m in range(2):
                            for r0, r1 in turns:
                                act.wait_ge(s["slot_full"], h * nslot + (n + 1))
                                src = PS[:, 6 + n % 2, 0:P * (r1 - r0)]
                                if i == 0:
                                    A(qst[:, m, P * r0:P * r1], src, ACT.Copy, scale=SC).then_inc(s["slot_hi"], 1)
                                else:
                                    A(kst[:, 0, m, P * r0:P * r1], src, ACT.Copy).then_inc(s["slot_hi"], 1)
                                n += 1
                    def exps(t, m):
                        q = t - ts[0]
                        w = 256 if t < CTX_TILES else ROWS
                        act.wait_ge(s[f"max{m}"], h * nq + (q + 1))
                        A(prob[:, q % 2, m, 0:w], PF[:, 1536 * m:1536 * m + w], ACT.Exp,
                          bias=nmax[:, m, q % 2:q % 2 + 1], accum_out=Z[:, m, q % 2:q % 2 + 1]).then_inc(s[f"exp{m}"], 1)

                    for tile, behind in head_rounds(l):
                        exps(tile, 0)
                        second_due = True
                        for kind, what in behind:
                            if kind == "turn":
                                q = (what - chunk_of(what)[0]) * P
                                for k0, k1 in key_turns(what):
                                    if second_due and k0:
                                        exps(tile, 1)
                                        second_due = False
                                    act.wait_ge(s["slot_full"], h * nslot + (n + 1))
                                    A(aT[:, 0, k0:k1, q:q + P], PS[:, 6 + n % 2, 0:P * (k1 - k0)].rearrange("p (k q) -> p k q", q=P),
                                      ACT.Copy).then_inc(s["slot_hi"], 1)
                                    n += 1
                                continue
                            if second_due:
                                exps(tile, 1)
                                second_due = False
                            w = P * (what[1] - what[0])
                            act.wait_ge(s["slot_full"], h * nslot + (n + 1))
                            if kind == "values":
                                A(SM[:, 0:w], PS[:, 6 + n % 2, 0:w], ACT.Square).then_inc(s["slot_hi"], 1)
                            else:
                                ch = chunks.index(what)
                                A(SM[:, 512:512 + w], PS[:, 6 + n % 2, 0:w], ACT.Ln).then_inc(s["ln_done"], 1)
                                act.wait_ge(s["ln_done"], h * len(chunks) + (ch + 1))
                                A(SM[:, 512:512 + w], SM[:, 512:512 + w], ACT.Exp, scale=-0.5).then_inc(s["slot_hi"], 1)
                            n += 1
                        if second_due:
                            exps(tile, 1)
                    act.wait_ge(s["slot_full"], h * nslot + nslot)
                act.wait_ge(s["slot_free"], HEADS * nslot)
                for i in range(KT):
                    act.wait_ge(s["y_in"][i % 4], 16 * (i // 4 + 1) + 32 * l)
                    o = XT + ROWS * (i % 4)
                    A(Hs[:, 0, i, lo:], QX[:, o + lo:o + ROWS], ACT.Copy).then_inc(s["y_hi"], 1)
                split_hi(l, G_O1)
                if l < DEPTH - 1:
                    split_hi(l + 1, G_UV)
                else:
                    for n, r in enumerate(ts):
                        act.wait_ge(s["o_x"], nq + n + 1)
                        if n:
                            act.wait_ge(s["f_sq"], n)
                        A(QX[:, XT + 2048:XT + 3072], X[:, r, :], ACT.Square, accum_out=stat[:, 0, r:r + 1]).then_inc(s["f_sq"], 1)
                        act.wait_ge(s["f_ms"], n + 1)
                        A(stat[:, 1, r:r + 1], stat[:, 1, r:r + 1], ACT.Sqrt).then_inc(s["f_root"], 1)

        @block.vector
        def _(dve):
            V = nc.vector
            dve.wait_ge(vec_in, 16 * 22)
            for l in range(DEPTH):
                lv = SM[:, 256 * l:256 * (l + 1)].rearrange("p (a b n) -> p a b n", a=2, b=2)
                o = SM[:, 512 + P * l:512 + P * (l + 1)].rearrange("p (a n) -> p a n", a=2)
                V.tensor_tensor(o, lv[:, :, 0, :], lv[:, :, 1, :], ALU.mult).then_inc(lam_dve, 1)
                dve.wait_ge(lam_dve, 2 * l + 1)
                V.reduce_sum(lamE[:, l, 0:2], o, AX.X).then_inc(lam_dve, 1)
            for l in range(DEPTH):
                dve.wait_ge(lam_exp, l + 1)
                V.scalar_tensor_tensor(out=nlam[:, l:l + 1], in0=lamE[:, l, 3:4], scalar=lam_init(l), in1=lamE[:, l, 2:3],
                                       op0=ALU.subtract, op1=ALU.subtract).then_inc(lam_dve, 1)
            dve.wait_ge(setup_turned, 1)
            dve.wait_ge(cond_ready, 1)
            V.tensor_copy(vc[:, :, :], PS[:, 0, 0:128].rearrange("p (l v) -> p l v", l=2)[:, :, 0:V_ROWS]).then_inc(setup_cols, 1)
            dve.wait_ge(setup_cols, 1)
            for l in range(DEPTH):
                V.tensor_scalar(gsub[:, l:l + 1], vc[:, l, V_SUB:V_SUB + 1], 1.0 - lam_init(l), None, ALU.mult).then_inc(setup_cols, 1)
            for l in range(DEPTH):
                dve.wait_ge(mod_turned, l + 1)
                for part in range(2):
                    V.tensor_tensor(shA[:, l, part, :, :], PS[:, 7, 16 * part:16 * part + 16].rearrange("p (k j) -> p j k", j=2),
                                    vc[:, l, 8 * part:8 * part + 8].unsqueeze(1).to_broadcast([P, 2, KT]), ALU.add).then_inc(mod_cols, 1)
                dve.wait_ge(mod_cols, 3 * l + 2)
                V.scalar_tensor_tensor(out=shA[:, l, 1, :, :], in0=shA[:, l, 1, :, :], scalar=1.0,
                                       in1=vc[:, l, V_G:V_G + 8].unsqueeze(1).to_broadcast([P, 2, KT]),
                                       op0=ALU.add, op1=ALU.mult).then_inc(mod_cols, 1)
                dve.wait_ge(bgate_in, 16 * (l + 1))
                for j in range(2):
                    for b in range(2):
                        n = 4 * l + 2 * j + b
                        dve.wait_ge(gate_sums, n + 1)
                        if b == 0 and n:
                            dve.wait_ge(gate_out, 16 * (n // 2))
                        V.tensor_tensor(RAW[:, 4 * D + 512 * b:4 * D + 512 * (b + 1)], PS[:, 1 + b, :],
                                        RAW[:, 3 * D + 512 * b:3 * D + 512 * (b + 1)], ALU.add).then_inc(gate_rows, 1)

            def split_lo(l, g):
                n = NG * l + g
                w = GROUPS[g][1]
                for k in range(KT):
                    dve.wait_ge(w_hi, KT * n + k + 1)
                    V.tensor_tensor(W[:, 1, k, 0:w], wraw[:, k, 0:w], W[:, 0, k, 0:w].bitcast(F32), ALU.subtract).then_inc(w_lo, 1)

            split_lo(0, G_UV)
            for l in range(DEPTH):
                s = S[l]
                ts = q_tiles(l)
                nq, ub = len(ts), unit_base(l)
                lo = ts[0] * P
                for ci, (a, b) in enumerate(NORM_CHUNKS):
                    dve.wait_ge(s["n_sq"], b + 10 * l)
                    V.tensor_scalar(stat[:, 1, a:b], stat[:, 0, a:b], 1.0 / D, EPS, ALU.mult, ALU.add).then_inc(s["n_ms"], 1)
                    dve.wait_ge(s["n_root"], ci + 1 + 3 * l)
                    V.reciprocal(stat[:, 1, a:b], stat[:, 1, a:b]).then_inc(s["n_rstd"], 1)
                    dve.wait_ge(s["n_rstd"], ci + 1 + 3 * l)
                    for r in range(a, b):
                        if l:
                            dve.wait_ge(S[l - 1]["x_out"], 16 * TILES)
                        V.tensor_scalar(X[:, r, :], X[:, r, :], stat[:, 1, r:r + 1], None, ALU.mult).then_inc(s["n_xn"], 1)
                for ci, (a, b) in enumerate(NORM_CHUNKS):
                    j = 1 if ci == 0 else 0
                    for k in range(KT):
                        n = KT * ci + k
                        w = P * (b - a)
                        ht = QX[:, XT + 1024 + 512 * (k % 4):XT + 1024 + 512 * (k % 4) + w]
                        dve.wait_ge(s["n_hi"], n + 1 + 24 * l)
                        if n >= 4:
                            dve.wait_ge(s["n_lo"], n - 3 + 24 * l)
                        V.tensor_scalar(ht, PS[:, k, 0:w], shA[:, l, 1, j, k:k + 1], shA[:, l, 0, j, k:k + 1],
                                        ALU.mult, ALU.add).then_inc(s["n_h"], 1)
                        dve.wait_ge(s["n_h"], n + 1 + 24 * l)
                        V.tensor_tensor(Hs[:, 1, k, P * a:P * b], ht, Hs[:, 0, k, P * a:P * b].bitcast(F32), ALU.subtract).then_inc(s["n_lo"], 1)
                split_lo(l, G_AZ)
                dve.wait_ge(s["sg_sq"], nq)
                V.tensor_scalar(stat[:, 0, ts[0]:], stat[:, 2, ts[0]:], 1.0 / 256, EPS, ALU.mult, ALU.add).then_inc(s["sg_ms"], 1)
                dve.wait_ge(s["sg_root"], 1 + 1 * l)
                V.reciprocal(stat[:, 0, ts[0]:], stat[:, 0, ts[0]:]).then_inc(s["sg_rstd"], 1)
                dve.wait_ge(s["sg_rstd"], 1 + 1 * l)
                dve.wait_ge(s["sg_in"], 32 + 32 * l)
                for r in ts:
                    V.scalar_tensor_tensor(out=uv[:, r, 256:512], in0=uv[:, r, 256:512], scalar=stat[:, 0, r:r + 1],
                                           in1=sguG[:, :], op0=ALU.mult, op1=ALU.mult).then_inc(s["sg_v"], 1)
                split_lo(l, G_CBC)
                half = nq // 2
                for hh in range(4):
                    for i in range(2):
                        a = ts[0] + half * i
                        u = uv[:, a:a + half, HD * hh:HD * (hh + 1)]
                        dve.wait_ge(s["sg_full"], 2 * hh + i + 1 + 8 * l)
                        V.scalar_tensor_tensor(out=u, in0=PS[:, 6 + i, 0:half * HD].rearrange("p (r n) -> p r n", n=HD),
                                               scalar=vc[:, l, V_SB + hh:V_SB + hh + 1], in1=u, op0=ALU.add, op1=ALU.mult).then_inc(s["sg_free"], 1)
                dve.wait_ge(s["sg_free"], 8 + 8 * l)
                dve.wait_ge(s["p_free"], ub[G_CBC])
                V.tensor_tensor(uv[:, ts[0]:, 0:256], uv[:, ts[0]:, 0:256], az[:, ts[0]:, :], ALU.mult).then_inc(s["ya_ready"], 1)
                split_lo(l, G_CXZ)
                for i in range(2):
                    dve.wait_ge(s["p_free"], ub[G_CXZ] + i + 1)
                    V.tensor_tensor(cbc[:, 2 + i, lo:], cbc[:, 2 + i, lo:], cxz[:, i, lo:], ALU.mult).then_inc(s["cc_cx"], 1)
                split_lo(l, G_BZ)
                nconv = 0
                for i in range(2):
                    t, acc = cbc[:, 2 + i, :], SM[:, 0:ROWS]
                    tap = [vc[:, l, V_CW + 2 * j + i:V_CW + 2 * j + i + 1] for j in range(3)]
                    dve.wait_ge(s["cc_cx"], i + 1 + 2 * l)
                    if i:
                        dve.wait_ge(s["yc_out"], 16 * i + 32 * l)
                    V.tensor_scalar(acc[:, lo:], t[:, lo:], tap[1], vc[:, l, V_CB + i:V_CB + i + 1], ALU.mult, ALU.add).then_inc(s["conv"], 1)
                    nconv += 1
                    for a, b in ([(0, 256), (256, ROWS)] if l == 0 else [(256, ROWS)]):
                        for j, (oa, ob, ia, ib) in enumerate(((a + 1, b, a, b - 1), (a, b - 1, a + 1, b))):
                            dve.wait_ge(s["conv"], nconv)
                            V.scalar_tensor_tensor(out=acc[:, oa:ob], in0=t[:, ia:ib], scalar=tap[2 * j], in1=acc[:, oa:ob],
                                                   op0=ALU.mult, op1=ALU.add).then_inc(s["conv"], 1)
                            nconv += 1
                    dve.wait_ge(s["conv"], nconv)
                    V.tensor_tensor(acc[:, lo:], acc[:, lo:], cbc[:, i, lo:], ALU.mult).then_inc(s["conv"], 1)
                    nconv += 1
                    dve.wait_ge(s["conv"], nconv)
                    dve.wait_ge(s["p_free"], ub[G_CXZ] + 3 + i)
                    V.tensor_tensor(acc[:, lo:], acc[:, lo:], cxz[:, i, lo:], ALU.mult).then_inc(s["yc_ready"], 1)
                split_lo(l, G_Q)
                if l == DEPTH - 1:
                    split_lo(l, G_K)
                g0 = G_Q if l < DEPTH - 1 else G_K
                with dve.Fori(0, G_O0 - g0) as i:
                    for k in range(KT):
                        dve.wait_ge(w_hi, i * KT + (KT * (NG * l + g0 + 1) + k + 1))
                        V.tensor_tensor(W[:, 1, k, :], wraw[:, k, :], W[:, 0, k, :].bitcast(F32), ALU.subtract).then_inc(w_lo, 1)

                nslot = head_slots(l)
                chunks = NORM_CHUNKS if l == 0 else NORM_CHUNKS[1:]
                nch = len(chunks)
                dve.wait_ge(s["p_free"], ub[-1])
                dve.wait_ge(w_lo, KT * (NG * l + G_O0 + 1))
                with dve.Fori(0, HEADS) as h:
                    for i in range(2):
                        src = qkv[:, CTX_TILES:TILES, bass.ds(h * P + GW * i, P)].rearrange("p r (m n) -> p r m n", m=2)
                        for m in range(2):
                            dst = rope[:, i, CTX_TILES:TILES, P * m:P * (m + 1)].rearrange("p r (d n) -> p r d n", d=2)
                            V.tensor_tensor(dst, src[:, :, m, :].unsqueeze(2).to_broadcast([P, LAT_TILES, 2, HD]),
                                            cosT[:, :, :].unsqueeze(2).to_broadcast([P, LAT_TILES, 2, HD]), ALU.mult).then_inc(s["rope_mul"], 1)
                    dve.wait_ge(s["v_hi"], h + 1 + 4 * l)
                    V.tensor_tensor(vhl[:, 1, :, :], qkv[:, :, bass.ds(h * P + 2 * GW, P)], vhl[:, 0, :, :].bitcast(F32),
                                    ALU.subtract).then_inc(s["v_lo"], 1)
                    for i in range(2):
                        dve.wait_ge(s["rope_mul"], h * 4 + 2 * (i + 1) + 16 * l)
                        dve.wait_ge(s["rope_swap"], h * 8 + 4 * (i + 1) + 32 * l)
                        for m in range(2):
                            dst = rope[:, i, CTX_TILES:TILES, P * m:P * (m + 1)].rearrange("p r (d n) -> p r d n", d=2)
                            t = V.tensor_tensor(dst, dst, swap[:, :, HD * m:HD * (m + 1)].unsqueeze(2).to_broadcast(
                                [P, LAT_TILES, 2, HD]), ALU.add)
                        t.then_inc(s["rope_ready"], 1)
                    n = 0
                    for i, turns in enumerate((q_turns(l), K_TURNS)):
                        for m in range(2):
                            for r0, r1 in turns:
                                dve.wait_ge(s["slot_hi"], h * nslot + (n + 1))
                                w = P * (r1 - r0)
                                if i == 0:
                                    q = qst[HD:P, m, P * r0:P * r1]
                                    V.scalar_tensor_tensor(out=q, in0=PS[HD:P, 6 + n % 2, 0:w], scalar=SC, in1=q.bitcast(F32),
                                                           op0=ALU.mult, op1=ALU.subtract).then_inc(s["slot_free"], 1)
                                else:
                                    V.tensor_tensor(kst[:, 1, m, P * r0:P * r1], PS[:, 6 + n % 2, 0:w],
                                                    kst[:, 0, m, P * r0:P * r1].bitcast(F32), ALU.subtract).then_inc(s["slot_free"], 1)
                                n += 1

                    def coef(t):
                        b = (t - ts[0]) % 2
                        n = h * nq + (t - ts[0] + 1)
                        z0, z1 = Z[:, 0, b:b + 1], Z[:, 1, b:b + 1]
                        dve.wait_ge(s["exp0"], n)
                        V.tensor_scalar(rz[:, 1, b:b + 1], z0, nlam[:, l:l + 1], None, ALU.mult)
                        V.scalar_tensor_tensor(out=ez[:, t:t + 1], in0=z0, scalar=EPS * P, in1=z0, op0=ALU.mult, op1=ALU.mult)
                        dve.wait_ge(s["exp1"], n)
                        V.reciprocal(rz[:, 0, b:b + 1], z1).then_inc(s["rz_done"], 1)
                        dve.wait_ge(s["rz_done"], n)
                        V.tensor_tensor(rz[:, 3, b:b + 1], rz[:, 1, b:b + 1], rz[:, 0, b:b + 1], ALU.mult).then_inc(s["coef"], 1)

                    def combine_low(t):
                        b = (t - ts[0]) % 2
                        half = (256 if t < CTX_TILES else ROWS) // 2
                        e0, e1 = prob[:, b, 0, 0:half], prob[:, b, 1, 0:half]
                        dve.wait_ge(s["coef"], h * nq + (t - ts[0] + 1))
                        V.scalar_tensor_tensor(out=e0, in0=e1, scalar=rz[:, 3, b:b + 1], in1=e0,
                                               op0=ALU.mult, op1=ALU.add).then_inc(s["comb_low"], 1)

                    for tile, behind in head_rounds(l):
                        q = tile - ts[0]
                        w = 256 if tile < CTX_TILES else ROWS
                        for m in range(2):
                            dve.wait_ge(s[f"s_full{m}"], h * nq + (q + 1))
                            V.tensor_reduce(nmax[:, m, q % 2:q % 2 + 1], PF[:, 1536 * m:1536 * m + w], AX.X, ALU.max,
                                            negate=True).then_inc(s[f"max{m}"], 1)
                        coef_due = True
                        if not behind or behind[0][0] != "turn":
                            coef(tile)
                            combine_low(tile)
                            coef_due = False
                        for kind, what in behind:
                            if kind == "turn":
                                q = (what - chunk_of(what)[0]) * P
                                for k0, k1 in key_turns(what):
                                    if coef_due and k0:
                                        coef(tile)
                                    dve.wait_ge(s["slot_hi"], h * nslot + (n + 1))
                                    V.tensor_tensor(aT[:, 1, k0:k1, q:q + P],
                                                    PS[:, 6 + n % 2, 0:P * (k1 - k0)].rearrange("p (k q) -> p k q", q=P),
                                                    aT[:, 0, k0:k1, q:q + P].bitcast(F32), ALU.subtract).then_inc(s["slot_free"], 1)
                                    if coef_due and k0:
                                        combine_low(tile)
                                        coef_due = False
                                    n += 1
                            ch = None if kind == "turn" else chunks.index(what)
                            o = SM[:, 1024:1536]
                            if kind == "values":
                                w = P * (what[1] - what[0])
                                dve.wait_ge(s["slot_hi"], h * nslot + (n + 1))
                                dve.wait_ge(s["y_out"], h * (16 * nch) + (16 * ch + 32))
                                V.tensor_scalar(o[:, 0:w], PS[:, 6 + n % 2, 0:w], gsub[:, l:l + 1], None, ALU.mult).then_inc(s["slot_free"], 1)
                                for r in range(*what):
                                    sq = SM[:, P * (r - what[0]):P * (r - what[0] + 1)]
                                    t = V.scalar_tensor_tensor(out=sq, in0=ident[:, :], scalar=ez[:, r:r + 1], in1=sq,
                                                               op0=ALU.mult, op1=ALU.add)
                                t.then_inc(s["sq_done"], 1)
                                n += 1
                            if kind == "rms":
                                w = P * (what[1] - what[0])
                                dve.wait_ge(s["slot_free"], h * nslot + n)
                                dve.wait_ge(s["slot_hi"], h * nslot + (n + 1))
                                V.tensor_tensor(o[:, 0:w], o[:, 0:w], SM[:, 512:512 + w], ALU.mult).then_inc(s["slot_free"], 1)
                                dve.wait_ge(s["slot_free"], h * nslot + (n + 1))
                                dve.wait_ge(s["bzh_in"], h * (16 * nch) + 16 * (ch + 1))
                                V.tensor_tensor(o[:, 0:w], o[:, 0:w], SM[:, 1536:1536 + w], ALU.mult).then_inc(s["yb_ready"], 1)
                                n += 1
                        if coef_due:
                            coef(tile)
                            combine_low(tile)
                for i in range(KT):
                    dve.wait_ge(s["y_hi"], i + 1 + 8 * l)
                    o = XT + ROWS * (i % 4)
                    V.tensor_tensor(Hs[:, 1, i, lo:], QX[:, o + lo:o + ROWS], Hs[:, 0, i, lo:].bitcast(F32), ALU.subtract).then_inc(s["y_lo"], 1)
                dve.wait_ge(s["gate_in"], 32 + 32 * l)
                dve.wait_ge(s["y_lo"], KT + 8 * l)
                dve.wait_ge(s["x_in"][0], 48 + 16 * l)
                for g in range(2):
                    for n, r in enumerate(ts):
                        if g == 0 and n == nq - 1:
                            split_lo(l, G_O1)
                        if g == 1 and n == nq - 1 and l < DEPTH - 1:
                            split_lo(l + 1, G_UV)
                        u = nq * g + n
                        z = QX[:, XT + 4096 + 512 * (u % 2):XT + 4608 + 512 * (u % 2)]
                        j = 1 if r < CTX_TILES else 0
                        dve.wait_ge(s["o_full"], u + 1)
                        if u >= 2:
                            dve.wait_ge(s["o_x"], u - 1)
                        V.tensor_tensor(z, PS[:, u % 5, :], SM[:, D * j + GW * g:D * j + GW * (g + 1)], ALU.mult).then_inc(s["o_z"], 1)
                        dve.wait_ge(s["o_z"], u + 1)
                        xs = X[:, r, GW * g:GW * (g + 1)]
                        V.tensor_tensor(xs, xs, z, ALU.add).then_inc(s["o_x"], 1)
                        if g == 1 and l == DEPTH - 1:
                            dve.wait_ge(s["f_sq"], n + 1)
                            V.tensor_scalar(stat[:, 1, r:r + 1], stat[:, 0, r:r + 1], 1.0 / D, EPS, ALU.mult, ALU.add).then_inc(s["f_ms"], 1)
                            dve.wait_ge(s["f_root"], n + 1)
                            V.reciprocal(stat[:, 1, r:r + 1], stat[:, 1, r:r + 1]).then_inc(s["f_rstd"], 1)
                            dve.wait_ge(s["f_rstd"], n + 1)
                            dve.wait_ge(s["fg_in"], 16)
                            V.scalar_tensor_tensor(out=X[:, r, :], in0=X[:, r, :], scalar=stat[:, 1, r:r + 1],
                                                   in1=QX[:, XT + 1024:XT + 2048], op0=ALU.mult, op1=ALU.mult).then_inc(s["f_y"], 1)


def rope_tables():
    row = np.repeat(np.arange(LAT_TILES * P // GRID_W), GRID_W).astype(np.float32)
    col = np.tile(np.arange(GRID_W), LAT_TILES * P // GRID_W).astype(np.float32)
    n = HD // 4
    inv = (np.float32(10000.0) ** (-np.arange(n, dtype=np.float32) / np.float32(n))).astype(np.float32)
    cos, sin = [], []
    for pos in (row, col):
        ang = pos[:, None] * inv
        cos += [np.cos(ang), np.cos(ang)]
        sin += [-np.sin(ang), np.sin(ang)]
    lay = lambda a: np.ascontiguousarray(np.concatenate(a, 1).astype(np.float32).reshape(LAT_TILES, P, HD).transpose(1, 0, 2))
    return lay(cos), lay(sin)


_INS = ["x", "c", "ctx", "c_ctx", "w_mod", "b_mod", "norm_g", "w_in", "w_out", "sgu_norm_g", "sgu_w", "sgu_b",
        "lambda_q1", "lambda_k1", "lambda_q2", "lambda_k2", "subln_g", "conv_w", "conv_b", "final_g"]


def kernel(**inputs):
    import concourse.bacc as _bacc
    from concourse.bass_utils import run_bass_kernel_spmd as _run

    nc = _bacc.Bacc("TRN2", target_bir_lowering=False, num_devices=1)
    arrays, args = {}, []
    cos, sin = rope_tables()
    for name, a in [(n, np.ascontiguousarray(inputs[n])) for n in _INS] + [("cos_t", cos), ("sin_t", sin)]:
        arrays[f"in_{name}"] = a
        args.append(nc.dram_tensor(f"in_{name}", a.shape, mybir.dt.from_np(a.dtype), kind="ExternalInput").ap())
    args.append(nc.dram_tensor("out_0", (1, LAT_TILES * P, D), F32, kind="ExternalOutput").ap())
    for name, shape in (("x1_d", (TILES, P, D)), ("yT_d", (KT, P, ROWS)), ("bz_d", (HEADS, P, ROWS)),
                        ("gate_d", (DEPTH, 2, P, D))):
        args.append(nc.dram_tensor(name, shape, F32, kind="Internal").ap())
    build(nc, *args)
    r = _run(nc, [arrays], core_ids=[0])
    return r.results[0]["out_0"]
```

```python
import math
from contextlib import ExitStack

import numpy as np

import concourse.bass as bass
from concourse import mybir

F32 = mybir.dt.float32
F32R = mybir.dt.float32r
ACT = mybir.ActivationFunctionType
ALU = mybir.AluOpType
AX = mybir.AxisListType

P = 128
D = 1024
KT = D // P
DEPTH = 2
CTX_TILES = 2
LAT_TILES = 8
TILES = CTX_TILES + LAT_TILES
ROWS = TILES * P
D_IN = 3840
GRID_W = 64
HEADS = 4
HD = 64
EPS = 1e-6
GW = 512

COL_U, COL_AZ, COL_Q, COL_K, COL_V, COL_BZ, COL_CB, COL_CX = 0, 512, 768, 1280, 1792, 2304, 2816, 3328
GROUPS = [(COL_U, 512), (COL_AZ, 256), (COL_CB, 512), (COL_CX, 512), (COL_BZ, 512),
          (COL_Q, 512), (COL_K, 512), (COL_V, 512), (0, 512), (512, 512)]
G_UV, G_AZ, G_CBC, G_CXZ, G_BZ, G_Q, G_K, G_V, G_O0, G_O1 = range(10)
NG = len(GROUPS)
NORM_CHUNKS = [(0, 2), (2, 6), (6, 10)]
SC = 1.0 / math.sqrt(HD)

V_BSH, V_BSC, V_G, V_SUB, V_CW, V_CB, V_SB, V_ROWS = 0, 8, 16, 24, 25, 31, 33, 37


def q_tiles(l):
    return list(range(TILES)) if l < DEPTH - 1 else list(range(CTX_TILES, TILES))


def row_chunks(l):
    c = [(0, 256, 0, 256), (256, 512, 1, 0), (768, 512, 2, 0)]
    return c if l < DEPTH - 1 else c[1:]


def lam_init(l):
    return 0.8 - 0.6 * math.exp(-0.3 * l)


def q_turns(l):
    return [(0, 4), (4, 8), (8, 10)] if l < DEPTH - 1 else [(2, 6), (6, 10)]


K_TURNS = [(0, 4), (4, 8), (8, 10)]
LOW_KEYS = 6
PREP_BANKS = (0, 1, 2, 6, 7)


def key_turns(t):
    return [(0, 2)] if t < CTX_TILES else [(0, 4), (4, LOW_KEYS), (LOW_KEYS, TILES)]


def chunk_of(t):
    return (0, 2) if t < 2 else ((2, 6) if t < 6 else (6, 10))


def chunk_due(l, n):
    t = q_tiles(l)[n] if n >= 0 else None
    return chunk_of(t) if t is not None and chunk_of(t)[1] == t + 1 else None


def prep_turns(l):
    return [(i, m, r0, r1) for i, turns in enumerate((q_turns(l), K_TURNS)) for m in range(2) for r0, r1 in turns]


def slot_plan(l):
    what = []
    for t in range(1, len(q_tiles(l)) + 1):
        if chunk_due(l, t - 2):
            what.append("values")
        what += ["turn"] * len(key_turns(q_tiles(l)[t - 1]))
    what.append("values")
    banks = [6 + n % 2 for n in range(len(what))]
    banks += [PREP_BANKS[n % 5] for n in range(len(prep_turns(l)))]
    what += ["prep"] * len(prep_turns(l))
    total = len(banks)
    plan = []
    for n, b in enumerate(banks):
        back = next(d for d in range(1, total + 1) if banks[(n - d) % total] == b)
        plan.append((what[n], b, back))
    return plan


def build(nc, x, c, ctx_in, c_ctx, w_mod, b_mod, norm_g, w_in, w_out, sgu_g, sgu_w, sgu_b,
          lq1, lk1, lq2, lk2, subln_g, conv_w, conv_b, final_g, cos_t, sin_t, out,
          x1_d, yT_d, bz_d, gate_d):
    with ExitStack() as st:
        def sb(name, shape, dt=F32):
            return st.enter_context(nc.sbuf_tensor(name, shape, dt))

        def sem(name):
            return st.enter_context(nc.semaphore(name))

        H = sb("H", [P, 2 * KT * ROWS], F32R)
        QX = sb("QX", [P, TILES * 3 * GW])
        W = sb("W", [P, 2, KT, GW], F32R)
        RAW = sb("RAW", [P, 4 * ROWS])
        SM = sb("SM", [P, ROWS + LAT_TILES * P])
        ident = sb("ident", [P, P])
        ones = sb("ones", [P, P])
        cosT = sb("cosT", [P, LAT_TILES, HD])
        sinT = sb("sinT", [P, LAT_TILES, HD])
        vc = sb("vc", [P, DEPTH, V_ROWS])
        condT = sb("condT", [P, 2, KT])
        shA = sb("shA", [P, DEPTH, 2, 2, KT])
        stat = sb("stat", [P, 3, TILES])
        lamE = sb("lamE", [P, DEPTH, 4])
        nlam = sb("nlam", [P, DEPTH])
        gsub = sb("gsub", [P, DEPTH])
        nmax = sb("nmax", [P, 2, 2])
        Z = sb("Z", [P, 2, 2])
        rz = sb("rz", [P, 4, 2])
        ez = sb("ez", [P, TILES])
        PS = st.enter_context(nc.psum_tensor("PS", [P, 8, 512], F32))
        PF = PS[:, :, :].rearrange("p b n -> p (b n)")

        Hs = H[:, :].rearrange("p (s k n) -> p s k n", s=2, k=KT)
        X = QX[:, 0:TILES * D].rearrange("p (r d) -> p r d", d=D)
        XT = TILES * D
        uv = QX[:, 0:5120].rearrange("p (r n) -> p r n", n=512)
        az = QX[:, 5120:7680].rearrange("p (r n) -> p r n", n=256)
        cbc = QX[:, 7680:12800].rearrange("p (c n) -> p c n", c=4)
        cxz = QX[:, 12800:15360].rearrange("p (c n) -> p c n", c=2)
        ws_in = QX[:, 12800:13312].rearrange("p (h n) -> p h n", h=4)
        wsT = QX[:, 13312:13824].rearrange("p (h n) -> p h n", h=4)
        bzs = QX[:, 0:5120].rearrange("p (c n) -> p c n", c=4)
        qkv = QX[:, :].rearrange("p (r n) -> p r n", n=3 * GW)
        wraw = RAW[:, 0:KT * GW].rearrange("p (k n) -> p k n", k=KT)
        sguG = SM[:, 2048:2304]
        kst = H[:, 0:5120].rearrange("p (s m n) -> p s m n", s=2, m=2)
        qst = H[:, 5120:7680].rearrange("p (m n) -> p m n", m=2)
        vhl = H[:, 7680:10240].rearrange("p (s r e) -> p s r e", s=2, e=P)
        aT = H[:, 10240:20480].rearrange("p (s k q) -> p s k q", s=2, q=512)
        prob = RAW[:, :].rearrange("p (b m n) -> p b m n", b=2, m=2)
        rope = RAW[:, :].rearrange("p (b r n) -> p b r n", b=2, n=2 * P)

        def head_cols(h, off):
            return slice(off, off + P) if h is None else bass.ds(h * P + off, P)

        def swapped(h, i):
            if i == 0 and h is not None:
                return qkv[:, CTX_TILES:TILES, bass.ds(h * P + GW, P)]
            return SM[:, ROWS * i:ROWS * i + LAT_TILES * P].rearrange("p (r n) -> p r n", n=P)

        vec_in, tab_in = sem("vec_in"), sem("tab_in")
        ident_ready, setup_turned, setup_cols = sem("ident_ready"), sem("setup_turned"), sem("setup_cols")
        cond_ready, lam_dve, lam_exp = sem("cond_ready"), sem("lam_dve"), sem("lam_exp")
        wm_in = [sem(f"wm_in{b}") for b in range(5)]
        wm_used, mod_sums, mod_rows = sem("wm_used"), sem("mod_sums"), sem("mod_rows")
        mod_turned, mod_cols, gate_sums = sem("mod_turned"), sem("mod_cols"), sem("gate_sums")
        gate_rows, gate_out, bgate_in = sem("gate_rows"), sem("gate_out"), sem("bgate_in")
        w_raw, w_hi, w_lo, w_used = sem("w_raw"), sem("w_hi"), sem("w_lo"), sem("w_used")
        shared = [
            "n_sq", "n_ms", "n_root", "n_rstd", "n_xn", "n_turned", "n_hi", "n_h", "sg_ms",
            "sg_root", "sg_rstd", "sg_in", "sgw_turned", "sgw_ready", "sg_full", "sg_free",
            "ya_ready", "cc_cx", "yc_ready", "yc_out", "bz_ready", "bz_out", "rope_mul",
            "rope_swap", "rope_ready", "ctx_qk", "v_hi", "v_lo", "gate_in", "y_hi", "y_lo", "n_lo"]
        own = [
            "p_full", "p_free", "sg_sq", "sg_v", "ya_turned", "ya_cols", "conv", "slot_full",
            "slot_hi", "slot_free", "max0", "max1", "s_full0", "s_full1", "exp0", "exp1", "rz_done",
            "coef", "comb", "comb_mul", "comb_low", "sq_done", "ms_full", "ln_done", "rstd_done", "yb_ready",
            "y_out", "bzh_in", "o_full", "o_z",
            "o_x"]
        once = [
            "f_sq", "f_ms", "f_root", "f_rstd", "f_y", "f_out", "fg_in", "x_out"]
        common = {n: sem(n) for n in shared + once}
        common["x_in"] = [sem(f"x_in{i}") for i in range(3)]
        common["y_in"] = [sem(f"y_in{i}") for i in range(4)]
        S = [{**common, **{n: sem(f"L{l}_{n}") for n in own}} for l in range(DEPTH)]

        def unit_base(l):
            nq = len(q_tiles(l))
            base, n = [], 0
            for units in (nq, nq, 4, 4, 4, nq, TILES, TILES):
                base.append(n)
                n += units
            return base + [n]

        def group_end(l, g):
            if g >= G_O0:
                return S[l]["o_full"], len(q_tiles(l)) * (g - G_O0 + 1)
            return S[l]["p_full"], unit_base(l)[g + 1]

        block = st.enter_context(nc.Block())

        @block.sync
        def _(sp):
            for l in range(DEPTH):
                v = RAW[0:V_ROWS, 256 * l:256 * l + P]
                rows = [(V_BSH, b_mod[l, 0:2 * D], 16), (V_G, norm_g[l, :], 8), (V_SUB, subln_g[l, :], 1)]
                for at, src, n in rows:
                    sp.dma_start(v[at:at + n, :], src.rearrange("(n p) -> n p", p=P)).then_inc(vec_in, 16)
                sp.dma_start(v[V_CW:V_CW + 6, :], conv_w[l].rearrange("w (n p) -> (w n) p", p=P)).then_inc(vec_in, 16)
                sp.dma_start(v[V_CB:V_CB + 2, :], conv_b[l].rearrange("(n p) -> n p", p=P)).then_inc(vec_in, 16)
                sp.dma_start(v[V_SB:V_SB + 4, :], sgu_b[l]).then_inc(vec_in, 16)
                for i, a in enumerate((lq1, lk1, lq2, lk2)):
                    sp.dma_start(SM[:, 256 * l + HD * i:256 * l + HD * (i + 1)],
                                 a[l].partition_broadcast(P)).then_inc(vec_in, 16)
            sp.dma_start(RAW[0:8, 512:640], c[0].rearrange("(n p) -> n p", p=P)).then_inc(vec_in, 16)
            sp.dma_start(RAW[8:16, 512:640], c_ctx.rearrange("(n p) -> n p", p=P)).then_inc(vec_in, 16)
            def load_gate_bias(l):
                sp.dma_start(RAW[:, 3 * D:4 * D], b_mod[l, 2 * D:3 * D].partition_broadcast(P)).then_inc(bgate_in, 16)

            def store_gates(l):
                for j in range(2):
                    sp.wait_ge(gate_rows, 4 * l + 2 * j + 2)
                    sp.dma_start(gate_d[l, j], RAW[:, 4 * D:5 * D]).then_inc(gate_out, 16)

            for j in range(DEPTH * KT):
                if j >= 5:
                    sp.wait_ge(wm_used, j - 4)
                sp.dma_start(QX[:, 3 * D * (j % 5):3 * D * (j % 5 + 1)],
                             w_mod[j // KT, P * (j % KT):P * (j % KT + 1), :]).then_inc(wm_in[j % 5], 16)
                if j == 4:
                    sp.wait_ge(setup_turned, 1)
                    load_gate_bias(0)
                    sp.dma_start(cosT[:, :, :], cos_t).then_inc(tab_in, 16)
                    sp.dma_start(sinT[:, :, :], sin_t).then_inc(tab_in, 16)
                if j == KT + 4:
                    store_gates(0)
                    load_gate_bias(1)
            store_gates(1)

            def load_group(l, g):
                n = NG * l + g
                if n:
                    sp.wait_ge(w_lo, KT * n)
                else:
                    sp.wait_ge(gate_out, 16 * 2 * DEPTH)
                col, w = GROUPS[g]
                src = (w_out if g >= G_O0 else w_in)[l, :, col:col + w]
                sp.dma_start(wraw[:, :, 0:w], src.rearrange("(k p) n -> p k n", p=P)).then_inc(w_raw, 16)

            for l in range(DEPTH):
                s = S[l]
                ts = q_tiles(l)
                nq, lo_row = len(ts), ts[0] * P
                if l == 0:
                    load_group(l, G_UV)
                    sp.wait_ge(wm_used, DEPTH * KT)
                    sp.dma_start(X[:, 0:2, :], ctx_in[0].rearrange("(r p) d -> p r d", p=P)).then_inc(s["x_in"][0], 16)
                    xv = x[0].rearrange("(r p) d -> p r d", p=P)
                    sp.dma_start(X[:, 2:6, :], xv[:, 0:4, :]).then_inc(s["x_in"][1], 16)
                    sp.dma_start(X[:, 6:10, :], xv[:, 4:8, :]).then_inc(s["x_in"][2], 16)
                if l:
                    sp.wait_ge(S[l - 1]["sg_v"], len(q_tiles(l - 1)))
                sp.dma_start(sguG[:, :], sgu_g[l].partition_broadcast(P)).then_inc(s["sg_in"], 16)
                load_group(l, G_AZ)
                sp.wait_ge(s["n_lo"], 8 * len(NORM_CHUNKS) + 24 * l)
                sp.dma_start(ws_in, sgu_w[l].rearrange("h p q -> p h q")).then_inc(s["sg_in"], 16)
                load_group(l, G_CBC)
                load_group(l, G_CXZ)
                load_group(l, G_BZ)
                sp.wait_ge(s["ya_cols"], 6 if l == 0 else 4)
                for a in range(2):
                    sp.dma_start(yT_d[a, :, lo_row:ROWS].rearrange("p (r n) -> p r n", n=P),
                                 uv[:, ts[0]:TILES, 256 + P * a:256 + P * (a + 1)]).then_inc(s["y_out"], 16)
                load_group(l, G_Q)
                for i in range(2):
                    sp.wait_ge(s["yc_ready"], i + 1 + 2 * l)
                    sp.dma_start(yT_d[6 + i, :, lo_row:ROWS], SM[:, lo_row:ROWS]).then_inc(s["yc_out"], 16)
                for i in range(4):
                    sp.wait_ge(s["bz_ready"], i + 1 + 4 * l)
                    sp.dma_start(bz_d[i, :, lo_row:ROWS], bzs[:, i, lo_row:ROWS]).then_inc(s["bz_out"], 16)
                load_group(l, G_K)
                load_group(l, G_V)
                load_group(l, G_O0)
                with sp.Fori(0, HEADS) as h:
                    sp.wait_ge(s["v_lo"], h + (1 + 4 * l))
                    sp.dma_start(qkv[:, ts[0]:TILES, bass.ds(h * P + 2 * GW, P)],
                                 bz_d[bass.ds(h, 1), :, lo_row:ROWS].rearrange("o p (r n) -> p (o r) n", n=P)).then_inc(s["bzh_in"], 16)
                    sp.wait_ge(s["yb_ready"], h + 1)
                    sp.dma_start(yT_d[bass.ds(h + 2, 1), :, lo_row:ROWS].rearrange("o p (r n) -> p (o r) n", n=P),
                                 qkv[:, ts[0]:TILES, bass.ds(h * P, P)]).then_inc(s["y_out"], 16)
                sp.wait_ge(s["y_out"], 16 * HEADS + 32)
                sp.wait_ge(s["yc_out"], 32 + 32 * l)
                sp.wait_ge(s["slot_free"], HEADS * len(slot_plan(l)) + len(prep_turns(l)))
                for j in range(2):
                    sp.dma_start(SM[:, D * j:D * (j + 1)], gate_d[l, j]).then_inc(s["gate_in"], 16)
                for i in range(KT):
                    if i >= 4:
                        sp.wait_ge(s["y_lo"], i - 3 + 8 * l)
                    o = XT + ROWS * (i % 4)
                    sp.dma_start(QX[:, o + lo_row:o + ROWS], yT_d[i, :, lo_row:ROWS]).then_inc(s["y_in"][i % 4], 16)
                if l == 0:
                    x0 = S[l]["x_in"][0]
                    sp.dma_start(X[:, 0:2, :], ctx_in[0].rearrange("(r p) d -> p r d", p=P)).then_inc(x0, 16)
                    sp.dma_start(X[:, 2:10, :], x[0].rearrange("(r p) d -> p r d", p=P)).then_inc(x0, 16)
                else:
                    sp.wait_ge(S[0]["x_out"], 16 * TILES)
                    sp.dma_start(X[:, 2:10, :], x1_d[2:10].rearrange("r p d -> p r d")).then_inc(s["x_in"][0], 16)
                load_group(l, G_O1)
                if l == 0:
                    load_group(l + 1, G_UV)
                    for n, r in enumerate(ts):
                        sp.wait_ge(s["o_x"], nq + n + 1)
                        sp.dma_start(x1_d[r], X[:, r, :]).then_inc(s["x_out"], 16)
                else:
                    sp.wait_ge(s["y_lo"], KT + 8 * l)
                    sp.dma_start(QX[:, XT + 1024:XT + 2048], final_g.partition_broadcast(P)).then_inc(s["fg_in"], 16)
                    for n, r in enumerate(ts):
                        sp.wait_ge(s["f_y"], n + 1)
                        sp.dma_start(out[0, P * n:P * (n + 1), :], X[:, r, :]).then_inc(s["f_out"], 16)
                    sp.wait_ge(s["f_out"], 16 * nq)

        @block.gpsimd
        def _(pool):
            nc.gpsimd.memset(ident[:, :], 0.0).then_inc(ident_ready, 1)
            pool.wait_ge(ident_ready, 1)
            nc.gpsimd.affine_select(out=ident[:, :], in_=ident[:, :], compare_op=ALU.not_equal, fill=1.0,
                                    base=0, pattern=[[-1, P]], channel_multiplier=1).then_inc(ident_ready, 1)
            nc.gpsimd.memset(ones[:, :], 1.0 / P).then_inc(ident_ready, 1)
            pool.wait_ge(tab_in, 32)
            for l in range(DEPTH):
                s = S[l]
                nq, n0 = len(q_tiles(l)), q_tiles(l)[0]
                pool.wait_ge(s["p_full"], unit_base(l)[-1])
                pool.wait_ge(s["p_free"], unit_base(l)[-1])
                pool.wait_ge(w_lo, KT * (NG * l + G_O0 + 1))

                def swap_halves(h, off, i):
                    src = qkv[:, CTX_TILES:TILES, head_cols(h, off + GW * i)].rearrange("p r (a f e) -> p r a f e", f=2, e=16)
                    dst = swapped(h, i).rearrange("p r (a f e) -> p r a f e", f=2, e=16)
                    tab = sinT[:, :, :].rearrange("p r (a f e) -> p r a f e", f=2, e=16)
                    for m in range(2):
                        for f in range(2):
                            nc.gpsimd.tensor_tensor(dst[:, :, 2 * m:2 * m + 2, f, :], src[:, :, 2 * m:2 * m + 2, 1 - f, :],
                                                    tab[:, :, :, f, :], ALU.mult).then_inc(s["rope_swap"], 1)

                swap_halves(None, 0, 0)
                swap_halves(None, 0, 1)
                with pool.Fori(0, HEADS) as h:
                    full = 0
                    for n in range(nq):
                        if n + n0 >= CTX_TILES:
                            b = n % 2
                            pool.wait_ge(s["coef"], h * nq + (n + 1))
                            e0, e1 = prob[:, b, 0, P * LOW_KEYS:], prob[:, b, 1, P * LOW_KEYS:]
                            nc.gpsimd.tensor_tensor(e1, e1, rz[:, 3, b:b + 1].to_broadcast([P, ROWS - P * LOW_KEYS]), ALU.mult).then_inc(s["comb_mul"], 1)
                            pool.wait_ge(s["comb_mul"], h * LAT_TILES + (full + 1))
                            nc.gpsimd.tensor_tensor(e0, e0, e1, ALU.add).then_inc(s["comb"], 1)
                            full += 1
                        if n == 0:
                            pool.wait_ge(s["v_hi"], h + (1 + 4 * l))
                            nc.gpsimd.tensor_tensor(vhl[:, 1, :, :], qkv[:, :, bass.ds(h * P + 2 * GW, P)],
                                                    vhl[:, 0, :, :].bitcast(F32), ALU.subtract).then_inc(s["v_lo"], 1)
                        if n == nq - 4:
                            swap_halves(h, P, 0)
                        if n == nq - 3:
                            swap_halves(h, P, 1)
                    y = qkv[:, n0:, bass.ds(h * P, P)]
                    pool.wait_ge(s["rstd_done"], h + 1)
                    pool.wait_ge(s["sq_done"], h * (3 - l) + (3 - l))
                    nc.gpsimd.tensor_tensor(y, y, SM[:, P * n0:ROWS].rearrange("p (r n) -> p r n", n=P), ALU.mult).then_inc(s["yb_ready"], 1)

        @block.tensor
        def _(pe):
            mm = nc.tensor.matmul
            pe.wait_ge(ident_ready, 3)
            pe.wait_ge(vec_in, 16 * 22)
            for l in range(DEPTH):
                nc.tensor.transpose(PS[:, 0, 64 * l:64 * l + V_ROWS], RAW[0:V_ROWS, 256 * l:256 * l + P],
                                    ident[0:V_ROWS, 0:V_ROWS])
            nc.tensor.transpose(PS[:, 0, 128:144], RAW[0:16, 512:640], ident[0:16, 0:16]).then_inc(setup_turned, 1)
            pe.wait_ge(cond_ready, 1)
            for l in range(DEPTH):
                if l:
                    pe.wait_ge(mod_rows, 6 * l)
                    pe.wait_ge(gate_rows, 4 * l)
                for k in range(KT):
                    j = KT * l + k
                    pe.wait_ge(wm_in[j % 5], 16 * (j // 5 + 1))
                    for b in range(6):
                        o = 3 * D * (j % 5) + 512 * b
                        last = mm(PS[0:2, 1 + b, :], condT[:, :, k], QX[:, o:o + 512], start=(k == 0), stop=(k == KT - 1))
                    last.then_inc(wm_used, 1)
                pe.wait_ge(mod_rows, 6 * l + 6)
                for n in range(16):
                    last = nc.tensor.transpose(PS[:, 7, 2 * n:2 * n + 2], RAW[0:2, P * n:P * (n + 1)], ident[0:2, 0:2])
                last.then_inc(mod_turned, 1)
                for j in range(2):
                    for b in range(2):
                        if j:
                            pe.wait_ge(gate_rows, 4 * l + 2 * (j - 1) + b + 1)
                        mm(PS[:, 1 + b, :], ident[0:2, j:j + 1].to_broadcast([2, P]), RAW[0:2, 2 * D + 512 * b:2 * D + 512 * (b + 1)],
                           start=True, stop=True).then_inc(gate_sums, 1)

            def three(o, wt, mv, start, stop):
                mm(o, wt(0), mv(0), start=start, stop=False)
                mm(o, wt(0), mv(1), start=False, stop=False)
                return mm(o, wt(1), mv(0), start=False, stop=stop)

            def rows_unit(bank, r, w, wait_n, last_of_group):
                for k in range(KT):
                    if wait_n is not None:
                        pe.wait_ge(w_lo, wait_n + k + 1)
                    t = three(PS[:, bank, 0:w], lambda i: Hs[:, i, k, P * r:P * (r + 1)],
                              lambda i: W[:, i, k, 0:w], k == 0, k == KT - 1)
                    if last_of_group and k < KT - 1:
                        t.then_inc(w_used, 1)
                return t

            def cols_unit(bank, ct, l, wait_n, last_of_group):
                for k in range(KT):
                    if wait_n is not None:
                        pe.wait_ge(w_lo, wait_n + k + 1)
                    for r0, n, b, o in row_chunks(l):
                        t = three(PS[:, bank + b, o:o + n], lambda i: W[:, i, k, P * ct:P * (ct + 1)],
                                  lambda i: Hs[:, i, k, r0:r0 + n], k == 0, k == KT - 1)
                    if last_of_group and k < KT - 1:
                        t.then_inc(w_used, 1)
                return t

            for l in range(DEPTH):
                s = S[l]
                ts = q_tiles(l)
                nq, ub, lo_row = len(ts), unit_base(l), ts[0] * P
                if l == 0:
                    pe.wait_ge(mod_cols, DEPTH * 2)
                    pe.wait_ge(gate_rows, 4 * DEPTH)
                else:
                    pe.wait_ge(S[l - 1]["o_z"], 2 * len(q_tiles(l - 1)))
                for ci, (a, b) in enumerate(NORM_CHUNKS):
                    for k in range(KT):
                        if k == 0:
                            pe.wait_ge(s["n_xn"], b + 10 * l)
                        if ci:
                            pe.wait_ge(s["n_lo"], KT * (ci - 1) + k + 1 + 24 * l)
                        for r in range(a, b):
                            t = nc.tensor.transpose(PS[:, k, P * (r - a):P * (r - a + 1)], X[:, r, P * k:P * (k + 1)], ident[:, :])
                        t.then_inc(s["n_turned"], 1)
                pe.wait_ge(s["n_lo"], KT * len(NORM_CHUNKS) + 24 * l)
                for g in (G_UV, G_AZ):
                    for n, r in enumerate(ts):
                        u = ub[g] + n
                        if u >= 5:
                            pe.wait_ge(s["p_free"], u - 4)
                        t = rows_unit(u % 5, r, GROUPS[g][1], KT * (NG * l + g) if n == 0 else None, n == nq - 1)
                        t.then_inc(s["p_full"], 1)
                pe.wait_ge(s["p_free"], ub[G_CBC])
                for g in (G_CBC, G_CXZ, G_BZ):
                    for ct in range(4):
                        u = ub[g] + ct
                        if u >= ub[G_CBC] + 2:
                            pe.wait_ge(s["p_free"], u - 1)
                        t = cols_unit(3 * (ct % 2), ct, l, KT * (NG * l + g) if ct == 0 else None, ct == 3)
                        t.then_inc(s["p_full"], 1)
                        if (g, ct) == (G_CBC, 0):
                            pe.wait_ge(s["sg_in"], 32 + 32 * l)
                            for hh in range(4):
                                t = nc.tensor.transpose(PS[:, 6, P * hh:P * (hh + 1)], ws_in[:, hh, :], ident[:, :])
                            t.then_inc(s["sgw_turned"], 1)
                        if (g, ct) == (G_CBC, 1):
                            pe.wait_ge(s["sgw_ready"], 1 + 1 * l)
                            pe.wait_ge(s["sg_v"], nq)
                            half = nq // 2
                            for hh in range(4):
                                for i in range(2):
                                    n = 2 * hh + i
                                    if n >= 2:
                                        pe.wait_ge(s["sg_free"], n - 1 + 8 * l)
                                    a = ts[0] + half * i
                                    mm(PS[:, 6 + i, 0:half * HD].rearrange("p (r n) -> p r n", n=HD), wsT[:, hh, :],
                                       uv[:, a:a + half, 256 + HD * hh:256 + HD * (hh + 1)],
                                       start=True, stop=True).then_inc(s["sg_full"], 1)
                        if (g, ct) == (G_CXZ, 1):
                            pe.wait_ge(s["ya_ready"], 1 + 1 * l)
                            n = 0
                            for a in range(2):
                                for r0, r1 in q_turns(l):
                                    if n >= 2:
                                        pe.wait_ge(s["ya_cols"], n - 1)
                                    for r in range(r0, r1):
                                        t = nc.tensor.transpose(PS[:, 6 + n % 2, P * (r - r0):P * (r - r0 + 1)],
                                                                uv[:, r, P * a:P * (a + 1)], ident[:, :])
                                    t.then_inc(s["ya_turned"], 1)
                                    n += 1
                pe.wait_ge(s["p_free"], ub[G_Q])
                if l == DEPTH - 1:
                    for n, r in enumerate(ts):
                        if n >= 5:
                            pe.wait_ge(s["p_free"], ub[G_Q] + n - 4)
                        t = rows_unit(n % 5, r, GW, KT * (NG * l + G_Q) if n == 0 else None, n == nq - 1)
                        t.then_inc(s["p_full"], 1)
                    pe.wait_ge(s["p_free"], ub[G_K])
                g0 = G_Q if l < DEPTH - 1 else G_K
                with pe.Fori(0, G_O0 - g0) as i:
                    for r in range(TILES):
                        pe.wait_ge(s["p_free"], i * TILES + (ub[g0] + r - 4))
                        t = rows_unit(r % 5, r, GW, None if r else i * KT + KT * (NG * l + g0), r == TILES - 1)
                        t.then_inc(s["p_full"], 1)

                pe.wait_ge(s["p_free"], ub[-1])
                plan, nprep = slot_plan(l), len(prep_turns(l))
                nslot = len(plan)
                used = [0]

                def slot(h):
                    _, bank, back = plan[used[0]]
                    pe.wait_ge(s["slot_free"], h * nslot + (nprep + used[0] - back + 1))
                    used[0] += 1
                    return bank

                def prep(h):
                    for n, (i, m, r0, r1) in enumerate(prep_turns(l)):
                        if m == 0 and r0 == (q_turns(l) if i == 0 else K_TURNS)[0][0]:
                            at = i + 1 + 10 * l if h is None else h * 2 + (i + 3 + 10 * l)
                            pe.wait_ge(s["rope_ready"], at)
                            pe.wait_ge(s["ctx_qk"], at)
                        if h is not None:
                            b = slot(h)
                        else:
                            b = PREP_BANKS[n % 5]
                            if n >= 5:
                                pe.wait_ge(s["slot_free"], n - 4)
                        for r in range(r0, r1):
                            t = nc.tensor.transpose(PS[:, b, P * (r - r0):P * (r - r0 + 1)],
                                                    rope[:, i, r, P * m:P * (m + 1)], ident[:, :])
                        t.then_inc(s["slot_full"], 1)

                prep(None)
                with pe.Fori(0, HEADS) as h:
                    used[0] = 0

                    def scores(n, m):
                        if n:
                            pe.wait_ge(s[f"exp{m}"], h * nq + n)
                        tile = ts[n]
                        for r0, w in (((0, 256),) if tile < CTX_TILES else ((0, 512), (512, 512), (1024, 256))):
                            o = 1536 * m + r0
                            for part in range(2):
                                t = mm(PF[:, o:o + w], qst[:, m, P * tile:P * (tile + 1)],
                                       kst[:, part, m, r0:r0 + w], start=(part == 0), stop=(part == 1))
                        t.then_inc(s[f"s_full{m}"], 1)

                    def turn(n, k0, k1):
                        b = slot(h)
                        for kk in range(k0, k1):
                            t = nc.tensor.transpose(PS[:, b, P * (kk - k0):P * (kk - k0 + 1)],
                                                    prob[:, n % 2, 0, P * kk:P * (kk + 1)], ident[:, :])
                        t.then_inc(s["slot_full"], 1)

                    def values(chunk):
                        a, e = chunk
                        w = P * (e - a)
                        nk = CTX_TILES if a < CTX_TILES else TILES
                        pe.wait_ge(s["slot_free"], h * nslot + (nprep + used[0]))
                        pe.wait_ge(s["v_lo"], h + (1 + 4 * l))
                        b = slot(h)
                        for kk in range(nk):
                            t = three(PS[:, b, 0:w], lambda i: vhl[:, i, kk, :], lambda i: aT[:, i, kk, 0:w],
                                      kk == 0, kk == nk - 1)
                        t.then_inc(s["slot_full"], 1)

                    pe.wait_ge(s["slot_free"], h * nslot + nprep)
                    scores(0, 0)
                    pe.wait_ge(s["ln_done"], h + 1)
                    scores(0, 1)
                    scores(1, 0)
                    for t in range(1, nq + 1):
                        if t < nq:
                            scores(t, 1)
                        if chunk_due(l, t - 2):
                            values(chunk_due(l, t - 2))
                        runs = key_turns(ts[t - 1])
                        pe.wait_ge(s["comb_low"], h * nq + t)
                        for run in runs[:2]:
                            turn(t - 1, *run)
                        if t + 1 < nq:
                            scores(t + 1, 0)
                        for run in runs[2:]:
                            pe.wait_ge(s["comb"], h * LAT_TILES + (ts[t - 1] - CTX_TILES + 1))
                            turn(t - 1, *run)
                    values(chunk_due(l, nq - 1))
                    prep(h)
                    pe.wait_ge(s["sq_done"], h * (3 - l) + (3 - l))
                    for r0, w in ((lo_row, 512 - lo_row), (512, 512), (1024, 256)):
                        t = mm(PF[:, 1536 + r0:1536 + r0 + w], ones[:, :], SM[:, r0:r0 + w], start=True, stop=True)
                    t.then_inc(s["ms_full"], 1)
                pe.wait_ge(s["slot_free"], HEADS * nslot + nprep)
                pe.wait_ge(s["ln_done"], 1 + HEADS)
                pe.wait_ge(s["y_lo"], KT + 8 * l)
                for g in range(2):
                    for n, r in enumerate(ts):
                        u = nq * g + n
                        if u >= 5:
                            pe.wait_ge(s["o_z"], u - 4)
                        t = rows_unit(u % 5, r, GW, KT * (NG * l + G_O0 + g) if n == 0 else None, n == nq - 1)
                        t.then_inc(s["o_full"], 1)

        @block.scalar
        def _(act):
            A = nc.scalar.activation
            act.wait_ge(setup_turned, 1)
            A(condT[:, :, :], PS[:, 0, 128:144].rearrange("p (j k) -> p j k", j=2), ACT.Silu).then_inc(cond_ready, 1)
            act.wait_ge(lam_dve, 2 * DEPTH)
            for l in range(DEPTH):
                A(lamE[:, l, 2:4], lamE[:, l, 0:2], ACT.Exp).then_inc(lam_exp, 1)
            for l in range(DEPTH):
                act.wait_ge(wm_used, KT * (l + 1))
                if l:
                    act.wait_ge(gate_rows, 4 * l)
                    act.wait_ge(mod_turned, l)
                for b in range(6):
                    A(RAW[0:2, 512 * b:512 * (b + 1)], PS[0:2, 1 + b, :], ACT.Copy).then_inc(mod_rows, 1)

            def split_hi(l, g):
                n = NG * l + g
                w = GROUPS[g][1]
                act.wait_ge(w_raw, 16 * (n + 1))
                for k in range(KT):
                    if n and k < KT - 1:
                        act.wait_ge(w_used, (KT - 1) * (n - 1) + k + 1)
                    elif n:
                        act.wait_ge(*group_end(*divmod(n - 1, NG)))
                    A(W[:, 0, k, 0:w], wraw[:, k, 0:w], ACT.Copy).then_inc(w_hi, 1)

            split_hi(0, G_UV)
            for l in range(DEPTH):
                s = S[l]
                ts = q_tiles(l)
                nq, ub = len(ts), unit_base(l)
                lo = ts[0] * P
                for ci, (a, b) in enumerate(NORM_CHUNKS):
                    if l == 0:
                        act.wait_ge(s["x_in"][ci], 16)
                    for r in range(a, b):
                        if l:
                            act.wait_ge(S[l - 1]["o_x"], len(q_tiles(l - 1)) + r + 1)
                        if r:
                            act.wait_ge(s["n_sq"], r + 10 * l)
                        A(QX[:, XT:XT + D], X[:, r, :], ACT.Square, accum_out=stat[:, 0, r:r + 1]).then_inc(s["n_sq"], 1)
                    act.wait_ge(s["n_ms"], ci + 1 + 3 * l)
                    A(stat[:, 1, a:b], stat[:, 1, a:b], ACT.Sqrt).then_inc(s["n_root"], 1)
                for ci, (a, b) in enumerate(NORM_CHUNKS):
                    j = 1 if ci == 0 else 0
                    for k in range(KT):
                        act.wait_ge(s["n_turned"], KT * ci + k + 1 + 24 * l)
                        A(Hs[:, 0, k, P * a:P * b], PS[:, k, 0:P * (b - a)], ACT.Identity,
                          scale=shA[:, l, 1, j, k:k + 1], bias=shA[:, l, 0, j, k:k + 1]).then_inc(s["n_hi"], 1)
                for n, r in enumerate(ts):
                    if n == nq - 1:
                        split_hi(l, G_AZ)
                    act.wait_ge(s["p_full"], n + 1)
                    A(uv[:, r, :], PS[:, n % 5, :], ACT.Gelu_apprx_tanh).then_inc(s["p_free"], 1)
                    act.wait_ge(s["p_free"], n + 1)
                    if n:
                        act.wait_ge(s["sg_sq"], n)
                    A(QX[:, 7680:7936], uv[:, r, 256:512], ACT.Square, accum_out=stat[:, 2, r:r + 1]).then_inc(s["sg_sq"], 1)
                act.wait_ge(s["sg_ms"], 1 + 1 * l)
                A(stat[:, 0, ts[0]:], stat[:, 0, ts[0]:], ACT.Sqrt).then_inc(s["sg_root"], 1)
                for n, r in enumerate(ts):
                    if n == nq - 1:
                        split_hi(l, G_CBC)
                    u = ub[G_AZ] + n
                    act.wait_ge(s["p_full"], u + 1)
                    A(az[:, r, :], PS[:, u % 5, 0:256], ACT.Silu).then_inc(s["p_free"], 1)
                for g in (G_CBC, G_CXZ, G_BZ):
                    for ct in range(4):
                        if ct == 3:
                            split_hi(l, g + 1)
                        u = ub[g] + ct
                        act.wait_ge(s["p_full"], u + 1)
                        src = PF[:, 1536 * (ct % 2) + 256 + lo:1536 * (ct % 2) + 256 + ROWS]
                        if g == G_CBC:
                            A(cbc[:, ct, lo:], src, ACT.Copy).then_inc(s["p_free"], 1)
                        elif g == G_CXZ:
                            if ct < 2:
                                act.wait_ge(s["sg_full"], 8 + 8 * l)
                                A(cxz[:, ct, lo:], src, ACT.Copy).then_inc(s["p_free"], 1)
                            else:
                                act.wait_ge(s["cc_cx"], ct - 1 + 2 * l)
                                A(cxz[:, ct - 2, lo:], src, ACT.Silu).then_inc(s["p_free"], 1)
                        else:
                            if ct == 0:
                                act.wait_ge(s["y_out"], 32)
                            A(bzs[:, ct, lo:], src, ACT.Silu).then_inc(s["p_free"], 1)
                            act.wait_ge(s["p_free"], u + 1)
                            A(stat[0:1, 1, 0:1], stat[0:1, 1, 0:1], ACT.Copy).then_inc(s["bz_ready"], 1)
                        if (g, ct) == (G_CBC, 0):
                            act.wait_ge(s["sgw_turned"], 1 + 1 * l)
                            A(wsT[:, :, :], PS[:, 6, :].rearrange("p (h n) -> p h n", h=4), ACT.Copy).then_inc(s["sgw_ready"], 1)
                        if (g, ct) == (G_CXZ, 1):
                            n = 0
                            for a in range(2):
                                for r0, r1 in q_turns(l):
                                    act.wait_ge(s["ya_turned"], n + 1)
                                    A(uv[:, r0:r1, 256 + P * a:256 + P * (a + 1)],
                                      PS[:, 6 + n % 2, 0:P * (r1 - r0)].rearrange("p (r n) -> p r n", n=P),
                                      ACT.Copy).then_inc(s["ya_cols"], 1)
                                    n += 1
                act.wait_ge(s["bz_out"], 64 + 64 * l)
                act.wait_ge(s["yc_out"], 32 + 32 * l)
                if l == DEPTH - 1:
                    for n, r in enumerate(ts):
                        if n == nq - 1:
                            split_hi(l, G_K)
                        act.wait_ge(s["p_full"], ub[G_Q] + n + 1)
                        A(qkv[:, r, 0:GW], PS[:, n % 5, :], ACT.Copy).then_inc(s["p_free"], 1)
                g0 = G_Q if l < DEPTH - 1 else G_K
                with act.Fori(0, G_O0 - g0) as i:
                    for r in range(TILES):
                        if r == TILES - 1:
                            n = NG * l + g0
                            act.wait_ge(w_raw, i * 16 + 16 * (n + 2))
                            for k in range(KT):
                                if k < KT - 1:
                                    act.wait_ge(w_used, i * (KT - 1) + ((KT - 1) * n + k + 1))
                                else:
                                    act.wait_ge(s["p_full"], i * TILES + ub[g0 + 1])
                                A(W[:, 0, k, :], wraw[:, k, :], ACT.Copy).then_inc(w_hi, 1)
                        act.wait_ge(s["p_full"], i * TILES + (ub[g0] + r + 1))
                        A(qkv[:, r, bass.ds(i * GW + GW * (g0 - G_Q), GW)], PS[:, r % 5, :], ACT.Copy).then_inc(s["p_free"], 1)

                nprep, nslot = len(prep_turns(l)), len(slot_plan(l))
                act.wait_ge(s["p_free"], ub[-1])
                act.wait_ge(w_lo, KT * (NG * l + G_O0 + 1))

                def ctx_rows(h, off):
                    for i in range(2):
                        src = qkv[:, 0:CTX_TILES, head_cols(h, off + GW * (i if l == 0 else 1))]
                        for m in range(2):
                            t = A(rope[:, i, 0:CTX_TILES, P * m:P * (m + 1)].rearrange("p r (d n) -> p r d n", d=2),
                                  src[:, :, HD * m:HD * (m + 1)].unsqueeze(2).to_broadcast([P, CTX_TILES, 2, HD]), ACT.Copy)
                        t.then_inc(s["ctx_qk"], 1)

                def prep(full, at):
                    for n, (i, m, r0, r1) in enumerate(prep_turns(l)):
                        act.wait_ge(s["slot_full"], full + (at + n + 1))
                        src = PS[:, PREP_BANKS[n % 5], 0:P * (r1 - r0)]
                        if i == 0:
                            A(qst[:, m, P * r0:P * r1], src, ACT.Copy, scale=SC).then_inc(s["slot_hi"], 1)
                        else:
                            A(kst[:, 0, m, P * r0:P * r1], src, ACT.Copy).then_inc(s["slot_hi"], 1)

                ctx_rows(None, 0)
                prep(0, 0)
                A(lamE[:, l, 2:3], lamE[:, l, 0:1], ACT.Exp).then_inc(s["ln_done"], 1)
                with act.Fori(0, HEADS) as h:
                    n = nprep

                    def exps(q, m):
                        w = 256 if ts[q] < CTX_TILES else ROWS
                        act.wait_ge(s[f"max{m}"], h * nq + (q + 1))
                        A(prob[:, q % 2, m, 0:w], PF[:, 1536 * m:1536 * m + w], ACT.Exp,
                          bias=nmax[:, m, q % 2:q % 2 + 1], accum_out=Z[:, m, q % 2:q % 2 + 1]).then_inc(s[f"exp{m}"], 1)

                    def turned_hi(q, k0, k1, n):
                        c0 = (ts[q] - chunk_of(ts[q])[0]) * P
                        act.wait_ge(s["slot_full"], h * nslot + (n + 1))
                        A(aT[:, 0, k0:k1, c0:c0 + P], PS[:, 6 + (n - nprep) % 2, 0:P * (k1 - k0)].rearrange("p (k q) -> p k q", q=P),
                          ACT.Copy).then_inc(s["slot_hi"], 1)

                    def squares(chunk, n):
                        w = P * (chunk[1] - chunk[0])
                        act.wait_ge(s["slot_full"], h * nslot + (n + 1))
                        A(SM[:, P * chunk[0]:P * chunk[1]], PS[:, 6 + (n - nprep) % 2, 0:w], ACT.Square).then_inc(s["slot_hi"], 1)

                    exps(0, 0)
                    exps(0, 1)
                    A(vhl[:, 0, :, :], qkv[:, :, bass.ds(h * P + 2 * GW, P)], ACT.Copy).then_inc(s["v_hi"], 1)
                    for t in range(1, nq + 1):
                        for run in key_turns(ts[t - 2])[2:] if t >= 2 else []:
                            turned_hi(t - 2, *run, n)
                            n += 1
                        if t < nq:
                            exps(t, 0)
                        if chunk_due(l, t - 2):
                            squares(chunk_due(l, t - 2), n)
                            n += 1
                        for run in key_turns(ts[t - 1])[:2]:
                            turned_hi(t - 1, *run, n)
                            n += 1
                        if t < nq:
                            exps(t, 1)
                    for run in key_turns(ts[nq - 1])[2:]:
                        turned_hi(nq - 1, *run, n)
                        n += 1
                    ctx_rows(h, P)
                    squares(chunk_due(l, nq - 1), n)
                    n += 1
                    prep(h * nslot, n)
                    r = SM[:, lo:ROWS]
                    act.wait_ge(s["ms_full"], h + 1)
                    A(r, PF[:, 1536 + lo:1536 + ROWS], ACT.Ln).then_inc(s["ln_done"], 1)
                    act.wait_ge(s["ln_done"], h + 2)
                    A(r, r, ACT.Exp, scale=-0.5).then_inc(s["rstd_done"], 1)
                act.wait_ge(s["slot_free"], HEADS * nslot + nprep)
                for i in range(KT):
                    act.wait_ge(s["y_in"][i % 4], 16 * (i // 4 + 1) + 32 * l)
                    o = XT + ROWS * (i % 4)
                    A(Hs[:, 0, i, lo:], QX[:, o + lo:o + ROWS], ACT.Copy).then_inc(s["y_hi"], 1)
                split_hi(l, G_O1)
                if l < DEPTH - 1:
                    split_hi(l + 1, G_UV)
                else:
                    for n, r in enumerate(ts):
                        act.wait_ge(s["o_x"], nq + n + 1)
                        if n:
                            act.wait_ge(s["f_sq"], n)
                        A(QX[:, XT + 2048:XT + 3072], X[:, r, :], ACT.Square, accum_out=stat[:, 0, r:r + 1]).then_inc(s["f_sq"], 1)
                        act.wait_ge(s["f_ms"], n + 1)
                        A(stat[:, 1, r:r + 1], stat[:, 1, r:r + 1], ACT.Sqrt).then_inc(s["f_root"], 1)

        @block.vector
        def _(dve):
            V = nc.vector
            dve.wait_ge(vec_in, 16 * 22)
            for l in range(DEPTH):
                lv = SM[:, 256 * l:256 * (l + 1)].rearrange("p (a b n) -> p a b n", a=2, b=2)
                o = SM[:, 512 + P * l:512 + P * (l + 1)].rearrange("p (a n) -> p a n", a=2)
                V.tensor_tensor(o, lv[:, :, 0, :], lv[:, :, 1, :], ALU.mult).then_inc(lam_dve, 1)
                dve.wait_ge(lam_dve, 2 * l + 1)
                V.reduce_sum(lamE[:, l, 0:2], o, AX.X).then_inc(lam_dve, 1)
            for l in range(DEPTH):
                dve.wait_ge(lam_exp, l + 1)
                V.scalar_tensor_tensor(out=nlam[:, l:l + 1], in0=lamE[:, l, 3:4], scalar=lam_init(l), in1=lamE[:, l, 2:3],
                                       op0=ALU.subtract, op1=ALU.subtract).then_inc(lam_dve, 1)
            dve.wait_ge(setup_turned, 1)
            dve.wait_ge(cond_ready, 1)
            V.tensor_copy(vc[:, :, :], PS[:, 0, 0:128].rearrange("p (l v) -> p l v", l=2)[:, :, 0:V_ROWS]).then_inc(setup_cols, 1)
            dve.wait_ge(setup_cols, 1)
            for l in range(DEPTH):
                V.tensor_scalar(gsub[:, l:l + 1], vc[:, l, V_SUB:V_SUB + 1], 1.0 - lam_init(l), None, ALU.mult).then_inc(setup_cols, 1)
            for l in range(DEPTH):
                dve.wait_ge(mod_turned, l + 1)
                for part in range(2):
                    V.tensor_tensor(shA[:, l, part, :, :], PS[:, 7, 16 * part:16 * part + 16].rearrange("p (k j) -> p j k", j=2),
                                    vc[:, l, 8 * part:8 * part + 8].unsqueeze(1).to_broadcast([P, 2, KT]), ALU.add).then_inc(mod_cols, 1)
                dve.wait_ge(mod_cols, 3 * l + 2)
                V.scalar_tensor_tensor(out=shA[:, l, 1, :, :], in0=shA[:, l, 1, :, :], scalar=1.0,
                                       in1=vc[:, l, V_G:V_G + 8].unsqueeze(1).to_broadcast([P, 2, KT]),
                                       op0=ALU.add, op1=ALU.mult).then_inc(mod_cols, 1)
                dve.wait_ge(bgate_in, 16 * (l + 1))
                for j in range(2):
                    for b in range(2):
                        n = 4 * l + 2 * j + b
                        dve.wait_ge(gate_sums, n + 1)
                        if b == 0 and n:
                            dve.wait_ge(gate_out, 16 * (n // 2))
                        V.tensor_tensor(RAW[:, 4 * D + 512 * b:4 * D + 512 * (b + 1)], PS[:, 1 + b, :],
                                        RAW[:, 3 * D + 512 * b:3 * D + 512 * (b + 1)], ALU.add).then_inc(gate_rows, 1)

            def split_lo(l, g):
                n = NG * l + g
                w = GROUPS[g][1]
                for k in range(KT):
                    dve.wait_ge(w_hi, KT * n + k + 1)
                    V.tensor_tensor(W[:, 1, k, 0:w], wraw[:, k, 0:w], W[:, 0, k, 0:w].bitcast(F32), ALU.subtract).then_inc(w_lo, 1)

            split_lo(0, G_UV)
            for l in range(DEPTH):
                s = S[l]
                ts = q_tiles(l)
                nq, ub = len(ts), unit_base(l)
                lo = ts[0] * P
                for ci, (a, b) in enumerate(NORM_CHUNKS):
                    dve.wait_ge(s["n_sq"], b + 10 * l)
                    V.tensor_scalar(stat[:, 1, a:b], stat[:, 0, a:b], 1.0 / D, EPS, ALU.mult, ALU.add).then_inc(s["n_ms"], 1)
                    dve.wait_ge(s["n_root"], ci + 1 + 3 * l)
                    V.reciprocal(stat[:, 1, a:b], stat[:, 1, a:b]).then_inc(s["n_rstd"], 1)
                    dve.wait_ge(s["n_rstd"], ci + 1 + 3 * l)
                    for r in range(a, b):
                        if l:
                            dve.wait_ge(S[l - 1]["x_out"], 16 * TILES)
                        V.tensor_scalar(X[:, r, :], X[:, r, :], stat[:, 1, r:r + 1], None, ALU.mult).then_inc(s["n_xn"], 1)
                for ci, (a, b) in enumerate(NORM_CHUNKS):
                    j = 1 if ci == 0 else 0
                    for k in range(KT):
                        n = KT * ci + k
                        w = P * (b - a)
                        ht = QX[:, XT + 1024 + 512 * (k % 4):XT + 1024 + 512 * (k % 4) + w]
                        dve.wait_ge(s["n_hi"], n + 1 + 24 * l)
                        if n >= 4:
                            dve.wait_ge(s["n_lo"], n - 3 + 24 * l)
                        V.tensor_scalar(ht, PS[:, k, 0:w], shA[:, l, 1, j, k:k + 1], shA[:, l, 0, j, k:k + 1],
                                        ALU.mult, ALU.add).then_inc(s["n_h"], 1)
                        dve.wait_ge(s["n_h"], n + 1 + 24 * l)
                        V.tensor_tensor(Hs[:, 1, k, P * a:P * b], ht, Hs[:, 0, k, P * a:P * b].bitcast(F32), ALU.subtract).then_inc(s["n_lo"], 1)
                split_lo(l, G_AZ)
                dve.wait_ge(s["sg_sq"], nq)
                V.tensor_scalar(stat[:, 0, ts[0]:], stat[:, 2, ts[0]:], 1.0 / 256, EPS, ALU.mult, ALU.add).then_inc(s["sg_ms"], 1)
                dve.wait_ge(s["sg_root"], 1 + 1 * l)
                V.reciprocal(stat[:, 0, ts[0]:], stat[:, 0, ts[0]:]).then_inc(s["sg_rstd"], 1)
                dve.wait_ge(s["sg_rstd"], 1 + 1 * l)
                dve.wait_ge(s["sg_in"], 32 + 32 * l)
                for r in ts:
                    V.scalar_tensor_tensor(out=uv[:, r, 256:512], in0=uv[:, r, 256:512], scalar=stat[:, 0, r:r + 1],
                                           in1=sguG[:, :], op0=ALU.mult, op1=ALU.mult).then_inc(s["sg_v"], 1)
                split_lo(l, G_CBC)
                half = nq // 2
                for hh in range(4):
                    for i in range(2):
                        a = ts[0] + half * i
                        u = uv[:, a:a + half, HD * hh:HD * (hh + 1)]
                        dve.wait_ge(s["sg_full"], 2 * hh + i + 1 + 8 * l)
                        V.scalar_tensor_tensor(out=u, in0=PS[:, 6 + i, 0:half * HD].rearrange("p (r n) -> p r n", n=HD),
                                               scalar=vc[:, l, V_SB + hh:V_SB + hh + 1], in1=u, op0=ALU.add, op1=ALU.mult).then_inc(s["sg_free"], 1)
                dve.wait_ge(s["sg_free"], 8 + 8 * l)
                dve.wait_ge(s["p_free"], ub[G_CBC])
                V.tensor_tensor(uv[:, ts[0]:, 0:256], uv[:, ts[0]:, 0:256], az[:, ts[0]:, :], ALU.mult).then_inc(s["ya_ready"], 1)
                split_lo(l, G_CXZ)
                for i in range(2):
                    dve.wait_ge(s["p_free"], ub[G_CXZ] + i + 1)
                    V.tensor_tensor(cbc[:, 2 + i, lo:], cbc[:, 2 + i, lo:], cxz[:, i, lo:], ALU.mult).then_inc(s["cc_cx"], 1)
                split_lo(l, G_BZ)
                nconv = 0
                for i in range(2):
                    t, acc = cbc[:, 2 + i, :], SM[:, 0:ROWS]
                    tap = [vc[:, l, V_CW + 2 * j + i:V_CW + 2 * j + i + 1] for j in range(3)]
                    dve.wait_ge(s["cc_cx"], i + 1 + 2 * l)
                    if i:
                        dve.wait_ge(s["yc_out"], 16 * i + 32 * l)
                    V.tensor_scalar(acc[:, lo:], t[:, lo:], tap[1], vc[:, l, V_CB + i:V_CB + i + 1], ALU.mult, ALU.add).then_inc(s["conv"], 1)
                    nconv += 1
                    for a, b in ([(0, 256), (256, ROWS)] if l == 0 else [(256, ROWS)]):
                        for j, (oa, ob, ia, ib) in enumerate(((a + 1, b, a, b - 1), (a, b - 1, a + 1, b))):
                            dve.wait_ge(s["conv"], nconv)
                            V.scalar_tensor_tensor(out=acc[:, oa:ob], in0=t[:, ia:ib], scalar=tap[2 * j], in1=acc[:, oa:ob],
                                                   op0=ALU.mult, op1=ALU.add).then_inc(s["conv"], 1)
                            nconv += 1
                    dve.wait_ge(s["conv"], nconv)
                    V.tensor_tensor(acc[:, lo:], acc[:, lo:], cbc[:, i, lo:], ALU.mult).then_inc(s["conv"], 1)
                    nconv += 1
                    dve.wait_ge(s["conv"], nconv)
                    dve.wait_ge(s["p_free"], ub[G_CXZ] + 3 + i)
                    V.tensor_tensor(acc[:, lo:], acc[:, lo:], cxz[:, i, lo:], ALU.mult).then_inc(s["yc_ready"], 1)
                split_lo(l, G_Q)
                if l == DEPTH - 1:
                    split_lo(l, G_K)
                g0 = G_Q if l < DEPTH - 1 else G_K
                with dve.Fori(0, G_O0 - g0) as i:
                    for k in range(KT):
                        dve.wait_ge(w_hi, i * KT + (KT * (NG * l + g0 + 1) + k + 1))
                        V.tensor_tensor(W[:, 1, k, :], wraw[:, k, :], W[:, 0, k, :].bitcast(F32), ALU.subtract).then_inc(w_lo, 1)

                nprep, nslot = len(prep_turns(l)), len(slot_plan(l))
                dve.wait_ge(s["p_free"], ub[-1])
                dve.wait_ge(w_lo, KT * (NG * l + G_O0 + 1))

                def rope_muls(h, off):
                    for i in range(2):
                        dve.wait_ge(s["rope_swap"], 4 * (i + 1) + 40 * l if h is None else h * 8 + (8 + 4 * (i + 1) + 40 * l))
                        x = qkv[:, CTX_TILES:TILES, head_cols(h, off + GW * i)].rearrange("p r (m n) -> p r m n", m=2)
                        V.tensor_tensor(x, x, cosT[:, :, :].unsqueeze(2).to_broadcast([P, LAT_TILES, 2, HD]), ALU.mult).then_inc(s["rope_mul"], 1)

                def rope_adds(h, off):
                    for i in range(2):
                        dve.wait_ge(s["rope_mul"], i + 1 + 10 * l if h is None else h * 2 + (i + 3 + 10 * l))
                        x = qkv[:, CTX_TILES:TILES, head_cols(h, off + GW * i)]
                        for m in range(2):
                            dst = rope[:, i, CTX_TILES:TILES, P * m:P * (m + 1)].rearrange("p r (d n) -> p r d n", d=2)
                            c, w = [a[:, :, HD * m:HD * (m + 1)].unsqueeze(2).to_broadcast([P, LAT_TILES, 2, HD])
                                    for a in (x, swapped(h, i))]
                            t = V.tensor_tensor(dst, c, w, ALU.add)
                        t.then_inc(s["rope_ready"], 1)

                def prep_lo(full, at):
                    for n, (i, m, r0, r1) in enumerate(prep_turns(l)):
                        dve.wait_ge(s["slot_hi"], full + (at + n + 1))
                        src = PS[HD * (1 - i):P, PREP_BANKS[n % 5], 0:P * (r1 - r0)]
                        if i == 0:
                            q = qst[HD:P, m, P * r0:P * r1]
                            V.scalar_tensor_tensor(out=q, in0=src, scalar=SC, in1=q.bitcast(F32),
                                                   op0=ALU.mult, op1=ALU.subtract).then_inc(s["slot_free"], 1)
                        else:
                            V.tensor_tensor(kst[:, 1, m, P * r0:P * r1], src,
                                            kst[:, 0, m, P * r0:P * r1].bitcast(F32), ALU.subtract).then_inc(s["slot_free"], 1)

                rope_muls(None, 0)
                rope_adds(None, 0)
                prep_lo(0, 0)
                with dve.Fori(0, HEADS) as h:
                    n = nprep

                    def maxima(q, m):
                        w = 256 if ts[q] < CTX_TILES else ROWS
                        dve.wait_ge(s[f"s_full{m}"], h * nq + (q + 1))
                        V.tensor_reduce(nmax[:, m, q % 2:q % 2 + 1], PF[:, 1536 * m:1536 * m + w], AX.X, ALU.max,
                                        negate=True).then_inc(s[f"max{m}"], 1)

                    def combine(q):
                        b = q % 2
                        w = 256 if ts[q] < CTX_TILES else P * LOW_KEYS
                        z0, z1 = Z[:, 0, b:b + 1], Z[:, 1, b:b + 1]
                        at = h * nq + (q + 1)
                        dve.wait_ge(s["exp0"], at)
                        V.tensor_scalar(rz[:, 1, b:b + 1], z0, nlam[:, l:l + 1], None, ALU.mult)
                        V.scalar_tensor_tensor(out=ez[:, ts[q]:ts[q] + 1], in0=z0, scalar=EPS * P, in1=z0, op0=ALU.mult, op1=ALU.mult)
                        dve.wait_ge(s["exp1"], at)
                        V.reciprocal(rz[:, 0, b:b + 1], z1).then_inc(s["rz_done"], 1)
                        dve.wait_ge(s["rz_done"], at)
                        V.tensor_tensor(rz[:, 3, b:b + 1], rz[:, 1, b:b + 1], rz[:, 0, b:b + 1], ALU.mult).then_inc(s["coef"], 1)
                        e0, e1 = prob[:, b, 0, 0:w], prob[:, b, 1, 0:w]
                        dve.wait_ge(s["coef"], at)
                        V.scalar_tensor_tensor(out=e0, in0=e1, scalar=rz[:, 3, b:b + 1], in1=e0,
                                               op0=ALU.mult, op1=ALU.add).then_inc(s["comb_low"], 1)

                    def turned_lo(q, k0, k1, n):
                        c0 = (ts[q] - chunk_of(ts[q])[0]) * P
                        dve.wait_ge(s["slot_hi"], h * nslot + (n + 1))
                        V.tensor_tensor(aT[:, 1, k0:k1, c0:c0 + P],
                                        PS[:, 6 + (n - nprep) % 2, 0:P * (k1 - k0)].rearrange("p (k q) -> p k q", q=P),
                                        aT[:, 0, k0:k1, c0:c0 + P].bitcast(F32), ALU.subtract).then_inc(s["slot_free"], 1)

                    def outputs(chunk, n):
                        a, e = chunk
                        dve.wait_ge(s["slot_hi"], h * nslot + (n + 1))
                        dve.wait_ge(s["bzh_in"], h * 16 + 16)
                        V.scalar_tensor_tensor(out=qkv[:, a:e, bass.ds(h * P, P)],
                                               in0=PS[:, 6 + (n - nprep) % 2, 0:P * (e - a)].rearrange("p (r n) -> p r n", n=P),
                                               scalar=gsub[:, l:l + 1], in1=qkv[:, a:e, bass.ds(h * P + 2 * GW, P)],
                                               op0=ALU.mult, op1=ALU.mult).then_inc(s["slot_free"], 1)
                        for r in range(a, e):
                            sq = SM[:, P * r:P * (r + 1)]
                            t = V.scalar_tensor_tensor(out=sq, in0=ident[:, :], scalar=ez[:, r:r + 1], in1=sq,
                                                       op0=ALU.mult, op1=ALU.add)
                        t.then_inc(s["sq_done"], 1)

                    maxima(0, 0)
                    maxima(0, 1)
                    for t in range(1, nq + 1):
                        if t < nq:
                            maxima(t, 0)
                        for run in key_turns(ts[t - 2])[2:] if t >= 2 else []:
                            turned_lo(t - 2, *run, n)
                            n += 1
                        combine(t - 1)
                        if t < nq:
                            maxima(t, 1)
                        else:
                            rope_muls(h, P)
                        if chunk_due(l, t - 2):
                            outputs(chunk_due(l, t - 2), n)
                            n += 1
                        for run in key_turns(ts[t - 1])[:2]:
                            turned_lo(t - 1, *run, n)
                            n += 1
                    for run in key_turns(ts[nq - 1])[2:]:
                        turned_lo(nq - 1, *run, n)
                        n += 1
                    rope_adds(h, P)
                    outputs(chunk_due(l, nq - 1), n)
                    n += 1
                    prep_lo(h * nslot, n)
                for i in range(KT):
                    dve.wait_ge(s["y_hi"], i + 1 + 8 * l)
                    o = XT + ROWS * (i % 4)
                    V.tensor_tensor(Hs[:, 1, i, lo:], QX[:, o + lo:o + ROWS], Hs[:, 0, i, lo:].bitcast(F32), ALU.subtract).then_inc(s["y_lo"], 1)
                dve.wait_ge(s["gate_in"], 32 + 32 * l)
                dve.wait_ge(s["y_lo"], KT + 8 * l)
                dve.wait_ge(s["x_in"][0], 48 + 16 * l)
                for g in range(2):
                    for n, r in enumerate(ts):
                        if g == 0 and n == nq - 1:
                            split_lo(l, G_O1)
                        if g == 1 and n == nq - 1 and l < DEPTH - 1:
                            split_lo(l + 1, G_UV)
                        u = nq * g + n
                        z = QX[:, XT + 4096 + 512 * (u % 2):XT + 4608 + 512 * (u % 2)]
                        j = 1 if r < CTX_TILES else 0
                        dve.wait_ge(s["o_full"], u + 1)
                        if u >= 2:
                            dve.wait_ge(s["o_x"], u - 1)
                        V.tensor_tensor(z, PS[:, u % 5, :], SM[:, D * j + GW * g:D * j + GW * (g + 1)], ALU.mult).then_inc(s["o_z"], 1)
                        dve.wait_ge(s["o_z"], u + 1)
                        xs = X[:, r, GW * g:GW * (g + 1)]
                        V.tensor_tensor(xs, xs, z, ALU.add).then_inc(s["o_x"], 1)
                        if g == 1 and l == DEPTH - 1:
                            dve.wait_ge(s["f_sq"], n + 1)
                            V.tensor_scalar(stat[:, 1, r:r + 1], stat[:, 0, r:r + 1], 1.0 / D, EPS, ALU.mult, ALU.add).then_inc(s["f_ms"], 1)
                            dve.wait_ge(s["f_root"], n + 1)
                            V.reciprocal(stat[:, 1, r:r + 1], stat[:, 1, r:r + 1]).then_inc(s["f_rstd"], 1)
                            dve.wait_ge(s["f_rstd"], n + 1)
                            dve.wait_ge(s["fg_in"], 16)
                            V.scalar_tensor_tensor(out=X[:, r, :], in0=X[:, r, :], scalar=stat[:, 1, r:r + 1],
                                                   in1=QX[:, XT + 1024:XT + 2048], op0=ALU.mult, op1=ALU.mult).then_inc(s["f_y"], 1)


def rope_tables():
    row = np.repeat(np.arange(LAT_TILES * P // GRID_W), GRID_W).astype(np.float32)
    col = np.tile(np.arange(GRID_W), LAT_TILES * P // GRID_W).astype(np.float32)
    n = HD // 4
    inv = (np.float32(10000.0) ** (-np.arange(n, dtype=np.float32) / np.float32(n))).astype(np.float32)
    cos, sin = [], []
    for pos in (row, col):
        ang = pos[:, None] * inv
        cos += [np.cos(ang), np.cos(ang)]
        sin += [-np.sin(ang), np.sin(ang)]
    lay = lambda a: np.ascontiguousarray(np.concatenate(a, 1).astype(np.float32).reshape(LAT_TILES, P, HD).transpose(1, 0, 2))
    return lay(cos), lay(sin)


_INS = ["x", "c", "ctx", "c_ctx", "w_mod", "b_mod", "norm_g", "w_in", "w_out", "sgu_norm_g", "sgu_w", "sgu_b",
        "lambda_q1", "lambda_k1", "lambda_q2", "lambda_k2", "subln_g", "conv_w", "conv_b", "final_g"]


def kernel(**inputs):
    import concourse.bacc as _bacc
    from concourse.bass_utils import run_bass_kernel_spmd as _run

    nc = _bacc.Bacc("TRN2", target_bir_lowering=False, num_devices=1)
    arrays, args = {}, []
    cos, sin = rope_tables()
    for name, a in [(n, np.ascontiguousarray(inputs[n])) for n in _INS] + [("cos_t", cos), ("sin_t", sin)]:
        arrays[f"in_{name}"] = a
        args.append(nc.dram_tensor(f"in_{name}", a.shape, mybir.dt.from_np(a.dtype), kind="ExternalInput").ap())
    args.append(nc.dram_tensor("out_0", (1, LAT_TILES * P, D), F32, kind="ExternalOutput").ap())
    for name, shape in (("x1_d", (TILES, P, D)), ("yT_d", (KT, P, ROWS)), ("bz_d", (HEADS, P, ROWS)),
                        ("gate_d", (DEPTH, 2, P, D))):
        args.append(nc.dram_tensor(name, shape, F32, kind="Internal").ap())
    build(nc, *args)
    r = _run(nc, [arrays], core_ids=[0])
    return r.results[0]["out_0"]
```

```python
import math
from contextlib import ExitStack

import numpy as np

import concourse.bass as bass
from concourse import mybir

F32 = mybir.dt.float32
F32R = mybir.dt.float32r
ACT = mybir.ActivationFunctionType
ALU = mybir.AluOpType
AX = mybir.AxisListType

P = 128
D = 1024
KT = D // P
DEPTH = 2
CTX_TILES = 2
LAT_TILES = 8
TILES = CTX_TILES + LAT_TILES
ROWS = TILES * P
D_IN = 3840
GRID_W = 64
HEADS = 4
HD = 64
EPS = 1e-6
GW = 512

COL_U, COL_AZ, COL_Q, COL_K, COL_V, COL_BZ, COL_CB, COL_CX = 0, 512, 768, 1280, 1792, 2304, 2816, 3328
GROUPS = [(COL_U, 512), (COL_AZ, 256), (COL_CB, 512), (COL_CX, 512), (COL_BZ, 512),
          (COL_Q, 512), (COL_K, 512), (COL_V, 512), (0, 512), (512, 512)]
G_UV, G_AZ, G_CBC, G_CXZ, G_BZ, G_Q, G_K, G_V, G_O0, G_O1 = range(10)
NG = len(GROUPS)
NORM_BANKS = [(0, 7), (5, 6, 7)]
NORM_CHUNKS = [(0, 2), (2, 6), (6, 10)]
SC = 1.0 / math.sqrt(HD)

V_BSH, V_BSC, V_G, V_SUB, V_CW, V_CB, V_SB, V_ROWS = 0, 8, 16, 24, 25, 31, 33, 37


def q_tiles(l):
    return list(range(TILES)) if l < DEPTH - 1 else list(range(CTX_TILES, TILES))


def row_chunks(l):
    c = [(0, 256, 0, 256), (256, 512, 1, 0), (768, 512, 2, 0)]
    return c if l < DEPTH - 1 else c[1:]


def lam_init(l):
    return 0.8 - 0.6 * math.exp(-0.3 * l)


def q_turns(l):
    return [(0, 4), (4, 8), (8, 10)] if l < DEPTH - 1 else [(2, 6), (6, 10)]


Y_ORDER = (0, 1, 2, 3, 4, 6, 7, 5)
WM_COLS, WM_SLOTS = 1024, 8
WM_TILES = KT * 3 * D // WM_COLS
K_TURNS = [(0, 4), (4, 8), (8, 10)]
LOW_KEYS = 6
PREP_BANKS = (0, 1, 2, 6, 7)


def key_turns(t):
    return [(0, 2)] if t < CTX_TILES else [(0, 4), (4, LOW_KEYS), (LOW_KEYS, TILES)]


def chunk_of(t):
    return (0, 2) if t < 2 else ((2, 6) if t < 6 else (6, 10))


def norm_order(l):
    return NORM_CHUNKS if l == 0 else NORM_CHUNKS[1:] + NORM_CHUNKS[:1]


def n_xn_due(l, i):
    return sum(b - a for a, b in norm_order(l)[:i + 1])


def chunk_due(l, n):
    t = q_tiles(l)[n] if n >= 0 else None
    return chunk_of(t) if t is not None and chunk_of(t)[1] == t + 1 else None


def prep_turns(l):
    return [(i, m, r0, r1) for i, turns in enumerate((q_turns(l), K_TURNS)) for m in range(2) for r0, r1 in turns]


def slot_plan(l):
    what = []
    for t in range(1, len(q_tiles(l)) + 1):
        if chunk_due(l, t - 2):
            what.append("values")
        what += ["turn"] * len(key_turns(q_tiles(l)[t - 1]))
    what.append("values")
    banks = [6 + n % 2 for n in range(len(what))]
    banks += [PREP_BANKS[n % 5] for n in range(len(prep_turns(l)))]
    what += ["prep"] * len(prep_turns(l))
    total = len(banks)
    plan = []
    for n, b in enumerate(banks):
        back = next(d for d in range(1, total + 1) if banks[(n - d) % total] == b)
        plan.append((what[n], b, back))
    return plan


def build(nc, x, c, ctx_in, c_ctx, w_mod, b_mod, norm_g, w_in, w_out, sgu_g, sgu_w, sgu_b,
          lq1, lk1, lq2, lk2, subln_g, conv_w, conv_b, final_g, cos_t, sin_t, out,
          x1_d, yT_d, bz_d, gate_d):
    with ExitStack() as st:
        def sb(name, shape, dt=F32):
            return st.enter_context(nc.sbuf_tensor(name, shape, dt))

        def sem(name):
            return st.enter_context(nc.semaphore(name))

        H = sb("H", [P, 2 * KT * ROWS], F32R)
        QX = sb("QX", [P, TILES * 3 * GW])
        with nc.sbuf_tensor("WM", [P, WM_SLOTS, WM_COLS], F32) as WM:
            pass
        W = sb("W", [P, 2, KT, GW], F32R)
        RAW = sb("RAW", [P, 4 * ROWS])
        SM = sb("SM", [P, ROWS + LAT_TILES * P])
        ident = sb("ident", [P, P])
        ones = sb("ones", [P, P])
        cosT = sb("cosT", [P, LAT_TILES, HD])
        sinT = sb("sinT", [P, LAT_TILES, HD])
        vc = sb("vc", [P, DEPTH, V_ROWS])
        condT = sb("condT", [P, 2, KT])
        shA = sb("shA", [P, DEPTH, 2, 2, KT])
        stat = sb("stat", [P, 3, TILES])
        lamE = sb("lamE", [P, DEPTH, 4])
        nlam = sb("nlam", [P, DEPTH])
        gsub = sb("gsub", [P, DEPTH])
        nmax = sb("nmax", [P, 2, 2])
        Z = sb("Z", [P, 2, 2])
        rz = sb("rz", [P, 2, 2])
        ez = sb("ez", [P, TILES])
        PS = st.enter_context(nc.psum_tensor("PS", [P, 8, 512], F32))
        PF = PS[:, :, :].rearrange("p b n -> p (b n)")

        Hs = H[:, :].rearrange("p (s k n) -> p s k n", s=2, k=KT)
        X = QX[:, 0:TILES * D].rearrange("p (r d) -> p r d", d=D)
        XT = TILES * D
        uv = QX[:, 0:5120].rearrange("p (r n) -> p r n", n=512)
        az = QX[:, 5120:7680].rearrange("p (r n) -> p r n", n=256)
        cbc = QX[:, 7680:12800].rearrange("p (c n) -> p c n", c=4)
        cxz = QX[:, 12800:15360].rearrange("p (c n) -> p c n", c=2)
        ws_in = QX[:, 12800:13312].rearrange("p (h n) -> p h n", h=4)
        mod_row = QX[0:2, XT + 3072:XT + 5120]
        gate_row = [SM[0:2, D * (1 - l):D * (2 - l)] for l in range(DEPTH)]
        wsT = QX[:, 13312:13824].rearrange("p (h n) -> p h n", h=4)
        bzs = QX[:, 0:5120].rearrange("p (c n) -> p c n", c=4)
        qkv = QX[:, :].rearrange("p (r n) -> p r n", n=3 * GW)
        wraw = RAW[:, 0:KT * GW].rearrange("p (k n) -> p k n", k=KT)
        sguG = SM[:, 2048:2304]
        kst = H[:, 0:5120].rearrange("p (s m n) -> p s m n", s=2, m=2)
        qst = H[:, 5120:7680].rearrange("p (m n) -> p m n", m=2)
        vhl = H[:, 7680:10240].rearrange("p (s r e) -> p s r e", s=2, e=P)
        aT = H[:, 10240:20480].rearrange("p (s k q) -> p s k q", s=2, q=512)
        prob = RAW[:, :].rearrange("p (b m n) -> p b m n", b=2, m=2)
        rope = RAW[:, :].rearrange("p (b r n) -> p b r n", b=2, n=2 * P)

        def head_cols(h, off):
            return slice(off, off + P) if h is None else bass.ds(h * P + off, P)

        def swapped(h, i):
            if i == 0 and h is not None:
                return qkv[:, CTX_TILES:TILES, bass.ds(h * P + GW, P)]
            return SM[:, ROWS * i:ROWS * i + LAT_TILES * P].rearrange("p (r n) -> p r n", n=P)

        def y_rows(k, t0):
            at = P * (k - 2) if 2 <= k < 6 else GW + P * (k % 4)
            return qkv[:, t0:TILES, at:at + P]

        cond_in, cond_turned = sem("cond_in"), sem("cond_turned")
        vec_in, tab_in = sem("vec_in"), sem("tab_in")
        ident_ready, setup_turned, setup_cols = sem("ident_ready"), sem("setup_turned"), sem("setup_cols")
        cond_ready, lam_dve, lam_exp = sem("cond_ready"), sem("lam_dve"), sem("lam_exp")
        wm_in = [sem(f"wm_in{b}") for b in range(WM_SLOTS)]
        wm_used, mod_sums, mod_rows = sem("wm_used"), sem("mod_sums"), sem("mod_rows")
        mod_turned, mod_cols = sem("mod_turned"), sem("mod_cols")
        gate_rows, gate_out = sem("gate_rows"), sem("gate_out")
        bgate_in = [sem(f"bgate_in{l}") for l in range(DEPTH)]
        w_raw, w_hi, w_lo, w_used = sem("w_raw"), sem("w_hi"), sem("w_lo"), sem("w_used")
        shared = [
            "n_sq", "n_ms", "n_root", "n_rstd", "n_xn", "n_turned", "n_hi", "n_h", "sg_ms",
            "sg_root", "sg_rstd", "sg_in", "sgw_turned", "sgw_ready", "sg_full", "sg_free",
            "ya_ready", "cc_cx", "yc_ready", "yc_out", "bz_out", "rope_mul",
            "rope_swap", "rope_ready", "ctx_qk", "v_hi", "v_lo", "gate_in", "y_hi", "y_lo", "n_lo"]
        own = [
            "p_full", "p_free", "sg_sq", "sg_v", "ya_turned", "ya_cols", "conv", "slot_full",
            "slot_hi", "slot_free", "max0", "max1", "s_full0", "s_full1", "exp0", "exp1", "rz_done",
            "coef", "comb", "comb_mul", "comb_low", "sq_done", "ms_full", "ln_done", "rstd_done", "yb_ready",
            "y_out", "bzh_in", "o_full", "o_z",
            "o_x"]
        once = [
            "f_sq", "f_ms", "f_root", "f_rstd", "f_y", "f_out", "fg_in"]
        common = {n: sem(n) for n in shared + once}
        common["x_in"] = [sem(f"x_in{i}") for i in range(3)]
        common["x_out"] = [sem(f"x_out{i}") for i in range(2)]
        common["y_in"] = [sem(f"y_in{i}") for i in range(4)]
        S = [{**common, **{n: sem(f"L{l}_{n}") for n in own}} for l in range(DEPTH)]

        def unit_base(l):
            nq = len(q_tiles(l))
            base, n = [], 0
            for units in (nq, nq, 4, 4, 4, nq, TILES, TILES):
                base.append(n)
                n += units
            return base + [n]

        def group_end(l, g):
            if g >= G_O0:
                return S[l]["o_full"], len(q_tiles(l)) * (g - G_O0 + 1)
            return S[l]["p_full"], unit_base(l)[g + 1]

        block = st.enter_context(nc.Block())

        @block.sync
        def _(sp):
            sp.dma_start(RAW[0:8, 512:640], c[0].rearrange("(n p) -> n p", p=P)).then_inc(cond_in, 16)
            sp.dma_start(RAW[8:16, 512:640], c_ctx.rearrange("(n p) -> n p", p=P)).then_inc(cond_in, 16)
            def load_gate_bias(l):
                sp.dma_start(gate_row[l], b_mod[l, 2 * D:3 * D].partition_broadcast(2)).then_inc(bgate_in[l], 16)

            xv = x[0].rearrange("(r p) d -> p r d", p=P)
            for j in range(DEPTH * WM_TILES):
                k, c0 = j % WM_TILES // 3, WM_COLS * (j % 3)
                if j >= WM_SLOTS:
                    sp.wait_ge(wm_used, j - WM_SLOTS + 1)
                sp.dma_start(WM[:, j % WM_SLOTS, :],
                             w_mod[j // WM_TILES, P * k:P * (k + 1), c0:c0 + WM_COLS]).then_inc(wm_in[j % WM_SLOTS], 16)
                if j == 8:
                    load_gate_bias(0)
                    sp.dma_start(X[:, 0:2, :], ctx_in[0].rearrange("(r p) d -> p r d", p=P)).then_inc(S[0]["x_in"][0], 16)
                if j == 11:
                    sp.dma_start(X[:, 2:6, :], xv[:, 0:4, :]).then_inc(S[0]["x_in"][1], 16)
                if j == 15:
                    sp.dma_start(X[:, 6:10, :], xv[:, 4:8, :]).then_inc(S[0]["x_in"][2], 16)
                if j == 20:
                    sp.wait_ge(lam_dve, 2 * DEPTH)
                    load_gate_bias(1)
                if j == WM_TILES + 4:
                    sp.wait_ge(setup_turned, 1)
                    sp.dma_start(wraw[:, :, 0:GW], w_in[0, :, 0:GW].rearrange("(k p) n -> p k n", p=P)).then_inc(w_raw, 16)
                if j == WM_TILES + 12:
                    sp.dma_start(cosT[:, :, :], cos_t).then_inc(tab_in, 16)
                    sp.dma_start(sinT[:, :, :], sin_t).then_inc(tab_in, 16)
                    sp.wait_ge(gate_rows, 2)
                    sp.dma_start(gate_d[0], gate_row[0]).then_inc(gate_out, 16)

            def load_group(l, g):
                n = NG * l + g
                sp.wait_ge(w_lo, KT * n)
                col, w = GROUPS[g]
                src = (w_out if g >= G_O0 else w_in)[l, :, col:col + w]
                sp.dma_start(wraw[:, :, 0:w], src.rearrange("(k p) n -> p k n", p=P)).then_inc(w_raw, 16)

            for l in range(DEPTH):
                s = S[l]
                ts = q_tiles(l)
                nq, lo_row = len(ts), ts[0] * P
                if l:
                    sp.wait_ge(S[l - 1]["sg_v"], len(q_tiles(l - 1)))
                sp.dma_start(sguG[:, :], sgu_g[l].partition_broadcast(P)).then_inc(s["sg_in"], 16)
                load_group(l, G_AZ)
                sp.wait_ge(s["n_lo"], 8 * len(NORM_CHUNKS) + 24 * l)
                sp.dma_start(ws_in, sgu_w[l].rearrange("h p q -> p h q")).then_inc(s["sg_in"], 16)
                load_group(l, G_CBC)
                if l == 0:
                    sp.wait_ge(gate_rows, 4)
                    sp.dma_start(gate_d[1], gate_row[1]).then_inc(gate_out, 16)
                load_group(l, G_CXZ)
                load_group(l, G_BZ)
                sp.wait_ge(s["ya_cols"], 6 if l == 0 else 4)
                for a in range(2):
                    sp.dma_start(yT_d[a, :, lo_row:ROWS].rearrange("p (r n) -> p r n", n=P),
                                 uv[:, ts[0]:TILES, 256 + P * a:256 + P * (a + 1)]).then_inc(s["y_out"], 16)
                load_group(l, G_Q)
                for i in range(2):
                    sp.wait_ge(s["yc_ready"], i + 1 + 2 * l)
                    sp.dma_start(yT_d[2 + i, :, lo_row:ROWS], SM[:, lo_row:ROWS]).then_inc(s["yc_out"], 16)
                for i in range(4):
                    sp.wait_ge(s["p_free"], unit_base(l)[G_BZ] + i + 1)
                    sp.dma_start(bz_d[i, :, lo_row:ROWS], bzs[:, i, lo_row:ROWS]).then_inc(s["bz_out"], 16)
                load_group(l, G_K)
                load_group(l, G_V)
                load_group(l, G_O0)
                def load_bz(h):
                    sp.wait_ge(s["v_lo"], h + (1 + 4 * l))
                    sp.dma_start(qkv[:, ts[0]:TILES, bass.ds(h * P + 2 * GW, P)],
                                 bz_d[bass.ds(h, 1), :, lo_row:ROWS].rearrange("o p (r n) -> p (o r) n", n=P)).then_inc(s["bzh_in"], 16)

                with sp.Fori(0, HEADS - 1) as h:
                    load_bz(h)
                load_bz(HEADS - 1)
                sp.wait_ge(s["y_out"], 32)
                sp.wait_ge(s["yc_out"], 32 + 32 * l)
                sp.wait_ge(s["rope_ready"], 2 * HEADS * (l + 1))
                for i, k in enumerate((0, 1, 6, 7)):
                    sp.dma_start(y_rows(k, ts[0]), yT_d[i, :, lo_row:ROWS].rearrange("p (r n) -> p r n", n=P)).then_inc(s["y_in"][i], 16)
                sp.wait_ge(s["yb_ready"], HEADS)
                sp.wait_ge(gate_out, 32)
                for j in range(2):
                    sp.dma_start(SM[:, D * j:D * (j + 1)], gate_d[l, j].partition_broadcast(P)).then_inc(s["gate_in"], 16)
                sp.wait_ge(s["y_lo"], KT + 8 * l)
                if l == 0:
                    sp.dma_start(X[:, 0:2, :], ctx_in[0].rearrange("(r p) d -> p r d", p=P)).then_inc(s["x_in"][0], 16)
                else:
                    sp.wait_ge(S[0]["x_out"][0], 16 * 6)
                    sp.wait_ge(S[0]["x_out"][1], 16 * 4)
                for i, (a, b) in enumerate(NORM_CHUNKS[1:]):
                    src = xv[:, a - 2:b - 2, :] if l == 0 else x1_d[a:b].rearrange("r p d -> p r d")
                    sp.dma_start(X[:, a:b, :], src).then_inc(s["x_in"][i + 1], 16)
                load_group(l, G_O1)
                if l == 0:
                    load_group(l + 1, G_UV)
                    for n, r in enumerate(ts):
                        sp.wait_ge(s["o_x"], nq + n + 1)
                        sp.dma_start(x1_d[r], X[:, r, :]).then_inc(s["x_out"][r // 6], 16)
                else:
                    sp.dma_start(QX[:, XT + 1024:XT + 2048], final_g.partition_broadcast(P)).then_inc(s["fg_in"], 16)
                    for n, r in enumerate(ts):
                        sp.wait_ge(s["f_y"], n + 1)
                        sp.dma_start(out[0, P * n:P * (n + 1), :], X[:, r, :]).then_inc(s["f_out"], 16)
                    sp.wait_ge(s["f_out"], 16 * nq)

        @block.gpsimd
        def _(pool):
            nc.gpsimd.memset(ident[:, :], 0.0).then_inc(ident_ready, 1)
            pool.wait_ge(ident_ready, 1)
            nc.gpsimd.affine_select(out=ident[:, :], in_=ident[:, :], compare_op=ALU.not_equal, fill=1.0,
                                    base=0, pattern=[[-1, P]], channel_multiplier=1).then_inc(ident_ready, 1)
            nc.gpsimd.memset(ones[:, :], 1.0 / P).then_inc(ident_ready, 1)
            pool.wait_ge(tab_in, 32)
            for l in range(DEPTH):
                s = S[l]
                nq, n0 = len(q_tiles(l)), q_tiles(l)[0]
                pool.wait_ge(s["p_free"], unit_base(l)[G_V])

                def swap_halves(h, off, i):
                    src = qkv[:, CTX_TILES:TILES, head_cols(h, off + GW * i)].rearrange("p r (a f e) -> p r a f e", f=2, e=16)
                    dst = swapped(h, i).rearrange("p r (a f e) -> p r a f e", f=2, e=16)
                    tab = sinT[:, :, :].rearrange("p r (a f e) -> p r a f e", f=2, e=16)
                    for m in range(2):
                        for f in range(2):
                            nc.gpsimd.tensor_tensor(dst[:, :, 2 * m:2 * m + 2, f, :], src[:, :, 2 * m:2 * m + 2, 1 - f, :],
                                                    tab[:, :, :, f, :], ALU.mult).then_inc(s["rope_swap"], 1)

                swap_halves(None, 0, 0)
                swap_halves(None, 0, 1)
                def head(h, last):
                    full = 0
                    for n in range(nq):
                        if n + n0 >= CTX_TILES:
                            b = n % 2
                            pool.wait_ge(s["coef"], h * nq + (n + 1))
                            e0, e1 = prob[:, b, 0, P * LOW_KEYS:], prob[:, b, 1, P * LOW_KEYS:]
                            nc.gpsimd.tensor_tensor(e1, e1, rz[:, 1, b:b + 1].to_broadcast([P, ROWS - P * LOW_KEYS]), ALU.mult).then_inc(s["comb_mul"], 1)
                            pool.wait_ge(s["comb_mul"], h * LAT_TILES + (full + 1))
                            nc.gpsimd.tensor_tensor(e0, e0, e1, ALU.add).then_inc(s["comb"], 1)
                            full += 1
                        if n == 0:
                            pool.wait_ge(s["v_hi"], h + (1 + 4 * l))
                            nc.gpsimd.tensor_tensor(vhl[:, 1, :, :], qkv[:, :, bass.ds(h * P + 2 * GW, P)],
                                                    vhl[:, 0, :, :].bitcast(F32), ALU.subtract).then_inc(s["v_lo"], 1)
                        if n == nq - 4 and not last:
                            swap_halves(h, P, 0)
                        if n == nq - 3 and not last:
                            swap_halves(h, P, 1)
                    if last:
                        return
                    y = qkv[:, n0:, bass.ds(h * P, P)]
                    pool.wait_ge(s["rstd_done"], h + 1)
                    pool.wait_ge(s["sq_done"], h * (3 - l) + (3 - l))
                    nc.gpsimd.tensor_tensor(y, y, SM[:, P * n0:ROWS].rearrange("p (r n) -> p r n", n=P), ALU.mult).then_inc(s["yb_ready"], 1)

                with pool.Fori(0, HEADS - 1) as h:
                    head(h, False)
                head(HEADS - 1, True)

        @block.tensor
        def _(pe):
            mm = nc.tensor.matmul
            pe.wait_ge(ident_ready, 3)
            pe.wait_ge(cond_in, 32)
            nc.tensor.transpose(PS[:, 0, 128:144], RAW[0:16, 512:640], ident[0:16, 0:16]).then_inc(cond_turned, 1)
            def mod_tile(j):
                k, c = j % WM_TILES // 3, j % 3
                pe.wait_ge(wm_in[j % WM_SLOTS], 16 * (j // WM_SLOTS + 1))
                for b in range(2):
                    t = mm(PS[0:2, 1 + 2 * c + b, :], condT[:, :, k], WM[:, j % WM_SLOTS, 512 * b:512 * (b + 1)],
                           start=(k == 0), stop=(k == KT - 1))
                t.then_inc(wm_used, 1)

            def mod_turn(l):
                pe.wait_ge(mod_rows, 4 * (l + 1))
                for n in range(16):
                    t = nc.tensor.transpose(PS[:, 7, 2 * n:2 * n + 2], mod_row[:, P * n:P * (n + 1)], ident[0:2, 0:2])
                t.then_inc(mod_turned, 1)

            pe.wait_ge(cond_ready, 1)
            for j in range(WM_TILES):
                if j == 16:
                    pe.wait_ge(vec_in, 16 * 20)
                    for l in range(DEPTH):
                        t = nc.tensor.transpose(PS[:, 0, 64 * l:64 * l + V_ROWS], RAW[0:V_ROWS, 256 * l:256 * l + P],
                                                ident[0:V_ROWS, 0:V_ROWS])
                    t.then_inc(setup_turned, 1)
                mod_tile(j)
            mod_turn(0)
            pe.wait_ge(gate_rows, 2)

            def three(o, wt, mv, start, stop):
                mm(o, wt(0), mv(0), start=start, stop=False)
                mm(o, wt(0), mv(1), start=False, stop=False)
                return mm(o, wt(1), mv(0), start=False, stop=stop)

            def rows_unit(bank, r, w, wait_n, last_of_group, h_ready=None):
                for k in range(KT):
                    if h_ready is not None:
                        pe.wait_ge(h_ready[0], h_ready[1] + k + 1)
                    if wait_n is not None:
                        pe.wait_ge(w_lo, wait_n + k + 1)
                    t = three(PS[:, bank, 0:w], lambda i: Hs[:, i, k, P * r:P * (r + 1)],
                              lambda i: W[:, i, k, 0:w], k == 0, k == KT - 1)
                    if last_of_group and k < KT - 1:
                        t.then_inc(w_used, 1)
                return t

            def cols_unit(bank, ct, l, wait_n, last_of_group):
                for k in range(KT):
                    if wait_n is not None:
                        pe.wait_ge(w_lo, wait_n + k + 1)
                    for r0, n, b, o in row_chunks(l):
                        t = three(PS[:, bank + b, o:o + n], lambda i: W[:, i, k, P * ct:P * (ct + 1)],
                                  lambda i: Hs[:, i, k, r0:r0 + n], k == 0, k == KT - 1)
                    if last_of_group and k < KT - 1:
                        t.then_inc(w_used, 1)
                return t

            for l in range(DEPTH):
                s = S[l]
                ts = q_tiles(l)
                nq, ub, lo_row = len(ts), unit_base(l), ts[0] * P
                banks = NORM_BANKS[l]
                order = [(c, k) for c in norm_order(l) for k in range(KT)]
                if l == 0:
                    pe.wait_ge(mod_cols, 3)

                def norm_turn(n):
                    (a, b), k = order[n]
                    if k == 0:
                        pe.wait_ge(s["n_xn"], 10 * l + n_xn_due(l, n // KT))
                    if n >= len(banks):
                        pe.wait_ge(s["n_h"], n - len(banks) + 1 + 24 * l)
                    for r in range(a, b):
                        t = nc.tensor.transpose(PS[:, banks[n % len(banks)], P * (r - a):P * (r - a + 1)],
                                                X[:, r, P * k:P * (k + 1)], ident[:, :])
                    t.then_inc(s["n_turned"], 1)

                if l == 0:
                    for n in range(WM_TILES):
                        norm_turn(n)
                        mod_tile(WM_TILES + n)
                    turns = []
                else:
                    for n in range(KT):
                        norm_turn(n)
                    turns = list(range(KT, 3 * KT))
                for g in (G_UV, G_AZ):
                    for n, r in enumerate(ts):
                        u = ub[g] + n
                        for i in range(4):
                            if turns and n:
                                norm_turn(turns.pop(0))
                        if u >= 5:
                            pe.wait_ge(s["p_free"], u - 4)
                        first = g == G_UV and r == chunk_of(r)[0]
                        t = rows_unit(u % 5, r, GROUPS[g][1], KT * (NG * l + g) if n == 0 else None, n == nq - 1,
                                      (s["n_lo"], 24 * l + KT * norm_order(l).index(chunk_of(r))) if first else None)
                        t.then_inc(s["p_full"], 1)
                        if (l, g, n) == (0, G_UV, 0):
                            mod_turn(1)
                if l == 0:
                    pe.wait_ge(mod_cols, 6)
                    pe.wait_ge(gate_rows, 4)
                pe.wait_ge(s["p_free"], ub[G_CBC])
                for g in (G_CBC, G_CXZ, G_BZ):
                    for ct in range(4):
                        u = ub[g] + ct
                        if u >= ub[G_CBC] + 2:
                            pe.wait_ge(s["p_free"], u - 1)
                        t = cols_unit(3 * (ct % 2), ct, l, KT * (NG * l + g) if ct == 0 else None, ct == 3)
                        t.then_inc(s["p_full"], 1)
                        if (g, ct) == (G_CBC, 0):
                            pe.wait_ge(s["sg_in"], 32 + 32 * l)
                            for hh in range(4):
                                t = nc.tensor.transpose(PS[:, 6, P * hh:P * (hh + 1)], ws_in[:, hh, :], ident[:, :])
                            t.then_inc(s["sgw_turned"], 1)
                        if (g, ct) == (G_CBC, 1):
                            pe.wait_ge(s["sgw_ready"], 1 + 1 * l)
                            pe.wait_ge(s["sg_v"], nq)
                            half = nq // 2
                            for hh in range(4):
                                for i in range(2):
                                    n = 2 * hh + i
                                    if n >= 2:
                                        pe.wait_ge(s["sg_free"], n - 1 + 8 * l)
                                    a = ts[0] + half * i
                                    mm(PS[:, 6 + i, 0:half * HD].rearrange("p (r n) -> p r n", n=HD), wsT[:, hh, :],
                                       uv[:, a:a + half, 256 + HD * hh:256 + HD * (hh + 1)],
                                       start=True, stop=True).then_inc(s["sg_full"], 1)
                        if (g, ct) == (G_CXZ, 1):
                            pe.wait_ge(s["ya_ready"], 1 + 1 * l)
                            n = 0
                            for a in range(2):
                                for r0, r1 in q_turns(l):
                                    if n >= 2:
                                        pe.wait_ge(s["ya_cols"], n - 1)
                                    for r in range(r0, r1):
                                        t = nc.tensor.transpose(PS[:, 6 + n % 2, P * (r - r0):P * (r - r0 + 1)],
                                                                uv[:, r, P * a:P * (a + 1)], ident[:, :])
                                    t.then_inc(s["ya_turned"], 1)
                                    n += 1
                pe.wait_ge(s["p_free"], ub[G_Q])
                if l == DEPTH - 1:
                    for n, r in enumerate(ts):
                        if n >= 5:
                            pe.wait_ge(s["p_free"], ub[G_Q] + n - 4)
                        t = rows_unit(n % 5, r, GW, KT * (NG * l + G_Q) if n == 0 else None, n == nq - 1)
                        t.then_inc(s["p_full"], 1)
                    pe.wait_ge(s["p_free"], ub[G_K])
                g0 = G_Q if l < DEPTH - 1 else G_K
                with pe.Fori(0, G_O0 - g0) as i:
                    for r in range(TILES):
                        pe.wait_ge(s["p_free"], i * TILES + (ub[g0] + r - 4))
                        t = rows_unit(r % 5, r, GW, None if r else i * KT + KT * (NG * l + g0), r == TILES - 1)
                        t.then_inc(s["p_full"], 1)

                pe.wait_ge(s["p_free"], ub[-1])
                plan, nprep = slot_plan(l), len(prep_turns(l))
                nslot = len(plan)
                used = [0]

                def slot(h):
                    _, bank, back = plan[used[0]]
                    pe.wait_ge(s["slot_free"], h * nslot + (nprep + used[0] - back + 1))
                    used[0] += 1
                    return bank

                def prep(h):
                    for n, (i, m, r0, r1) in enumerate(prep_turns(l)):
                        if m == 0 and r0 == (q_turns(l) if i == 0 else K_TURNS)[0][0]:
                            at = i + 1 + 8 * l if h is None else h * 2 + (i + 3 + 8 * l)
                            pe.wait_ge(s["rope_ready"], at)
                            pe.wait_ge(s["ctx_qk"], at)
                        if h is not None:
                            b = slot(h)
                        else:
                            b = PREP_BANKS[n % 5]
                            if n >= 5:
                                pe.wait_ge(s["slot_free"], n - 4)
                        for r in range(r0, r1):
                            t = nc.tensor.transpose(PS[:, b, P * (r - r0):P * (r - r0 + 1)],
                                                    rope[:, i, r, P * m:P * (m + 1)], ident[:, :])
                        t.then_inc(s["slot_full"], 1)

                prep(None)
                def head(h, last):
                    used[0] = 0

                    def scores(n, m):
                        if n:
                            pe.wait_ge(s[f"exp{m}"], h * nq + n)
                        tile = ts[n]
                        for r0, w in (((0, 256),) if tile < CTX_TILES else ((0, 512), (512, 512), (1024, 256))):
                            o = 1536 * m + r0
                            for part in range(2):
                                t = mm(PF[:, o:o + w], qst[:, m, P * tile:P * (tile + 1)],
                                       kst[:, part, m, r0:r0 + w], start=(part == 0), stop=(part == 1))
                        t.then_inc(s[f"s_full{m}"], 1)

                    def turn(n, k0, k1):
                        b = slot(h)
                        for kk in range(k0, k1):
                            t = nc.tensor.transpose(PS[:, b, P * (kk - k0):P * (kk - k0 + 1)],
                                                    prob[:, n % 2, 0, P * kk:P * (kk + 1)], ident[:, :])
                        t.then_inc(s["slot_full"], 1)

                    def values(chunk):
                        a, e = chunk
                        w = P * (e - a)
                        nk = CTX_TILES if a < CTX_TILES else TILES
                        pe.wait_ge(s["slot_free"], h * nslot + (nprep + used[0]))
                        pe.wait_ge(s["v_lo"], h + (1 + 4 * l))
                        b = slot(h)
                        for kk in range(nk):
                            t = three(PS[:, b, 0:w], lambda i: vhl[:, i, kk, :], lambda i: aT[:, i, kk, 0:w],
                                      kk == 0, kk == nk - 1)
                        t.then_inc(s["slot_full"], 1)

                    pe.wait_ge(s["slot_free"], h * nslot + nprep)
                    scores(0, 0)
                    pe.wait_ge(s["ln_done"], h + 1)
                    scores(0, 1)
                    scores(1, 0)
                    for t in range(1, nq + 1):
                        if t < nq:
                            scores(t, 1)
                        if chunk_due(l, t - 2):
                            values(chunk_due(l, t - 2))
                        runs = key_turns(ts[t - 1])
                        pe.wait_ge(s["comb_low"], h * nq + t)
                        for run in runs[:2]:
                            turn(t - 1, *run)
                        if t + 1 < nq:
                            scores(t + 1, 0)
                        for run in runs[2:]:
                            pe.wait_ge(s["comb"], h * LAT_TILES + (ts[t - 1] - CTX_TILES + 1))
                            turn(t - 1, *run)
                    values(chunk_due(l, nq - 1))
                    if not last:
                        prep(h)
                    pe.wait_ge(s["sq_done"], h * (3 - l) + (3 - l))
                    for r0, w in ((lo_row, 512 - lo_row), (512, 512), (1024, 256)):
                        t = mm(PF[:, 1536 + r0:1536 + r0 + w], ones[:, :], SM[:, r0:r0 + w], start=True, stop=True)
                    t.then_inc(s["ms_full"], 1)

                with pe.Fori(0, HEADS - 1) as h:
                    head(h, False)
                head(HEADS - 1, True)
                pe.wait_ge(s["slot_free"], HEADS * nslot)
                for i, k in enumerate(Y_ORDER):
                    pe.wait_ge(s["y_lo"], i + 1 + 8 * l)
                    pe.wait_ge(w_lo, KT * (NG * l + G_O0) + k + 1)
                    for u in range(3):
                        t = three(PS[:, u, :], lambda i: Hs[:, i, k, P * ts[u]:P * (ts[u] + 1)],
                                  lambda i: W[:, i, k, :], i == 0, i == KT - 1)
                        if i == KT - 1:
                            t.then_inc(s["o_full"], 1)
                pe.wait_ge(s["ln_done"], 1 + HEADS)
                for g in range(2):
                    for n, r in enumerate(ts):
                        u = nq * g + n
                        if u < 3:
                            continue
                        if u >= 5:
                            pe.wait_ge(s["o_z"], u - 4)
                        t = rows_unit(u % 5, r, GW, KT * (NG * l + G_O0 + g) if n == 0 else None, n == nq - 1)
                        t.then_inc(s["o_full"], 1)

        @block.scalar
        def _(act):
            A = nc.scalar.activation
            act.wait_ge(cond_turned, 1)
            A(condT[:, :, :], PS[:, 0, 128:144].rearrange("p (j k) -> p j k", j=2), ACT.Silu).then_inc(cond_ready, 1)
            for l in range(DEPTH):
                v = RAW[0:V_ROWS, 256 * l:256 * l + P]
                rows = [(V_BSH, b_mod[l, 0:2 * D], 16), (V_G, norm_g[l, :], 8), (V_SUB, subln_g[l, :], 1)]
                for at, src, n in rows:
                    act.dma_start(v[at:at + n, :], src.rearrange("(n p) -> n p", p=P)).then_inc(vec_in, 16)
                act.dma_start(v[V_CW:V_CW + 6, :], conv_w[l].rearrange("w (n p) -> (w n) p", p=P)).then_inc(vec_in, 16)
                act.dma_start(v[V_CB:V_CB + 2, :], conv_b[l].rearrange("(n p) -> n p", p=P)).then_inc(vec_in, 16)
                act.dma_start(v[V_SB:V_SB + 4, :], sgu_b[l]).then_inc(vec_in, 16)
                for i, a in enumerate((lq1, lk1, lq2, lk2)):
                    act.dma_start(SM[:, 256 * l + HD * i:256 * l + HD * (i + 1)],
                                 a[l].partition_broadcast(P)).then_inc(vec_in, 16)
            act.wait_ge(lam_dve, 2 * DEPTH)
            for l in range(DEPTH):
                A(lamE[:, l, 2:4], lamE[:, l, 0:2], ACT.Exp).then_inc(lam_exp, 1)
            def norm_square(l, r):
                if r:
                    act.wait_ge(S[l]["n_sq"], r + 10 * l)
                A(QX[:, XT:XT + D], X[:, r, :], ACT.Square, accum_out=stat[:, 0, r:r + 1]).then_inc(S[l]["n_sq"], 1)

            def norm_root(l, i):
                a, b = norm_order(l)[i]
                act.wait_ge(S[l]["n_ms"], i + 1 + 3 * l)
                A(stat[:, 1, a:b], stat[:, 1, a:b], ACT.Sqrt).then_inc(S[l]["n_root"], 1)

            def copy_mod_rows(l):
                act.wait_ge(wm_used, WM_TILES * (l + 1))
                if l:
                    act.wait_ge(mod_turned, l)
                for b in range(4):
                    A(mod_row[:, 512 * b:512 * (b + 1)], PS[0:2, 1 + b, :], ACT.Copy).then_inc(mod_rows, 1)

            def split_hi(l, g):
                n = NG * l + g
                w = GROUPS[g][1]
                act.wait_ge(w_raw, 16 * (n + 1))
                for k in range(KT):
                    if n and k < KT - 1:
                        act.wait_ge(w_used, (KT - 1) * (n - 1) + k + 1)
                    elif n:
                        act.wait_ge(*group_end(*divmod(n - 1, NG)))
                    A(W[:, 0, k, 0:w], wraw[:, k, 0:w], ACT.Copy).then_inc(w_hi, 1)

            for i, (a, b) in enumerate(NORM_CHUNKS):
                act.wait_ge(S[0]["x_in"][i], 16)
                for r in range(a, b):
                    norm_square(0, r)
                norm_root(0, i)
            copy_mod_rows(0)
            for l in range(DEPTH):
                s = S[l]
                ts = q_tiles(l)
                nq, ub = len(ts), unit_base(l)
                lo = ts[0] * P
                act.wait_ge(mod_cols, 3 * (l + 1))
                for n, ((a, b), k) in enumerate([(c, k) for c in norm_order(l) for k in range(KT)]):
                    j = 1 if a < CTX_TILES else 0
                    w = P * (b - a)
                    act.wait_ge(s["n_turned"], n + 1 + 24 * l)
                    if n >= 4:
                        act.wait_ge(s["n_lo"], n - 3 + 24 * l)
                    A(QX[:, XT + 1024 + 512 * (n % 4):XT + 1024 + 512 * (n % 4) + w], PS[:, NORM_BANKS[l][n % len(NORM_BANKS[l])], 0:w],
                      ACT.Identity, scale=shA[:, l, 1, j, k:k + 1], bias=shA[:, l, 0, j, k:k + 1]).then_inc(s["n_h"], 1)
                if l == 0:
                    act.wait_ge(wm_used, DEPTH * WM_TILES)
                    split_hi(l, G_UV)
                    copy_mod_rows(1)
                for n, r in enumerate(ts):
                    if n == nq - 1:
                        split_hi(l, G_AZ)
                    act.wait_ge(s["p_full"], n + 1)
                    A(uv[:, r, :], PS[:, n % 5, :], ACT.Gelu_apprx_tanh).then_inc(s["p_free"], 1)
                    act.wait_ge(s["p_free"], n + 1)
                    if n:
                        act.wait_ge(s["sg_sq"], n)
                    A(QX[:, 7680:7936], uv[:, r, 256:512], ACT.Square, accum_out=stat[:, 2, r:r + 1]).then_inc(s["sg_sq"], 1)
                act.wait_ge(s["sg_ms"], 1 + 1 * l)
                A(stat[:, 0, ts[0]:], stat[:, 0, ts[0]:], ACT.Sqrt).then_inc(s["sg_root"], 1)
                for n, r in enumerate(ts):
                    if n == nq - 1:
                        split_hi(l, G_CBC)
                    u = ub[G_AZ] + n
                    act.wait_ge(s["p_full"], u + 1)
                    A(az[:, r, :], PS[:, u % 5, 0:256], ACT.Silu).then_inc(s["p_free"], 1)
                for g in (G_CBC, G_CXZ, G_BZ):
                    for ct in range(4):
                        if ct == 3:
                            split_hi(l, g + 1)
                        u = ub[g] + ct
                        act.wait_ge(s["p_full"], u + 1)
                        src = PF[:, 1536 * (ct % 2) + 256 + lo:1536 * (ct % 2) + 256 + ROWS]
                        if g == G_CBC:
                            A(cbc[:, ct, lo:], src, ACT.Copy).then_inc(s["p_free"], 1)
                        elif g == G_CXZ:
                            if ct < 2:
                                act.wait_ge(s["sg_full"], 8 + 8 * l)
                                A(cxz[:, ct, lo:], src, ACT.Copy).then_inc(s["p_free"], 1)
                            else:
                                act.wait_ge(s["cc_cx"], ct - 1 + 2 * l)
                                A(cxz[:, ct - 2, lo:], src, ACT.Silu).then_inc(s["p_free"], 1)
                        else:
                            if ct == 0:
                                act.wait_ge(s["y_out"], 32)
                            A(bzs[:, ct, lo:], src, ACT.Silu).then_inc(s["p_free"], 1)
                        if (g, ct) == (G_CBC, 0):
                            act.wait_ge(s["sgw_turned"], 1 + 1 * l)
                            A(wsT[:, :, :], PS[:, 6, :].rearrange("p (h n) -> p h n", h=4), ACT.Copy).then_inc(s["sgw_ready"], 1)
                        if (g, ct) == (G_CXZ, 1):
                            n = 0
                            for a in range(2):
                                for r0, r1 in q_turns(l):
                                    act.wait_ge(s["ya_turned"], n + 1)
                                    A(uv[:, r0:r1, 256 + P * a:256 + P * (a + 1)],
                                      PS[:, 6 + n % 2, 0:P * (r1 - r0)].rearrange("p (r n) -> p r n", n=P),
                                      ACT.Copy).then_inc(s["ya_cols"], 1)
                                    n += 1
                act.wait_ge(s["bz_out"], 64 + 64 * l)
                act.wait_ge(s["yc_out"], 32 + 32 * l)
                if l == DEPTH - 1:
                    for n, r in enumerate(ts):
                        if n == nq - 1:
                            split_hi(l, G_K)
                        act.wait_ge(s["p_full"], ub[G_Q] + n + 1)
                        A(qkv[:, r, 0:GW], PS[:, n % 5, :], ACT.Copy).then_inc(s["p_free"], 1)
                g0 = G_Q if l < DEPTH - 1 else G_K
                with act.Fori(0, G_O0 - g0) as i:
                    for r in range(TILES):
                        if r == TILES - 1:
                            n = NG * l + g0
                            act.wait_ge(w_raw, i * 16 + 16 * (n + 2))
                            for k in range(KT):
                                if k < KT - 1:
                                    act.wait_ge(w_used, i * (KT - 1) + ((KT - 1) * n + k + 1))
                                else:
                                    act.wait_ge(s["p_full"], i * TILES + ub[g0 + 1])
                                A(W[:, 0, k, :], wraw[:, k, :], ACT.Copy).then_inc(w_hi, 1)
                        act.wait_ge(s["p_full"], i * TILES + (ub[g0] + r + 1))
                        A(qkv[:, r, bass.ds(i * GW + GW * (g0 - G_Q), GW)], PS[:, r % 5, :], ACT.Copy).then_inc(s["p_free"], 1)

                nprep, nslot = len(prep_turns(l)), len(slot_plan(l))
                act.wait_ge(s["p_free"], ub[-1])
                act.wait_ge(w_lo, KT * (NG * l + G_O0 + 1))

                def ctx_rows(h, off):
                    for i in range(2):
                        src = qkv[:, 0:CTX_TILES, head_cols(h, off + GW * (i if l == 0 else 1))]
                        for m in range(2):
                            t = A(rope[:, i, 0:CTX_TILES, P * m:P * (m + 1)].rearrange("p r (d n) -> p r d n", d=2),
                                  src[:, :, HD * m:HD * (m + 1)].unsqueeze(2).to_broadcast([P, CTX_TILES, 2, HD]), ACT.Copy)
                        t.then_inc(s["ctx_qk"], 1)

                def split_y(i):
                    k = Y_ORDER[i]
                    if k in (0, 1, 6, 7):
                        act.wait_ge(s["y_in"][(0, 1, 6, 7).index(k)], 16 + 16 * l)
                    else:
                        act.wait_ge(s["yb_ready"], k - 1)
                    A(Hs[:, 0, k, lo:].rearrange("p (r n) -> p r n", n=P), y_rows(k, ts[0]), ACT.Copy).then_inc(s["y_hi"], 1)

                def prep(full, at):
                    for n, (i, m, r0, r1) in enumerate(prep_turns(l)):
                        act.wait_ge(s["slot_full"], full + (at + n + 1))
                        src = PS[:, PREP_BANKS[n % 5], 0:P * (r1 - r0)]
                        if i == 0:
                            A(qst[:, m, P * r0:P * r1], src, ACT.Copy, scale=SC).then_inc(s["slot_hi"], 1)
                        else:
                            A(kst[:, 0, m, P * r0:P * r1], src, ACT.Copy).then_inc(s["slot_hi"], 1)

                ctx_rows(None, 0)
                prep(0, 0)
                A(lamE[:, l, 2:3], lamE[:, l, 0:1], ACT.Exp).then_inc(s["ln_done"], 1)
                def head(h, last):
                    n = nprep

                    def exps(q, m):
                        w = 256 if ts[q] < CTX_TILES else ROWS
                        act.wait_ge(s[f"max{m}"], h * nq + (q + 1))
                        A(prob[:, q % 2, m, 0:w], PF[:, 1536 * m:1536 * m + w], ACT.Exp,
                          bias=nmax[:, m, q % 2:q % 2 + 1], accum_out=Z[:, m, q % 2:q % 2 + 1]).then_inc(s[f"exp{m}"], 1)

                    def turned_hi(q, k0, k1, n):
                        c0 = (ts[q] - chunk_of(ts[q])[0]) * P
                        act.wait_ge(s["slot_full"], h * nslot + (n + 1))
                        A(aT[:, 0, k0:k1, c0:c0 + P], PS[:, 6 + (n - nprep) % 2, 0:P * (k1 - k0)].rearrange("p (k q) -> p k q", q=P),
                          ACT.Copy).then_inc(s["slot_hi"], 1)

                    def squares(chunk, n):
                        w = P * (chunk[1] - chunk[0])
                        act.wait_ge(s["slot_full"], h * nslot + (n + 1))
                        A(SM[:, P * chunk[0]:P * chunk[1]], PS[:, 6 + (n - nprep) % 2, 0:w], ACT.Square).then_inc(s["slot_hi"], 1)

                    exps(0, 0)
                    exps(0, 1)
                    A(vhl[:, 0, :, :], qkv[:, :, bass.ds(h * P + 2 * GW, P)], ACT.Copy).then_inc(s["v_hi"], 1)
                    for t in range(1, nq + 1):
                        for run in key_turns(ts[t - 2])[2:] if t >= 2 else []:
                            turned_hi(t - 2, *run, n)
                            n += 1
                        if t < nq:
                            exps(t, 0)
                        if chunk_due(l, t - 2):
                            squares(chunk_due(l, t - 2), n)
                            n += 1
                        for run in key_turns(ts[t - 1])[:2]:
                            turned_hi(t - 1, *run, n)
                            n += 1
                        if t < nq:
                            exps(t, 1)
                    for run in key_turns(ts[nq - 1])[2:]:
                        turned_hi(nq - 1, *run, n)
                        n += 1
                    if last:
                        for i in range(5):
                            split_y(i)
                    else:
                        ctx_rows(h, P)
                    squares(chunk_due(l, nq - 1), n)
                    n += 1
                    if last:
                        split_y(5)
                        split_y(6)
                    else:
                        prep(h * nslot, n)
                    r = SM[:, lo:ROWS]
                    act.wait_ge(s["ms_full"], h + 1)
                    A(r, PF[:, 1536 + lo:1536 + ROWS], ACT.Ln).then_inc(s["ln_done"], 1)
                    act.wait_ge(s["ln_done"], h + 2)
                    A(r, r, ACT.Exp, scale=-0.5).then_inc(s["rstd_done"], 1)

                with act.Fori(0, HEADS - 1) as h:
                    head(h, False)
                head(HEADS - 1, True)
                split_y(7)
                split_hi(l, G_O1)
                if l < DEPTH - 1:
                    for n, r in enumerate(ts):
                        if n == nq - 1:
                            split_hi(l + 1, G_UV)
                        act.wait_ge(s["o_x"], nq + n + 1)
                        norm_square(l + 1, r)
                        if r + 1 == norm_order(l + 1)[0][1]:
                            norm_root(l + 1, 0)
                    norm_root(l + 1, 1)
                    norm_root(l + 1, 2)
                else:
                    for n, r in enumerate(ts):
                        act.wait_ge(s["o_x"], nq + n + 1)
                        if n:
                            act.wait_ge(s["f_sq"], n)
                        A(QX[:, XT + 2048:XT + 3072], X[:, r, :], ACT.Square, accum_out=stat[:, 0, r:r + 1]).then_inc(s["f_sq"], 1)
                        act.wait_ge(s["f_ms"], n + 1)
                        A(stat[:, 1, r:r + 1], stat[:, 1, r:r + 1], ACT.Sqrt).then_inc(s["f_root"], 1)

        @block.vector
        def _(dve):
            V = nc.vector
            dve.wait_ge(vec_in, 16 * 20)
            for l in range(DEPTH):
                lv = SM[:, 256 * l:256 * (l + 1)].rearrange("p (a b n) -> p a b n", a=2, b=2)
                o = SM[:, 512 + P * l:512 + P * (l + 1)].rearrange("p (a n) -> p a n", a=2)
                V.tensor_tensor(o, lv[:, :, 0, :], lv[:, :, 1, :], ALU.mult).then_inc(lam_dve, 1)
                dve.wait_ge(lam_dve, 2 * l + 1)
                V.reduce_sum(lamE[:, l, 0:2], o, AX.X).then_inc(lam_dve, 1)
            for l in range(DEPTH):
                dve.wait_ge(lam_exp, l + 1)
                V.scalar_tensor_tensor(out=nlam[:, l:l + 1], in0=lamE[:, l, 3:4], scalar=lam_init(l), in1=lamE[:, l, 2:3],
                                       op0=ALU.subtract, op1=ALU.subtract).then_inc(lam_dve, 1)
            dve.wait_ge(setup_turned, 1)
            dve.wait_ge(cond_ready, 1)
            V.tensor_copy(vc[:, :, :], PS[:, 0, 0:128].rearrange("p (l v) -> p l v", l=2)[:, :, 0:V_ROWS]).then_inc(setup_cols, 1)
            dve.wait_ge(setup_cols, 1)
            for l in range(DEPTH):
                V.tensor_scalar(gsub[:, l:l + 1], vc[:, l, V_SUB:V_SUB + 1], 1.0 - lam_init(l), None, ALU.mult).then_inc(setup_cols, 1)

            def norm_rstd(l, i):
                s, (a, b) = S[l], norm_order(l)[i]
                dve.wait_ge(s["n_sq"], b + 10 * l)
                V.tensor_scalar(stat[:, 1, a:b], stat[:, 0, a:b], 1.0 / D, EPS, ALU.mult, ALU.add).then_inc(s["n_ms"], 1)
                dve.wait_ge(s["n_root"], i + 1 + 3 * l)
                V.reciprocal(stat[:, 1, a:b], stat[:, 1, a:b]).then_inc(s["n_rstd"], 1)

            def norm_scale(l, i):
                s, (a, b) = S[l], norm_order(l)[i]
                dve.wait_ge(s["n_rstd"], i + 1 + 3 * l)
                if l:
                    dve.wait_ge(s["x_out"][0], 16 * 6)
                    if i:
                        dve.wait_ge(s["x_out"][1], 16 * 4)
                for r in range(a, b):
                    V.tensor_scalar(X[:, r, :], X[:, r, :], stat[:, 1, r:r + 1], None, ALU.mult).then_inc(s["n_xn"], 1)

            def add_gates(l):
                dve.wait_ge(bgate_in[l], 16)
                dve.wait_ge(wm_used, WM_TILES * (l + 1))
                for b in range(2):
                    g = gate_row[l][:, 512 * b:512 * (b + 1)]
                    V.tensor_tensor(g, PS[0:2, 5 + b, :], g, ALU.add).then_inc(gate_rows, 1)

            def mod_columns(l):
                dve.wait_ge(mod_turned, l + 1)
                for part in range(2):
                    V.tensor_tensor(shA[:, l, part, :, :], PS[:, 7, 16 * part:16 * part + 16].rearrange("p (k j) -> p j k", j=2),
                                    vc[:, l, 8 * part:8 * part + 8].unsqueeze(1).to_broadcast([P, 2, KT]), ALU.add).then_inc(mod_cols, 1)
                dve.wait_ge(mod_cols, 3 * l + 2)
                V.scalar_tensor_tensor(out=shA[:, l, 1, :, :], in0=shA[:, l, 1, :, :], scalar=1.0,
                                       in1=vc[:, l, V_G:V_G + 8].unsqueeze(1).to_broadcast([P, 2, KT]),
                                       op0=ALU.add, op1=ALU.mult).then_inc(mod_cols, 1)

            def split_lo(l, g):
                n = NG * l + g
                w = GROUPS[g][1]
                for k in range(KT):
                    dve.wait_ge(w_hi, KT * n + k + 1)
                    V.tensor_tensor(W[:, 1, k, 0:w], wraw[:, k, 0:w], W[:, 0, k, 0:w].bitcast(F32), ALU.subtract).then_inc(w_lo, 1)

            for i in range(len(NORM_CHUNKS)):
                norm_rstd(0, i)
                norm_scale(0, i)
            add_gates(0)
            mod_columns(0)
            for l in range(DEPTH):
                s = S[l]
                ts = q_tiles(l)
                nq, ub = len(ts), unit_base(l)
                lo = ts[0] * P
                if l:
                    norm_rstd(l, 1)
                    norm_rstd(l, 2)
                for n, ((a, b), k) in enumerate([(c, k) for c in norm_order(l) for k in range(KT)]):
                    if l and n == KT:
                        norm_scale(l, 1)
                        norm_scale(l, 2)
                    ht = QX[:, XT + 1024 + 512 * (n % 4):XT + 1024 + 512 * (n % 4) + P * (b - a)]
                    dve.wait_ge(s["n_h"], n + 1 + 24 * l)
                    V.tensor_copy(Hs[:, 0, k, P * a:P * b], ht).then_inc(s["n_hi"], 1)
                    dve.wait_ge(s["n_hi"], n + 1 + 24 * l)
                    V.tensor_tensor(Hs[:, 1, k, P * a:P * b], ht, Hs[:, 0, k, P * a:P * b].bitcast(F32), ALU.subtract).then_inc(s["n_lo"], 1)
                if l == 0:
                    split_lo(0, G_UV)
                    add_gates(1)
                    mod_columns(1)
                split_lo(l, G_AZ)
                dve.wait_ge(s["sg_sq"], nq)
                V.tensor_scalar(stat[:, 0, ts[0]:], stat[:, 2, ts[0]:], 1.0 / 256, EPS, ALU.mult, ALU.add).then_inc(s["sg_ms"], 1)
                dve.wait_ge(s["sg_root"], 1 + 1 * l)
                V.reciprocal(stat[:, 0, ts[0]:], stat[:, 0, ts[0]:]).then_inc(s["sg_rstd"], 1)
                dve.wait_ge(s["sg_rstd"], 1 + 1 * l)
                dve.wait_ge(s["sg_in"], 32 + 32 * l)
                for r in ts:
                    V.scalar_tensor_tensor(out=uv[:, r, 256:512], in0=uv[:, r, 256:512], scalar=stat[:, 0, r:r + 1],
                                           in1=sguG[:, :], op0=ALU.mult, op1=ALU.mult).then_inc(s["sg_v"], 1)
                split_lo(l, G_CBC)
                half = nq // 2
                for hh in range(4):
                    for i in range(2):
                        a = ts[0] + half * i
                        u = uv[:, a:a + half, HD * hh:HD * (hh + 1)]
                        dve.wait_ge(s["sg_full"], 2 * hh + i + 1 + 8 * l)
                        V.scalar_tensor_tensor(out=u, in0=PS[:, 6 + i, 0:half * HD].rearrange("p (r n) -> p r n", n=HD),
                                               scalar=vc[:, l, V_SB + hh:V_SB + hh + 1], in1=u, op0=ALU.add, op1=ALU.mult).then_inc(s["sg_free"], 1)
                dve.wait_ge(s["sg_free"], 8 + 8 * l)
                dve.wait_ge(s["p_free"], ub[G_CBC])
                V.tensor_tensor(uv[:, ts[0]:, 0:256], uv[:, ts[0]:, 0:256], az[:, ts[0]:, :], ALU.mult).then_inc(s["ya_ready"], 1)
                split_lo(l, G_CXZ)
                for i in range(2):
                    dve.wait_ge(s["p_free"], ub[G_CXZ] + i + 1)
                    V.tensor_tensor(cbc[:, 2 + i, lo:], cbc[:, 2 + i, lo:], cxz[:, i, lo:], ALU.mult).then_inc(s["cc_cx"], 1)
                split_lo(l, G_BZ)
                nconv = 0
                if l == 0:
                    dve.wait_ge(gate_out, 32)
                for i in range(2):
                    t, acc = cbc[:, 2 + i, :], SM[:, 0:ROWS]
                    tap = [vc[:, l, V_CW + 2 * j + i:V_CW + 2 * j + i + 1] for j in range(3)]
                    dve.wait_ge(s["cc_cx"], i + 1 + 2 * l)
                    if i:
                        dve.wait_ge(s["yc_out"], 16 * i + 32 * l)
                    V.tensor_scalar(acc[:, lo:], t[:, lo:], tap[1], vc[:, l, V_CB + i:V_CB + i + 1], ALU.mult, ALU.add).then_inc(s["conv"], 1)
                    nconv += 1
                    for a, b in ([(0, 256), (256, ROWS)] if l == 0 else [(256, ROWS)]):
                        for j, (oa, ob, ia, ib) in enumerate(((a + 1, b, a, b - 1), (a, b - 1, a + 1, b))):
                            dve.wait_ge(s["conv"], nconv)
                            V.scalar_tensor_tensor(out=acc[:, oa:ob], in0=t[:, ia:ib], scalar=tap[2 * j], in1=acc[:, oa:ob],
                                                   op0=ALU.mult, op1=ALU.add).then_inc(s["conv"], 1)
                            nconv += 1
                    dve.wait_ge(s["conv"], nconv)
                    V.tensor_tensor(acc[:, lo:], acc[:, lo:], cbc[:, i, lo:], ALU.mult).then_inc(s["conv"], 1)
                    nconv += 1
                    dve.wait_ge(s["conv"], nconv)
                    dve.wait_ge(s["p_free"], ub[G_CXZ] + 3 + i)
                    V.tensor_tensor(acc[:, lo:], acc[:, lo:], cxz[:, i, lo:], ALU.mult).then_inc(s["yc_ready"], 1)
                split_lo(l, G_Q)
                if l == DEPTH - 1:
                    split_lo(l, G_K)
                g0 = G_Q if l < DEPTH - 1 else G_K
                with dve.Fori(0, G_O0 - g0) as i:
                    for k in range(KT):
                        dve.wait_ge(w_hi, i * KT + (KT * (NG * l + g0 + 1) + k + 1))
                        V.tensor_tensor(W[:, 1, k, :], wraw[:, k, :], W[:, 0, k, :].bitcast(F32), ALU.subtract).then_inc(w_lo, 1)

                nprep, nslot = len(prep_turns(l)), len(slot_plan(l))
                dve.wait_ge(w_lo, KT * (NG * l + G_O0 + 1))

                def rope_mul(h, off, i):
                    dve.wait_ge(s["rope_swap"], 4 * (i + 1) + 32 * l if h is None else h * 8 + (8 + 4 * (i + 1) + 32 * l))
                    x = qkv[:, CTX_TILES:TILES, head_cols(h, off + GW * i)].rearrange("p r (m n) -> p r m n", m=2)
                    V.tensor_tensor(x, x, cosT[:, :, :].unsqueeze(2).to_broadcast([P, LAT_TILES, 2, HD]), ALU.mult).then_inc(s["rope_mul"], 1)

                def rope_add(h, off, i):
                    dve.wait_ge(s["rope_mul"], i + 1 + 8 * l if h is None else h * 2 + (i + 3 + 8 * l))
                    x = qkv[:, CTX_TILES:TILES, head_cols(h, off + GW * i)]
                    for m in range(2):
                        dst = rope[:, i, CTX_TILES:TILES, P * m:P * (m + 1)].rearrange("p r (d n) -> p r d n", d=2)
                        c, w = [a[:, :, HD * m:HD * (m + 1)].unsqueeze(2).to_broadcast([P, LAT_TILES, 2, HD])
                                for a in (x, swapped(h, i))]
                        t = V.tensor_tensor(dst, c, w, ALU.add)
                    t.then_inc(s["rope_ready"], 1)

                def prep_lo(full, at):
                    for n, (i, m, r0, r1) in enumerate(prep_turns(l)):
                        dve.wait_ge(s["slot_hi"], full + (at + n + 1))
                        src = PS[HD * (1 - i):P, PREP_BANKS[n % 5], 0:P * (r1 - r0)]
                        if i == 0:
                            q = qst[HD:P, m, P * r0:P * r1]
                            V.scalar_tensor_tensor(out=q, in0=src, scalar=SC, in1=q.bitcast(F32),
                                                   op0=ALU.mult, op1=ALU.subtract).then_inc(s["slot_free"], 1)
                        else:
                            V.tensor_tensor(kst[:, 1, m, P * r0:P * r1], src,
                                            kst[:, 0, m, P * r0:P * r1].bitcast(F32), ALU.subtract).then_inc(s["slot_free"], 1)

                for i in range(2):
                    rope_mul(None, 0, i)
                    rope_add(None, 0, i)
                prep_lo(0, 0)
                def head(h, last):
                    n = nprep

                    def maxima(q, m):
                        w = 256 if ts[q] < CTX_TILES else ROWS
                        dve.wait_ge(s[f"s_full{m}"], h * nq + (q + 1))
                        V.tensor_reduce(nmax[:, m, q % 2:q % 2 + 1], PF[:, 1536 * m:1536 * m + w], AX.X, ALU.max,
                                        negate=True).then_inc(s[f"max{m}"], 1)

                    def combine(q):
                        b = q % 2
                        w = 256 if ts[q] < CTX_TILES else P * LOW_KEYS
                        z0, z1 = Z[:, 0, b:b + 1], Z[:, 1, b:b + 1]
                        at = h * nq + (q + 1)
                        dve.wait_ge(s["exp0"], at)
                        V.scalar_tensor_tensor(out=ez[:, ts[q]:ts[q] + 1], in0=z0, scalar=EPS * P, in1=z0, op0=ALU.mult, op1=ALU.mult)
                        dve.wait_ge(s["exp1"], at)
                        V.reciprocal(rz[:, 0, b:b + 1], z1).then_inc(s["rz_done"], 1)
                        dve.wait_ge(s["rz_done"], at)
                        V.scalar_tensor_tensor(out=rz[:, 1, b:b + 1], in0=rz[:, 0, b:b + 1], scalar=nlam[:, l:l + 1], in1=z0,
                                               op0=ALU.mult, op1=ALU.mult).then_inc(s["coef"], 1)
                        e0, e1 = prob[:, b, 0, 0:w], prob[:, b, 1, 0:w]
                        dve.wait_ge(s["coef"], at)
                        V.scalar_tensor_tensor(out=e0, in0=e1, scalar=rz[:, 1, b:b + 1], in1=e0,
                                               op0=ALU.mult, op1=ALU.add).then_inc(s["comb_low"], 1)

                    def turned_lo(q, k0, k1, n):
                        c0 = (ts[q] - chunk_of(ts[q])[0]) * P
                        dve.wait_ge(s["slot_hi"], h * nslot + (n + 1))
                        V.tensor_tensor(aT[:, 1, k0:k1, c0:c0 + P],
                                        PS[:, 6 + (n - nprep) % 2, 0:P * (k1 - k0)].rearrange("p (k q) -> p k q", q=P),
                                        aT[:, 0, k0:k1, c0:c0 + P].bitcast(F32), ALU.subtract).then_inc(s["slot_free"], 1)

                    def outputs(chunk, n):
                        a, e = chunk
                        dve.wait_ge(s["slot_hi"], h * nslot + (n + 1))
                        dve.wait_ge(s["bzh_in"], h * 16 + 16)
                        V.scalar_tensor_tensor(out=qkv[:, a:e, bass.ds(h * P, P)],
                                               in0=PS[:, 6 + (n - nprep) % 2, 0:P * (e - a)].rearrange("p (r n) -> p r n", n=P),
                                               scalar=gsub[:, l:l + 1], in1=qkv[:, a:e, bass.ds(h * P + 2 * GW, P)],
                                               op0=ALU.mult, op1=ALU.mult).then_inc(s["slot_free"], 1)
                        for r in range(a, e):
                            sq = SM[:, P * r:P * (r + 1)]
                            t = V.scalar_tensor_tensor(out=sq, in0=ident[:, :], scalar=ez[:, r:r + 1], in1=sq,
                                                       op0=ALU.mult, op1=ALU.add)
                        t.then_inc(s["sq_done"], 1)

                    maxima(0, 0)
                    maxima(0, 1)
                    for t in range(1, nq + 1):
                        if t < nq:
                            maxima(t, 0)
                        for run in key_turns(ts[t - 2])[2:] if t >= 2 else []:
                            turned_lo(t - 2, *run, n)
                            n += 1
                        combine(t - 1)
                        if t < nq:
                            maxima(t, 1)
                        elif not last:
                            rope_mul(h, P, 0)
                        if chunk_due(l, t - 2):
                            outputs(chunk_due(l, t - 2), n)
                            n += 1
                        for run in key_turns(ts[t - 1])[:2]:
                            turned_lo(t - 1, *run, n)
                            n += 1
                    for run in key_turns(ts[nq - 1])[2:]:
                        turned_lo(nq - 1, *run, n)
                        n += 1
                    if not last:
                        rope_add(h, P, 0)
                        rope_mul(h, P, 1)
                        rope_add(h, P, 1)
                    outputs(chunk_due(l, nq - 1), n)
                    n += 1
                    if not last:
                        prep_lo(h * nslot, n)

                with dve.Fori(0, HEADS - 1) as h:
                    head(h, False)
                head(HEADS - 1, True)
                def y_low(i):
                    k = Y_ORDER[i]
                    dve.wait_ge(s["y_hi"], i + 1 + 8 * l)
                    y = Hs[:, :, k, lo:].rearrange("p s (r n) -> p s r n", n=P)
                    V.tensor_tensor(y[:, 1, :, :], y_rows(k, ts[0]), y[:, 0, :, :].bitcast(F32), ALU.subtract).then_inc(s["y_lo"], 1)

                for i in range(KT - 1):
                    y_low(i)
                y = y_rows(Y_ORDER[-1], ts[0])
                dve.wait_ge(s["rstd_done"], HEADS)
                V.tensor_tensor(y, y, SM[:, lo:ROWS].rearrange("p (r n) -> p r n", n=P), ALU.mult).then_inc(s["yb_ready"], 1)
                y_low(KT - 1)
                dve.wait_ge(s["gate_in"], 32 + 32 * l)
                dve.wait_ge(s["y_lo"], KT + 8 * l)
                for g in range(2):
                    for n, r in enumerate(ts):
                        if g == 0 and n == nq - 1:
                            split_lo(l, G_O1)
                        if g == 1 and n == nq - 1 and l < DEPTH - 1:
                            norm_rstd(l + 1, 0)
                            norm_scale(l + 1, 0)
                            split_lo(l + 1, G_UV)
                        u = nq * g + n
                        z = QX[:, XT + 4096 + 512 * (u % 2):XT + 4608 + 512 * (u % 2)]
                        j = 1 if r < CTX_TILES else 0
                        dve.wait_ge(s["o_full"], u + 1)
                        if u >= 2:
                            dve.wait_ge(s["o_x"], u - 1)
                        V.tensor_tensor(z, PS[:, u % 5, :], SM[:, D * j + GW * g:D * j + GW * (g + 1)], ALU.mult).then_inc(s["o_z"], 1)
                        dve.wait_ge(s["o_z"], u + 1)
                        if g == 0:
                            c = NORM_CHUNKS.index(chunk_of(r))
                            dve.wait_ge(s["x_in"][c], 32 + 16 * l)
                        xs = X[:, r, GW * g:GW * (g + 1)]
                        V.tensor_tensor(xs, xs, z, ALU.add).then_inc(s["o_x"], 1)
                        if g == 1 and l == DEPTH - 1:
                            dve.wait_ge(s["f_sq"], n + 1)
                            V.tensor_scalar(stat[:, 1, r:r + 1], stat[:, 0, r:r + 1], 1.0 / D, EPS, ALU.mult, ALU.add).then_inc(s["f_ms"], 1)
                            dve.wait_ge(s["f_root"], n + 1)
                            V.reciprocal(stat[:, 1, r:r + 1], stat[:, 1, r:r + 1]).then_inc(s["f_rstd"], 1)
                            dve.wait_ge(s["f_rstd"], n + 1)
                            dve.wait_ge(s["fg_in"], 16)
                            V.scalar_tensor_tensor(out=X[:, r, :], in0=X[:, r, :], scalar=stat[:, 1, r:r + 1],
                                                   in1=QX[:, XT + 1024:XT + 2048], op0=ALU.mult, op1=ALU.mult).then_inc(s["f_y"], 1)


def rope_tables():
    row = np.repeat(np.arange(LAT_TILES * P // GRID_W), GRID_W).astype(np.float32)
    col = np.tile(np.arange(GRID_W), LAT_TILES * P // GRID_W).astype(np.float32)
    n = HD // 4
    inv = (np.float32(10000.0) ** (-np.arange(n, dtype=np.float32) / np.float32(n))).astype(np.float32)
    cos, sin = [], []
    for pos in (row, col):
        ang = pos[:, None] * inv
        cos += [np.cos(ang), np.cos(ang)]
        sin += [-np.sin(ang), np.sin(ang)]
    lay = lambda a: np.ascontiguousarray(np.concatenate(a, 1).astype(np.float32).reshape(LAT_TILES, P, HD).transpose(1, 0, 2))
    return lay(cos), lay(sin)


_INS = ["x", "c", "ctx", "c_ctx", "w_mod", "b_mod", "norm_g", "w_in", "w_out", "sgu_norm_g", "sgu_w", "sgu_b",
        "lambda_q1", "lambda_k1", "lambda_q2", "lambda_k2", "subln_g", "conv_w", "conv_b", "final_g"]


def kernel(**inputs):
    import concourse.bacc as _bacc
    from concourse.bass_utils import run_bass_kernel_spmd as _run

    nc = _bacc.Bacc("TRN2", target_bir_lowering=False, num_devices=1)
    arrays, args = {}, []
    cos, sin = rope_tables()
    for name, a in [(n, np.ascontiguousarray(inputs[n])) for n in _INS] + [("cos_t", cos), ("sin_t", sin)]:
        arrays[f"in_{name}"] = a
        args.append(nc.dram_tensor(f"in_{name}", a.shape, mybir.dt.from_np(a.dtype), kind="ExternalInput").ap())
    args.append(nc.dram_tensor("out_0", (1, LAT_TILES * P, D), F32, kind="ExternalOutput").ap())
    for name, shape in (("x1_d", (TILES, P, D)), ("yT_d", (4, P, ROWS)), ("bz_d", (HEADS, P, ROWS)),
                        ("gate_d", (DEPTH, 2, D))):
        args.append(nc.dram_tensor(name, shape, F32, kind="Internal").ap())
    build(nc, *args)
    r = _run(nc, [arrays], core_ids=[0])
    return r.results[0]["out_0"]
```
